# Optimizing a Trainium2 kernel written in Bass

```python
import jax, jax.numpy as jnp
from jax import lax
import numpy as np

D_MODEL = 1024
BATCH = 1
SEQ = 512
DEPTH = 1
DEC_BATCH = 8
DEC_SEQ = 1
PAST_LEN = 4096
PAGE_SIZE = 128

D_CONV = D_MODEL // 2
D_RWKV = D_MODEL - D_CONV
D_MIX = D_CONV + D_RWKV
CONV_W = 31
HEAD_DIM = 64
N_HEADS = D_RWKV // HEAD_DIM
LORA_W = 64
LORA_A = 64
LORA_G = 160
D_SHIFT = 3 * D_RWKV + LORA_W + LORA_A + LORA_G
D_IN = 2 * D_CONV + D_SHIFT
V_COL = 2 * D_CONV + 2 * D_RWKV
GN_EPS = 64e-5
LN_EPS = 1e-5
N_EXPERTS = 64
D_EXPERT = 256
TOP_K = 8
N_GROUPS = 8
TOPK_GROUPS = 4
ROUTED_SCALE = 2.5
MOE_BLOCK = 128
ALPHA = (2.0 * DEPTH) ** 0.25
BETA = (8.0 * DEPTH) ** -0.25

kernel_name = "hymba_conformer_rwkv7_moe_deepnorm_step"

def layer_norm(x, g, b, eps=LN_EPS):
    xf = x.astype(jnp.float32)
    mu = xf.mean(-1, keepdims=True)
    var = jnp.square(xf - mu).mean(-1, keepdims=True)
    return ((xf - mu) * lax.rsqrt(var + eps) * g + b).astype(x.dtype)

def wkv_scan(s0, r, w, k, v, a, b):
    def step(s, inp):
        r_t, w_t, k_t, v_t, a_t, b_t = inp
        sa = jnp.einsum("bhvk,bhk->bhv", s, a_t)
        s = s * w_t[:, :, None, :] + sa[..., None] * b_t[:, :, None, :] + v_t[..., None] * k_t[:, :, None, :]
        return s, jnp.einsum("bhvk,bhk->bhv", s, r_t)
    xs = tuple(jnp.swapaxes(t, 0, 1) for t in (r, w, k, v, a, b))
    s_final, ys = lax.scan(step, s0, xs)
    return jnp.swapaxes(ys, 0, 1), s_final

def moe(x2d, router_w, router_bias, exp_gate, exp_up, exp_down, sh_gate, sh_up, sh_down):
    T = x2d.shape[0]
    scores = jax.nn.sigmoid(jnp.dot(x2d, router_w).astype(jnp.float32))
    sel = scores + router_bias.astype(jnp.float32)
    grp = sel.reshape(T, N_GROUPS, N_EXPERTS // N_GROUPS)
    grp_score = lax.top_k(grp, 2)[0].sum(-1)
    _, gidx = lax.top_k(grp_score, TOPK_GROUPS)
    gmask = jax.nn.one_hot(gidx, N_GROUPS, dtype=jnp.float32).sum(-2) > 0
    emask = jnp.repeat(gmask, N_EXPERTS // N_GROUPS, axis=-1)
    _, eidx = lax.top_k(jnp.where(emask, sel, -jnp.inf), TOP_K)
    gates = jnp.take_along_axis(scores, eidx, axis=-1)
    gates = gates / (gates.sum(-1, keepdims=True) + 1e-20) * ROUTED_SCALE

    S = T * TOP_K
    n_blocks = -(-(S + N_EXPERTS * (MOE_BLOCK - 1)) // MOE_BLOCK)
    P = n_blocks * MOE_BLOCK
    flat_e = eidx.reshape(S)
    flat_t = jnp.repeat(jnp.arange(T, dtype=jnp.int32), TOP_K)
    flat_g = gates.reshape(S).astype(x2d.dtype)
    order = jnp.argsort(flat_e)
    se, st, sg = flat_e[order], flat_t[order], flat_g[order]
    counts = jnp.bincount(flat_e, length=N_EXPERTS)
    starts = jnp.cumsum(counts) - counts
    pcounts = (counts + MOE_BLOCK - 1) // MOE_BLOCK * MOE_BLOCK
    pends = jnp.cumsum(pcounts)
    pstarts = pends - pcounts
    dest = pstarts[se] + (jnp.arange(S) - starts[se])
    buf_t = jnp.zeros((P,), jnp.int32).at[dest].set(st)
    buf_g = jnp.zeros((P,), x2d.dtype).at[dest].set(sg)
    block_e = jnp.minimum(jnp.searchsorted(pends, jnp.arange(n_blocks) * MOE_BLOCK, side="right"), N_EXPERTS - 1)

    def block_fn(args):
        t_idx, g, e = args
        xb = x2d[t_idx]
        hb = jax.nn.silu(xb @ exp_gate[e]) * (xb @ exp_up[e])
        return (hb @ exp_down[e]) * g[:, None]

    yb = lax.map(block_fn, (buf_t.reshape(n_blocks, MOE_BLOCK), buf_g.reshape(n_blocks, MOE_BLOCK), block_e))
    routed = jax.ops.segment_sum(yb.reshape(P, -1), buf_t, num_segments=T)
    shared = (jax.nn.silu(x2d @ sh_gate) * (x2d @ sh_up)) @ sh_down
    return shared + routed

def hybrid_layer(x, conv_buf, shift_buf, wkv_state, lp):
    Bn, T, _ = x.shape
    z = jnp.einsum("btd,de->bte", x, lp["w_in"])
    z_conv, z_rw = z[..., :2 * D_CONV], z[..., 2 * D_CONV:]

    u = z_conv[..., :D_CONV] * jax.nn.sigmoid(z_conv[..., D_CONV:])
    u_full = jnp.concatenate([conv_buf.astype(u.dtype), u], axis=1)
    c = lax.conv_general_dilated(u_full, lp["conv_w"][:, None, :], (1,), "VALID",
                                 dimension_numbers=("NWC", "WIO", "NWC"),
                                 feature_group_count=D_CONV) + lp["conv_b"]
    c = jax.nn.silu(layer_norm(c, lp["conv_ln_g"], lp["conv_ln_b"]))
    new_conv = u_full[:, -(CONV_W - 1):]

    z_prev = jnp.concatenate([shift_buf[:, None].astype(z_rw.dtype), z_rw[:, :-1]], axis=1)
    zs = z_rw + (z_prev - z_rw) * lp["mu_shift"]
    new_shift = z_rw[:, -1]
    r, k, v, wd, ad, gd = jnp.split(
        zs, [D_RWKV, 2 * D_RWKV, 3 * D_RWKV, 3 * D_RWKV + LORA_W, 3 * D_RWKV + LORA_W + LORA_A], axis=-1)
    w_log = -jax.nn.softplus(-(lp["w0"] + jnp.tanh(wd) @ lp["w_up"])) - 0.5
    decay = jnp.exp(-jnp.exp(w_log.astype(jnp.float32)))
    a = jax.nn.sigmoid(lp["a0"] + ad @ lp["a_up"])
    g = jax.nn.sigmoid(gd) @ lp["g_up"]

    def heads(t):
        return t.reshape(Bn, T, N_HEADS, HEAD_DIM).astype(jnp.float32)

    kk = heads(k * lp["k_k"])
    kk = kk / jnp.maximum(jnp.sqrt(jnp.sum(kk * kk, -1, keepdims=True)), 1e-12)
    k = k * (1.0 + (a - 1.0) * lp["k_a"])
    rh, kh, vh, ah = heads(r), heads(k), heads(v), heads(a)
    y, new_wkv = wkv_scan(wkv_state.astype(jnp.float32), rh, heads(decay), kh, vh, -kk, kk * ah)
    y_mu = y.mean(-1, keepdims=True)
    y_var = jnp.square(y - y_mu).mean(-1, keepdims=True)
    yn = ((y - y_mu) * lax.rsqrt(y_var + GN_EPS)).reshape(Bn, T, D_RWKV) * lp["gn_g"] + lp["gn_b"]
    bonus = (jnp.sum(rh * kh * lp["r_k"].astype(jnp.float32), -1, keepdims=True) * vh).reshape(Bn, T, D_RWKV)
    o_rw = ((yn + bonus) * g).astype(x.dtype)

    h = jnp.einsum("btc,cd->btd", jnp.concatenate([c.astype(x.dtype), o_rw], axis=-1), lp["w_out"])
    x = layer_norm(ALPHA * x + h, lp["ln1_g"], lp["ln1_b"])
    f = moe(x.reshape(Bn * T, D_MODEL), lp["router_w"], lp["router_bias"], lp["exp_gate"], lp["exp_up"],
            lp["exp_down"], lp["sh_gate"], lp["sh_up"], lp["sh_down"]).reshape(Bn, T, D_MODEL)
    x = layer_norm(ALPHA * x + f.astype(x.dtype), lp["ln2_g"], lp["ln2_b"])
    return x, new_conv, new_shift.astype(shift_buf.dtype), new_wkv.astype(wkv_state.dtype)

def setup_inputs(seed: int = 0) -> dict:
    key = jax.random.key(seed)
    ks = jax.random.split(key, 40)
    f32 = jnp.float32

    def nrm(k, shape, s):
        return jax.random.normal(k, shape, f32) * s

    col_scale = jnp.ones((D_IN,), f32).at[V_COL:V_COL + D_RWKV].set(BETA)
    return {
        "x_prompt": nrm(ks[0], (BATCH, SEQ, D_MODEL), 1.0),
        "x_sample": nrm(ks[1], (DEC_BATCH, DEC_SEQ, D_MODEL), 1.0),
        "state_conv": nrm(ks[2], (DEPTH, DEC_BATCH, CONV_W - 1, D_CONV), 0.5),
        "state_shift": nrm(ks[3], (DEPTH, DEC_BATCH, D_SHIFT), 1.0),
        "state_wkv": nrm(ks[4], (DEPTH, DEC_BATCH, N_HEADS, HEAD_DIM, HEAD_DIM), 0.3),
        "w_in": nrm(ks[5], (DEPTH, D_MODEL, D_IN), D_MODEL ** -0.5) * col_scale,
        "mu_shift": jax.random.uniform(ks[6], (DEPTH, D_SHIFT), f32),
        "conv_w": nrm(ks[7], (DEPTH, CONV_W, D_CONV), CONV_W ** -0.5),
        "conv_b": nrm(ks[8], (DEPTH, D_CONV), 0.02),
        "conv_ln_g": 1.0 + nrm(ks[9], (DEPTH, D_CONV), 0.02),
        "conv_ln_b": nrm(ks[10], (DEPTH, D_CONV), 0.02),
        "w0": jax.random.uniform(ks[11], (DEPTH, D_RWKV), f32, minval=-6.0, maxval=1.0),
        "w_up": nrm(ks[12], (DEPTH, LORA_W, D_RWKV), 0.1 * LORA_W ** -0.5),
        "a0": nrm(ks[13], (DEPTH, D_RWKV), 0.5),
        "a_up": nrm(ks[14], (DEPTH, LORA_A, D_RWKV), LORA_A ** -0.5),
        "g_up": nrm(ks[15], (DEPTH, LORA_G, D_RWKV), LORA_G ** -0.5),
        "k_k": 0.85 + nrm(ks[16], (DEPTH, D_RWKV), 0.05),
        "k_a": 1.0 + nrm(ks[17], (DEPTH, D_RWKV), 0.05),
        "r_k": nrm(ks[18], (DEPTH, N_HEADS, HEAD_DIM), 0.1),
        "gn_g": 1.0 + nrm(ks[19], (DEPTH, D_RWKV), 0.02),
        "gn_b": nrm(ks[20], (DEPTH, D_RWKV), 0.02),
        "w_out": nrm(ks[21], (DEPTH, D_MIX, D_MODEL), BETA * D_MIX ** -0.5),
        "ln1_g": 1.0 + nrm(ks[22], (DEPTH, D_MODEL), 0.02),
        "ln1_b": nrm(ks[23], (DEPTH, D_MODEL), 0.02),
        "router_w": nrm(ks[24], (DEPTH, D_MODEL, N_EXPERTS), D_MODEL ** -0.5),
        "router_bias": nrm(ks[25], (DEPTH, N_EXPERTS), 0.01),
        "exp_gate": nrm(ks[26], (DEPTH, N_EXPERTS, D_MODEL, D_EXPERT), D_MODEL ** -0.5),
        "exp_up": nrm(ks[27], (DEPTH, N_EXPERTS, D_MODEL, D_EXPERT), D_MODEL ** -0.5),
        "exp_down": nrm(ks[28], (DEPTH, N_EXPERTS, D_EXPERT, D_MODEL), BETA * D_EXPERT ** -0.5),
        "sh_gate": nrm(ks[29], (DEPTH, D_MODEL, D_EXPERT), D_MODEL ** -0.5),
        "sh_up": nrm(ks[30], (DEPTH, D_MODEL, D_EXPERT), D_MODEL ** -0.5),
        "sh_down": nrm(ks[31], (DEPTH, D_EXPERT, D_MODEL), BETA * D_EXPERT ** -0.5),
        "ln2_g": 1.0 + nrm(ks[32], (DEPTH, D_MODEL), 0.02),
        "ln2_b": nrm(ks[33], (DEPTH, D_MODEL), 0.02),
    }

def reference(x_prompt, x_sample, state_conv, state_shift, state_wkv, w_in, mu_shift, conv_w, conv_b,
              conv_ln_g, conv_ln_b, w0, w_up, a0, a_up, g_up, k_k, k_a, r_k, gn_g, gn_b, w_out,
              ln1_g, ln1_b, router_w, router_bias, exp_gate, exp_up, exp_down, sh_gate, sh_up, sh_down,
              ln2_g, ln2_b):
    y_prompt, y_sample = x_prompt, x_sample
    conv_p, shift_p, wkv_p, conv_s, shift_s, wkv_s = [], [], [], [], [], []
    Bp = x_prompt.shape[0]
    for l in range(DEPTH):
        lp = {"w_in": w_in[l], "mu_shift": mu_shift[l], "conv_w": conv_w[l], "conv_b": conv_b[l],
              "conv_ln_g": conv_ln_g[l], "conv_ln_b": conv_ln_b[l], "w0": w0[l], "w_up": w_up[l],
              "a0": a0[l], "a_up": a_up[l], "g_up": g_up[l], "k_k": k_k[l], "k_a": k_a[l], "r_k": r_k[l],
              "gn_g": gn_g[l], "gn_b": gn_b[l], "w_out": w_out[l], "ln1_g": ln1_g[l], "ln1_b": ln1_b[l],
              "router_w": router_w[l], "router_bias": router_bias[l], "exp_gate": exp_gate[l],
              "exp_up": exp_up[l], "exp_down": exp_down[l], "sh_gate": sh_gate[l], "sh_up": sh_up[l],
              "sh_down": sh_down[l], "ln2_g": ln2_g[l], "ln2_b": ln2_b[l]}
        zc = jnp.zeros((Bp, CONV_W - 1, D_CONV), x_prompt.dtype)
        zsh = jnp.zeros((Bp, D_SHIFT), x_prompt.dtype)
        zw = jnp.zeros((Bp, N_HEADS, HEAD_DIM, HEAD_DIM), x_prompt.dtype)
        y_prompt, c_p, s_p, w_p = hybrid_layer(y_prompt, zc, zsh, zw, lp)
        y_sample, c_s, s_s, w_s = hybrid_layer(y_sample, state_conv[l], state_shift[l], state_wkv[l], lp)
        conv_p.append(c_p); shift_p.append(s_p); wkv_p.append(w_p)
        conv_s.append(c_s); shift_s.append(s_s); wkv_s.append(w_s)
    new_conv_p = jnp.stack(conv_p)
    new_shift_p = jnp.stack(shift_p)
    new_wkv_p = jnp.stack(wkv_p)
    new_conv_s = jnp.stack(conv_s)
    new_shift_s = jnp.stack(shift_s)
    new_wkv_s = jnp.stack(wkv_s)
    return (y_prompt, y_sample, new_conv_p, new_shift_p, new_wkv_p, new_conv_s, new_shift_s, new_wkv_s)


_drawn_inputs = setup_inputs


def setup_inputs(seed=0):
    import zlib

    import numpy as np

    out = dict(_drawn_inputs(seed))
    spreads = {}
    factors = {}
    for name, (base, spread) in spreads.items():
        noise = np.random.default_rng([zlib.crc32(name.encode()), seed]).standard_normal(out[name].shape)
        drawn = base * np.exp(spread * noise) if base else spread * noise
        out[name] = __import__('jax').numpy.asarray(drawn.astype(out[name].dtype))
    for name, factor in factors.items():
        out[name] = (out[name] * factor).astype(out[name].dtype)
    return out
```

```python
from contextlib import ExitStack

import concourse.bass as bass
from concourse import mybir

F32 = mybir.dt.float32
U32 = mybir.dt.uint32
BF16 = mybir.dt.bfloat16
ALU = mybir.AluOpType
ACT = mybir.ActivationFunctionType
AX = mybir.AxisListType.X

P = 128
D = 1024
KD = D // P
T = 512
B = 8
TT = T + B
TM = T // P
DC = 512
CT = DC // P
CW = 31
H = 8
N = 64
LW = 64
LA = 64
LG = 160
DS = 3 * 512 + LW + LA + LG
L = 32
NCH = T // L
CM = P // L
E = 64
FE = 256
K = 8
G = 8
KG = 4
CAP = 96
ALPHA = 2.0 ** 0.25
LN_EPS = 1e-5
GN_EPS = 64e-5
ROUTED_SCALE = 2.5
DECAY_SCALE = 0.6065306597126334
TOK_TILES = [(i * P, P) for i in range(TM)] + [(T, B)]
NT = len(TOK_TILES)

CONV_TILES = [(kind, i, off + i * P, P) for i in range(CT) for kind, off in (("glu_a", 0), ("glu_gate", DC))]
_RW = 2 * DC
SHIFT_TILES = [("lora", 0, _RW + 1536, P), ("gate0", 0, _RW + 1664, P)] \
    + [(kind, i, _RW + j * 512 + i * P, P) for i in range(CT) for j, kind in enumerate("rkv")] \
    + [("gate1", 0, _RW + 1792, 32)]
COL_TILES = CONV_TILES + SHIFT_TILES
NCOL = len(COL_TILES)
NCONV = len(CONV_TILES)
NSH = len(SHIFT_TILES)
LORA, GATE0, GATE1 = 0, 1, NSH - 1


def shift_index(kind, i):
    return 2 + 3 * i + "rkv".index(kind)


PARAMS = ["conv_b", "conv_ln_g", "conv_ln_b", "w0", "a0", "k_k", "k_a", "r_k"]
NPAR = CW + len(PARAMS)


def par(name):
    return CW + PARAMS.index(name)


class Chain:

    def __init__(self, eng, sem, state):
        self.eng, self.sem, self.state = eng, sem, state

    def link(self, ins):
        self.state[0] += 1
        ins.then_inc(self.sem, 1)
        self.eng.wait_ge(self.sem, self.state[0])


def cols(i):
    t0, n = TOK_TILES[i]
    return slice(t0, t0 + n)


def project(nc, m, ctx_out):
    WB = 6
    ZB = 3
    with ExitStack() as ctx:
        def sb(name, shape, dt=F32):
            return ctx.enter_context(nc.sbuf_tensor(name, shape, dt))

        def ps(name, shape, dt=F32):
            return ctx.enter_context(nc.psum_tensor(name, shape, dt))

        def sem(name):
            m.spent.append(ctx_out.enter_context(nc.semaphore(name)))
            return m.spent[-1]

        x_rows = sb("x_rows", [P, NT, D])
        x_t = sb("x_t", [P, KD, TT])
        w_col = sb("w_col", [P, WB, KD, P])
        staged = sb("staged", [P, ZB, T + 1])
        glu_stage = sb("glu_stage", [P, 2, T])
        u_pad = sb("u_pad", [P, CT, CW - 1 + T])
        z_last = sb("z_last", [P, NSH, 1 + B])
        z_diff = sb("z_diff", [P, 2, T])
        z_sample = sb("z_sample", [P, NCOL, B])
        gate_sample = sb("gate_sample", [P, CT, B])
        u_sample = sb("u_sample", [P, CT, B])
        zd_sample = sb("zd_sample", [P, NSH, B])
        par_rows = sb("par_rows", [NPAR, DC])
        shift_rows = sb("shift_rows", [B + 1, DS])
        conv_rows = sb("conv_rows", [120, 2, DC])
        shift_t = sb("shift_t", [P, NSH, B + 1])
        conv_state = sb("conv_state", [P, CT, B * (CW - 1)])
        conv_prod = sb("conv_prod", [P, CT, B * (CW - 1)])
        conv_sum = sb("conv_sum", [P, CT, B])
        tail_rows = sb("tail_rows", [38, DC])
        tail_in = sb("tail_in", [P, CT, 38])
        shift_out = sb("shift_out", [1 + B, DS])
        pt = ps("pt", [P, 2, 512])
        pz = ps("pz", [P, 3, 512])
        pzs = ps("pzs", [P, NCOL, B])
        pm = ps("pm", [P, 2, 512])

        x_loaded = sem("x_loaded")
        small_loaded = sem("small_loaded")
        w_loaded = [sem(f"w_loaded{i}") for i in range(WB)]
        consts_ready = sem("consts_ready")
        xt_turned = sem("xt_turned")
        xt_ready = sem("xt_ready")
        small_turned = sem("small_turned")
        small_ready = sem("small_ready")
        tile_projected = sem("tile_projected")
        tile_taken = sem("tile_taken")
        staged_used = sem("staged_used")
        glu_used = sem("glu_used")
        sample_taken = sem("sample_taken")
        sample_gated = sem("sample_gated")
        tails_ready = sem("tails_ready")
        tails_turned = sem("tails_turned")
        tails_copied = sem("tails_copied")
        state_stored = sem("state_stored")
        zeros_ready = sem("zeros_ready")
        XT_GROUPS = 2 * TM + 1
        SMALL = 4

        with nc.Block() as block:
            @block.sync
            def _(sp):
                for i, (t0, n) in enumerate(TOK_TILES):
                    src = m.x_prompt[t0:t0 + n, :] if i < TM else m.x_sample
                    sp.dma_start(x_rows[0:n, i, :], src).then_inc(x_loaded, 16)
                for c, (_, _, c0, w) in enumerate(COL_TILES):
                    if c >= WB:
                        sp.wait_ge(tile_projected, c - WB + 1)
                    sp.dma_start(w_col[:, c % WB, :, 0:w],
                                 m.w_in[:, c0:c0 + w].rearrange("(k p) n -> p k n", p=P)).then_inc(w_loaded[c % WB], 16)
                sp.wait_ge(tails_copied, 2)
                sp.dma_start(m.new_conv_p, tail_rows[0:30, :]).then_inc(state_stored, 16)
                sp.dma_start(m.new_conv_s[:, CW - 2, :], tail_rows[30:38, :]).then_inc(state_stored, 16)
                sp.wait_ge(tails_copied, 6)
                sp.dma_start(m.new_shift_p, shift_out[0:1, :]).then_inc(state_stored, 16)
                sp.dma_start(m.new_shift_s, shift_out[1:1 + B, :]).then_inc(state_stored, 16)
                sp.wait_ge(state_stored, 16 * 5)

            @block.scalar
            def _(act):
                act.dma_start(par_rows[0:CW, :], m.conv_w).then_inc(small_loaded, 16)
                for name in PARAMS:
                    act.dma_start(par_rows[par(name):par(name) + 1, :], m.vec[name]).then_inc(small_loaded, 16)
                act.dma_start(shift_rows[0:B, :], m.state_shift).then_inc(small_loaded, 16)
                act.dma_start(shift_rows[B:B + 1, :], m.mu_shift).then_inc(small_loaded, 16)
                for j in range(2):
                    act.dma_start(conv_rows[:, j, :],
                                  m.state_conv[4 * j:4 * j + 4].rearrange("b w c -> (b w) c")).then_inc(small_loaded, 16)
                act.dma_start(m.new_conv_s[:, 0:CW - 2, :], m.state_conv[:, 1:CW - 1, :]).then_inc(state_stored, 16)
                for g in range(XT_GROUPS):
                    act.wait_ge(xt_turned, g + 1)
                    if g < 2 * TM:
                        i, k0 = g // 2, 4 * (g % 2)
                        nc.scalar.copy(x_t[:, k0:k0 + 4, cols(i)],
                                       pt[:, g % 2, :].rearrange("p (k t) -> p k t", k=4)).then_inc(xt_ready, 1)
                    else:
                        nc.scalar.copy(x_t[:, :, cols(TM)],
                                       pt[:, g % 2, 0:KD * B].rearrange("p (k t) -> p k t", k=KD)).then_inc(xt_ready, 1)
                act.wait_ge(zeros_ready, 3)
                for c, (kind, i, _, w) in enumerate(COL_TILES):
                    act.wait_ge(tile_projected, c + 1)
                    z = pz[0:w, c % 3, :]
                    if kind == "glu_a":
                        if i >= 1:
                            act.wait_ge(glu_used, i)
                        nc.scalar.copy(glu_stage[:, 0, :], z).then_inc(tile_taken, 1)
                    elif kind == "glu_gate":
                        nc.scalar.activation(glu_stage[:, 1, :], z, ACT.Sigmoid).then_inc(tile_taken, 1)
                    else:
                        s = c - NCONV
                        if s >= ZB:
                            act.wait_ge(staged_used, s - ZB + 1)
                        nc.scalar.copy(z_last[0:w, s, 0:1], z[:, T - 1:T])
                        nc.scalar.copy(staged[0:w, s % ZB, 1:T + 1], z).then_inc(tile_taken, 1)
                nc.scalar.copy(z_sample[:, 0:NCOL - 1, :], pzs[:, 0:NCOL - 1, :])
                nc.scalar.copy(z_sample[0:32, NCOL - 1, :], pzs[0:32, NCOL - 1, :]).then_inc(sample_taken, 1)
                nc.scalar.activation(gate_sample[:], pzs[:, 1:NCONV:2, :], ACT.Sigmoid).then_inc(sample_gated, 1)

            @block.tensor
            def _(pe):
                pe.wait_ge(consts_ready, 1)
                for g in range(XT_GROUPS):
                    i = g // 2
                    pe.wait_ge(x_loaded, 16 * NT)
                    if g >= 2:
                        pe.wait_ge(xt_ready, g - 1)
                    if g < 2 * TM:
                        for k in range(4):
                            d0 = (4 * (g % 2) + k) * P
                            last = nc.tensor.transpose(pt[:, g % 2, k * P:(k + 1) * P], x_rows[:, i, d0:d0 + P], m.ident[:])
                    else:
                        for k in range(KD):
                            last = nc.tensor.transpose(pt[:, g % 2, k * B:(k + 1) * B],
                                                       x_rows[0:B, TM, k * P:(k + 1) * P], m.ident[0:B, 0:B])
                    last.then_inc(xt_turned, 1)
                pe.wait_ge(small_loaded, 16 * (1 + len(PARAMS) + 4))
                for i in range(CT):
                    last = nc.tensor.transpose(pm[:, 0, i * NPAR:(i + 1) * NPAR], par_rows[:, i * P:(i + 1) * P],
                                               m.ident[0:NPAR, 0:NPAR])
                last.then_inc(small_turned, 1)
                for s, (_, _, c0, w) in enumerate(SHIFT_TILES):
                    last = nc.tensor.transpose(pm[0:w, 1, s * (B + 1):(s + 1) * (B + 1)],
                                               shift_rows[:, c0 - _RW:c0 - _RW + w], m.ident[0:B + 1, 0:B + 1])
                last.then_inc(small_turned, 1)
                for h in range(2):
                    pe.wait_ge(small_ready, h + 1)
                    for i in range(2):
                        for j in range(2):
                            last = nc.tensor.transpose(pm[:, h, (2 * i + j) * 120:(2 * i + j + 1) * 120],
                                                       conv_rows[:, j, (2 * h + i) * P:(2 * h + i + 1) * P],
                                                       m.ident[0:120, 0:120])
                    last.then_inc(small_turned, 1)
                pe.wait_ge(xt_ready, XT_GROUPS)
                for c, (_, _, _, w) in enumerate(COL_TILES):
                    pe.wait_ge(w_loaded[c % WB], 16 * (c // WB + 1))
                    if c >= 3:
                        pe.wait_ge(tile_taken, c - 2)
                    for k in range(KD):
                        nc.tensor.matmul(pz[0:w, c % 3, :], w_col[:, c % WB, k, 0:w], x_t[:, k, 0:T],
                                         start=(k == 0), stop=(k == KD - 1))
                        last = nc.tensor.matmul(pzs[0:w, c, :], w_col[:, c % WB, k, 0:w], x_t[:, k, T:TT],
                                                start=(k == 0), stop=(k == KD - 1))
                    last.then_inc(tile_projected, 1)
                pe.wait_ge(tails_ready, 1)
                for i in range(CT):
                    last = nc.tensor.transpose(pm[0:38, 0, i * P:(i + 1) * P], tail_in[:, i, :], m.ident[:])
                last.then_inc(tails_turned, 1)
                pe.wait_ge(tails_ready, 2)
                for q in range(4):
                    if q >= 1:
                        pe.wait_ge(tails_copied, q + 1)
                    for s in range(4 * q, min(4 * q + 4, NSH)):
                        w = SHIFT_TILES[s][3]
                        last = nc.tensor.transpose(pm[0:1 + B, 1 - q % 2, (s % 4) * P:(s % 4) * P + w],
                                                   z_last[0:w, s, :], m.ident[0:w, 0:w])
                    last.then_inc(tails_turned, 1)

            @block.vector
            def _(dve):
                ch = Chain(dve, m.vector_step, m.vector_count)
                nc.vector.memset(u_pad[:, :, 0:CW - 1], 0.0).then_inc(zeros_ready, 1)
                for b in range(ZB):
                    last = nc.vector.memset(staged[:, b, 0:1], 0.0)
                last.then_inc(zeros_ready, 1)
                nc.vector.memset(shift_t[:], 0.0).then_inc(zeros_ready, 1)
                dve.wait_ge(zeros_ready, 3)
                dve.wait_ge(small_turned, 1)
                ch.link(nc.vector.tensor_copy(m.params[:], pm[:, 0, 0:CT * NPAR].rearrange("p (i n) -> p i n", i=CT)))
                dve.wait_ge(small_turned, 2)
                nc.vector.tensor_copy(shift_t[:, 0:NSH - 1, :], pm[:, 1, 0:(NSH - 1) * (B + 1)].rearrange("p (i n) -> p i n", n=B + 1))
                nc.vector.tensor_copy(shift_t[0:32, NSH - 1, :], pm[0:32, 1, (NSH - 1) * (B + 1):NSH * (B + 1)]).then_inc(small_ready, 2)
                for h in range(2):
                    dve.wait_ge(small_turned, 3 + h)
                    nc.vector.tensor_copy(conv_state[:, 2 * h:2 * h + 2, :],
                                          pm[:, h, 0:480].rearrange("p (i n) -> p i n", i=2)).then_inc(small_ready, 1)
                dve.wait_ge(small_ready, 4)
                for i in range(CT):
                    dve.wait_ge(tile_taken, 2 * i + 2)
                    nc.vector.tensor_tensor(u_pad[:, i, CW - 1:CW - 1 + T], glu_stage[:, 0, :], glu_stage[:, 1, :],
                                            ALU.mult).then_inc(glu_used, 1)
                    dve.wait_ge(glu_used, i + 1)
                    ch.link(nc.vector.tensor_scalar(m.conv[:, i, 0:T], u_pad[:, i, 0:T], m.params[:, i, 0:1],
                                                    m.params[:, i, par("conv_b"):par("conv_b") + 1], ALU.mult, ALU.add))
                    for j in range(1, CW):
                        ch.link(nc.vector.scalar_tensor_tensor(m.conv[:, i, 0:T], u_pad[:, i, j:j + T],
                                                               m.params[:, i, j:j + 1], m.conv[:, i, 0:T], ALU.mult, ALU.add))
                for s, (_, _, _, w) in enumerate(SHIFT_TILES):
                    dve.wait_ge(tile_taken, NCONV + s + 1)
                    st = staged[0:w, s % ZB, :]
                    ch.link(nc.vector.tensor_tensor(z_diff[0:w, s % 2, :], st[:, 0:T], st[:, 1:T + 1], ALU.subtract))
                    nc.vector.scalar_tensor_tensor(m.zs[0:w, s, 0:T], z_diff[0:w, s % 2, :], shift_t[0:w, s, B:B + 1],
                                                   st[:, 1:T + 1], ALU.mult, ALU.add).then_inc(staged_used, 1)
                dve.wait_ge(sample_taken, 1)
                nc.vector.tensor_copy(z_last[:, 0:NSH - 1, 1:], z_sample[:, NCONV:NCOL - 1, :])
                nc.vector.tensor_copy(z_last[0:32, NSH - 1, 1:], z_sample[0:32, NCOL - 1, :])
                for sl, w in ((slice(0, NSH - 1), P), (slice(NSH - 1, NSH), 32)):
                    zc = slice(NCONV + sl.start, NCONV + sl.stop)
                    n = sl.stop - sl.start
                    ch.link(nc.vector.tensor_tensor(zd_sample[0:w, sl, :], shift_t[0:w, sl, 0:B], z_sample[0:w, zc, :], ALU.subtract))
                    ch.link(nc.vector.tensor_tensor(zd_sample[0:w, sl, :], zd_sample[0:w, sl, :],
                                                    shift_t[0:w, sl, B:B + 1].broadcast_to([w, n, B]), ALU.mult))
                    ch.link(nc.vector.tensor_tensor(m.zs[0:w, sl, T:TT], zd_sample[0:w, sl, :], z_sample[0:w, zc, :], ALU.add))
                glu = z_sample[:, 0:NCONV, :].rearrange("p (i two) b -> p i two b", two=2)
                dve.wait_ge(sample_gated, 1)
                ch.link(nc.vector.tensor_tensor(u_sample[:], glu[:, :, 0, :], gate_sample[:], ALU.mult))
                ch.link(nc.vector.tensor_tensor(conv_prod[:].rearrange("p i (b j) -> p i b j", b=B),
                                                conv_state[:].rearrange("p i (b j) -> p i b j", b=B),
                                                m.params[:, :, 0:CW - 1].unsqueeze(2).broadcast_to([P, CT, B, CW - 1]), ALU.mult))
                ch.link(nc.vector.tensor_reduce(conv_sum[:], conv_prod[:].rearrange("p i (b j) -> p i b j", b=B), AX, ALU.add))
                ch.link(nc.vector.tensor_tensor(m.conv[:, :, T:TT], u_sample[:],
                                                m.params[:, :, CW - 1:CW].broadcast_to([P, CT, B]), ALU.mult))
                ch.link(nc.vector.tensor_tensor(conv_sum[:], conv_sum[:],
                                                m.params[:, :, par("conv_b"):par("conv_b") + 1].broadcast_to([P, CT, B]), ALU.add))
                ch.link(nc.vector.tensor_tensor(m.conv[:, :, T:TT], m.conv[:, :, T:TT], conv_sum[:], ALU.add))
                nc.vector.tensor_copy(tail_in[:, :, 0:30], u_pad[:, :, T:T + CW - 1])
                nc.vector.tensor_copy(tail_in[:, :, 30:38], u_sample[:]).then_inc(tails_ready, 2)
                dve.wait_ge(tails_turned, 1)
                nc.vector.tensor_copy(tail_rows[:], pm[0:38, 0, :]).then_inc(tails_copied, 2)
                for q in range(4):
                    dve.wait_ge(tails_turned, q + 2)
                    for s in range(4 * q, min(4 * q + 4, NSH)):
                        _, _, c0, w = SHIFT_TILES[s]
                        last = nc.vector.tensor_copy(shift_out[:, c0 - _RW:c0 - _RW + w],
                                                     pm[0:1 + B, 1 - q % 2, (s % 4) * P:(s % 4) * P + w])
                    last.then_inc(tails_copied, 1)

            @block.gpsimd
            def _(pool):
                constants(nc, m, consts_ready)(pool)



def time_prepare(nc, m, ctx_out):
    with ExitStack() as ctx:
        def sb(name, shape, dt=F32):
            return ctx.enter_context(nc.sbuf_tensor(name, shape, dt))

        def ps(name, shape, dt=F32):
            return ctx.enter_context(nc.psum_tensor(name, shape, dt))

        def sem(name):
            m.spent.append(ctx_out.enter_context(nc.semaphore(name)))
            return m.spent[-1]

        lora_w = sb("lora_w", [P, DC])
        g_up0 = sb("g_up0", [P, DC])
        g_up1 = sb("g_up1", [32, DC])
        wd_tanh = sb("wd_tanh", [LW, TT])
        gd_sig = sb("gd_sig", [P, 2, TT])
        decay = sb("decay", [P, CT, TT])
        rate = sb("rate", [P, CT, TT])
        sq = sb("sq", [P, TT])
        norm = sb("norm", [P, TT])
        kk = sb("kk", [P, TT])
        k2 = sb("k2", [P, TT])
        kb = sb("kb", [P, TT])
        tmp = sb("tmp", [P, TT])
        rk = sb("rk", [P, TT])
        cum = sb("cum", [P, T])
        cum_before = sb("cum_before", [P, T])
        cum_end = sb("cum_end", [P, T])
        e_before = sb("e_before", [P, T])
        e_after = sb("e_after", [P, T])
        e_inverse = sb("e_inverse", [P, T])
        e_end = sb("e_end", [P, T])
        b_end = sb("b_end", [P, T])
        k_end = sb("k_end", [P, T])
        big = ps("big", [P, 2, 1024])
        turn = ps("turn", [P, 2, 512])
        pg = ps("pg", [P, 512])
        pb = ps("pb", [P, NT * H])

        w_in2 = sem("lora_loaded")
        tanh_ready = sem("tanh_ready")
        lora_done = sem("lora_done")
        lora_taken = sem("lora_taken")
        sq_ready = sem("sq_ready")
        ss_done = sem("ss_done")
        norm_root = sem("norm_root")
        cum_ready = sem("cum_ready")
        exp_ready = sem("exp_ready")
        bonus_in = sem("bonus_in")
        bonus_done = sem("bonus_done")
        scaled_ready = sem("scaled_ready")
        turned = sem("turned")
        turned_taken = sem("turned_taken")
        gate_done = sem("gate_done")
        gate_taken = sem("gate_taken")
        kk_used = sem("kk_used")
        NTURN = 5

        with nc.Block() as block:
            @block.sync
            def _(sp):
                sp.dma_start(lora_w[0:LW, :], m.w_up).then_inc(w_in2, 16)
                sp.dma_start(lora_w[LW:P, :], m.a_up).then_inc(w_in2, 16)
                sp.dma_start(g_up0[:], m.g_up[0:P, :]).then_inc(w_in2, 16)
                sp.dma_start(g_up1[:], m.g_up[P:LG, :]).then_inc(w_in2, 16)

            @block.tensor
            def _(pe):
                pe.wait_ge(w_in2, 64)
                pe.wait_ge(tanh_ready, 1)
                for j in range(2 * CT):
                    i, rows = j // 2, slice(0, LW) if j % 2 == 0 else slice(LW, P)
                    src = wd_tanh[:, :] if j % 2 == 0 else m.zs[LW:P, LORA, :]
                    if j >= 2:
                        pe.wait_ge(lora_taken, j - 1)
                    for c0, c1 in ((0, T), (T, TT)):
                        last = nc.tensor.matmul(big[:, j % 2, c0:c1], lora_w[rows, i * P:(i + 1) * P], src[:, c0:c1],
                                                start=True, stop=True)
                    last.then_inc(lora_done, 1)
                pe.wait_ge(tanh_ready, 2)
                for i, (t0, n) in enumerate(TOK_TILES):
                    if i >= 1:
                        pe.wait_ge(gate_taken, i)
                    nc.tensor.matmul(pg[0:n, :], gd_sig[:, 0, t0:t0 + n], g_up0[:], start=True, stop=False)
                    nc.tensor.matmul(pg[0:n, :], gd_sig[0:32, 1, t0:t0 + n], g_up1[:], start=False, stop=True).then_inc(gate_done, 1)
                pe.wait_ge(lora_taken, 2 * CT)
                for i in range(CT):
                    pe.wait_ge(sq_ready, i + 1)
                    for c0, c1 in ((0, T), (T, TT)):
                        last = nc.tensor.matmul(big[:, 0, c0:c1], m.head_ones[:], sq[:, c0:c1], start=True, stop=True)
                    last.then_inc(ss_done, 1)
                    pe.wait_ge(bonus_in, i + 1)
                    for j, (t0, n) in enumerate(TOK_TILES):
                        last = nc.tensor.matmul(pb[0:n, j * H + 2 * i:j * H + 2 * i + 2], rk[:, t0:t0 + n], m.head_ones[:, 0:P:N],
                                                start=True, stop=True)
                    last.then_inc(bonus_done, 1)
                    for q in range(NTURN):
                        g = NTURN * i + q
                        if g >= 2:
                            pe.wait_ge(turned_taken, g - 1)
                        if q < 4:
                            if q == 0:
                                pe.wait_ge(scaled_ready, i + 1)
                            for j in range(TM):
                                src = (m.read_decayed[:, i, j, 0, :], b_end[:, cols(j)], k_end[:, cols(j)],
                                       m.zs[:, shift_index("v", i), cols(j)])[q]
                                last = nc.tensor.transpose(turn[:, g % 2, j * P:(j + 1) * P], src, m.ident[:])
                        else:
                            last = nc.tensor.transpose(turn[0:B, g % 2, 0:P], m.zs[:, shift_index("v", i), T:TT], m.ident[:])
                        last.then_inc(turned, 1)

            @block.scalar
            def _(act):
                nc.scalar.activation(wd_tanh[:], m.zs[0:LW, LORA, :], ACT.Tanh).then_inc(tanh_ready, 1)
                nc.scalar.activation(gd_sig[:, 0, :], m.zs[:, GATE0, :], ACT.Sigmoid)
                nc.scalar.activation(gd_sig[0:32, 1, :], m.zs[0:32, GATE1, :], ACT.Sigmoid).then_inc(tanh_ready, 1)
                for j in range(2 * CT):
                    i = j // 2
                    act.wait_ge(lora_done, j + 1)
                    dst, bias = (decay, "w0") if j % 2 == 0 else (rate, "a0")
                    nc.scalar.activation(dst[:, i, :], big[:, j % 2, 0:TT], ACT.Sigmoid,
                                         bias=m.params[:, i, par(bias):par(bias) + 1]).then_inc(lora_taken, 1)
                for i, (_, n) in enumerate(TOK_TILES):
                    act.wait_ge(gate_done, i + 1)
                    nc.scalar.copy(m.gate[0:n, i, :], pg[0:n, :]).then_inc(gate_taken, 1)
                for i in range(CT):
                    if i >= 1:
                        act.wait_ge(ss_done, i)
                    nc.scalar.activation(sq[:], m.zs[:, shift_index("k", i), :], ACT.Square,
                                         scale=m.params[:, i, par("k_k"):par("k_k") + 1]).then_inc(sq_ready, 1)
                    act.wait_ge(ss_done, i + 1)
                    if i >= 1:
                        act.wait_ge(kk_used, i)
                    nc.scalar.activation(norm[:], big[:, 0, 0:TT], ACT.Sqrt).then_inc(norm_root, 1)
                    act.wait_ge(cum_ready, i + 1)
                    if i >= 1:
                        act.wait_ge(scaled_ready, i)
                    nc.scalar.activation(e_before[:], cum_before[:], ACT.Exp, scale=-DECAY_SCALE)
                    nc.scalar.activation(e_after[:], cum[:], ACT.Exp, scale=-DECAY_SCALE)
                    nc.scalar.activation(e_inverse[:], cum[:], ACT.Exp, scale=DECAY_SCALE)
                    nc.scalar.activation(e_end[:], cum_end[:], ACT.Exp, scale=DECAY_SCALE)
                    nc.scalar.activation(m.chunk_decay[:, i, :], cum[:, L - 1:T:L], ACT.Exp, scale=-DECAY_SCALE)
                    nc.scalar.activation(m.sample_vec[:, 0, i, :], decay[:, i, T:TT], ACT.Exp, scale=-DECAY_SCALE).then_inc(exp_ready, 1)
                    for q in range(NTURN):
                        g = NTURN * i + q
                        act.wait_ge(turned, g + 1)
                        if q < 4:
                            nc.scalar.copy((m.a_rows, m.b_rows, m.k_rows, m.v_rows)[q][:, 0:TM, i * P:(i + 1) * P],
                                           turn[:, g % 2, :].rearrange("p (j c) -> p j c", j=TM)).then_inc(turned_taken, 1)
                        else:
                            nc.scalar.copy(m.v_rows[0:B, TM, i * P:(i + 1) * P], turn[0:B, g % 2, 0:P]).then_inc(turned_taken, 1)

            @block.vector
            def _(dve):
                ch = Chain(dve, m.vector_step, m.vector_count)
                for i in range(CT):
                    r = m.zs[:, shift_index("r", i), :]
                    k = m.zs[:, shift_index("k", i), :]
                    v = m.zs[:, shift_index("v", i), :]
                    if i == 0:
                        dve.wait_ge(lora_taken, 2 * CT)
                    if i >= 1:
                        dve.wait_ge(exp_ready, i)
                        dve.wait_ge(scaled_ready, i)
                    nc.vector.tensor_scalar(kk[:], k, m.params[:, i, par("k_k"):par("k_k") + 1], None, ALU.mult)
                    nc.vector.tensor_scalar(tmp[:], rate[:, i, :], 1.0, m.params[:, i, par("k_a"):par("k_a") + 1],
                                            ALU.subtract, ALU.mult)
                    ch.link(nc.vector.tensor_tensor_scan(cum[:], m.chunk_keep[:], decay[:, i, 0:T], 0.0, ALU.mult, ALU.add))
                    nc.vector.tensor_tensor(cum_before[:], cum[:], decay[:, i, 0:T], ALU.subtract)
                    nc.vector.tensor_tensor(cum_end[:].rearrange("p (c l) -> p c l", l=L), cum[:].rearrange("p (c l) -> p c l", l=L),
                                            cum[:, L - 1:T:L].unsqueeze(2).broadcast_to([P, NCH, L]), ALU.subtract).then_inc(cum_ready, 1)
                    ch.link(nc.vector.scalar_tensor_tensor(k2[:], tmp[:], 1.0, k, ALU.add, ALU.mult))
                    if i >= 1:
                        dve.wait_ge(bonus_done, i)
                    nc.vector.scalar_tensor_tensor(rk[:], r, m.params[:, i, par("r_k"):par("r_k") + 1], k2[:],
                                                   ALU.mult, ALU.mult).then_inc(bonus_in, 1)
                    dve.wait_ge(norm_root, i + 1)
                    ch.link(nc.vector.tensor_scalar(tmp[:], norm[:], 1e-12, None, ALU.max))
                    ch.link(nc.vector.reciprocal(tmp[:], tmp[:]))
                    ch.link(nc.vector.tensor_tensor(kk[:], kk[:], tmp[:], ALU.mult))
                    nc.vector.tensor_copy(m.sample_vec[:, 1, i, :], kk[:, T:TT]).then_inc(kk_used, 1)
                    ch.link(nc.vector.scalar_tensor_tensor(kb[:], kk[:], -1.0, rate[:, i, :], ALU.mult, ALU.mult))
                    nc.vector.tensor_copy(m.sample_vec[:, 2, i, :], kb[:, T:TT])
                    nc.vector.tensor_copy(m.sample_vec[:, 3, i, :], k2[:, T:TT])
                    nc.vector.tensor_copy(m.sample_vec[:, 4, i, :], r[:, T:TT])
                    nc.vector.tensor_copy(m.sample_vec[:, 5, i, :], v[:, T:TT])
                    dve.wait_ge(exp_ready, i + 1)
                    if i >= 1:
                        dve.wait_ge(turned, NTURN * (i - 1) + 3)
                    tiles = lambda ap: ap.rearrange("p (j t) -> p j t", j=TM)
                    nc.vector.tensor_tensor(m.read_decayed[:, i, :, 0, :], tiles(kk[:, 0:T]), tiles(e_before[:]), ALU.mult)
                    nc.vector.tensor_tensor(b_end[:], kb[:, 0:T], e_end[:], ALU.mult)
                    nc.vector.tensor_tensor(k_end[:], k2[:, 0:T], e_end[:], ALU.mult)
                    nc.vector.tensor_tensor(m.read_decayed[:, i, :, 1, :], tiles(r[:, 0:T]), tiles(e_after[:]), ALU.mult)
                    nc.vector.tensor_tensor(m.b_grown[:, i, :], kb[:, 0:T], e_inverse[:], ALU.mult)
                    nc.vector.tensor_tensor(m.k_grown[:, i, :], k2[:, 0:T], e_inverse[:], ALU.mult).then_inc(scaled_ready, 1)
                dve.wait_ge(bonus_done, CT)
                nc.vector.tensor_copy(m.bonus[:, 0:TM, :], pb[:, 0:TM * H].rearrange("p (j h) -> p j h", h=H))
                nc.vector.tensor_copy(m.bonus[0:B, TM, :], pb[0:B, TM * H:])

def solve_chunks(nc, m, ctx_out):
    SETS = TM * H
    with ExitStack() as ctx:
        def sb(name, shape, dt=F32):
            return ctx.enter_context(nc.sbuf_tensor(name, shape, dt))

        def ps(name, shape, dt=F32):
            return ctx.enter_context(nc.psum_tensor(name, shape, dt))

        def sem(name):
            m.spent.append(ctx_out.enter_context(nc.semaphore(name)))
            return m.spent[-1]

        lower = sb("lower", [P, SETS, L])
        sys_n = sb("sys_n", [P, L, L])
        sol_t = sb("sol_t", [P, L, L])
        prod = sb("prod", [P, L * L])
        sample_rows = sb("sample_rows", [B, 6, DC])
        sv = sb("sv", [P, 5, N])
        sval = sb("sval", [P, 32])
        free = m.zs[:].rearrange("p s t -> p (s t)")
        st, st_p, st_q = (free[:, i * 32 * N:(i + 1) * 32 * N].rearrange("p (v k) -> p v k", k=N) for i in range(3))
        s_a = sb("s_a", [P, 32])
        s_y = sb("s_y", [P, 32])
        sq = sb("ln_sq", [P, CT, TT])
        scale = sb("ln_scale", [P, TT])
        pa = ps("pa", [P, 2, 4, P])
        big = ps("big3", [P, 2, 1024])
        psv = ps("psv", [P, 2, 512])

        pairs_done = sem("pairs_done")
        pairs_taken = sem("pairs_taken")
        lower_stored = sem("lower_stored")
        sys_loaded = sem("sys_loaded")
        solved = sem("solved")
        inverse_cleared = sem("inverse_cleared")
        sol_stored = sem("sol_stored")
        sol_loaded = sem("sol_loaded")
        sample_turned = sem("sample_turned")
        sample_copied = sem("sample_copied")
        sample_stored = sem("sample_stored")
        sample_loaded = sem("sample_loaded")
        state_loaded = sem("state_loaded")
        outer_done = sem("outer_done")
        reduced = sem("reduced")
        y_stored = sem("y_stored")
        y_loaded = sem("y_loaded")
        mean_done = sem("mean_done")
        centred = sem("centred")
        squared = sem("squared")
        var_done = sem("var_done")
        rooted = sem("rooted")
        scaled = sem("scaled")
        gated = sem("gated")
        sample_state_stored = sem("sample_state_stored")

        with nc.Block() as block:
            @block.tensor
            def _(pe):
                for g in range(2 * TM):
                    j, odd = g // 2, g % 2
                    if g >= 2:
                        pe.wait_ge(pairs_taken, g - 1)
                    for h in range(odd, H, 2):
                        rows = slice(N * odd, N * odd + N)
                        last = nc.tensor.matmul(pa[:, odd, h // 2, :], m.read_decayed[rows, h // 2, j, 0, :],
                                                m.b_grown[rows, h // 2, j * P:(j + 1) * P], start=True, stop=True)
                    last.then_inc(pairs_done, 1)
                for s in range(6):
                    if s >= 2:
                        pe.wait_ge(sample_copied, s - 1)
                    for i in range(CT):
                        last = nc.tensor.transpose(psv[0:B, s % 2, i * P:(i + 1) * P], m.sample_vec[:, s, i, :], m.ident[:])
                    last.then_inc(sample_turned, 1)
                for c0, c1 in ((0, T), (T, TT)):
                    for i in range(CT):
                        last = nc.tensor.matmul(big[:, 0, c0:c1], m.ones_mean[:], m.conv[:, i, c0:c1], start=(i == 0), stop=(i == CT - 1))
                last.then_inc(mean_done, 1)
                pe.wait_ge(squared, 1)
                for c0, c1 in ((0, T), (T, TT)):
                    for i in range(CT):
                        last = nc.tensor.matmul(big[:, 1, c0:c1], m.ones_mean[:], sq[:, i, c0:c1], start=(i == 0), stop=(i == CT - 1))
                last.then_inc(var_done, 1)

            @block.sync
            def _(sp):
                sp.dma_start(st.rearrange("p v k -> p (v k)"), m.state_wkv).then_inc(state_loaded, 16)
                sp.wait_ge(pairs_taken, 2 * TM)
                sp.dma_start(m.scr_lower.rearrange("(s c) (t j) -> (c t) s j", c=CM, j=L), lower[:]).then_inc(lower_stored, 16)
                sp.wait_ge(sample_copied, 6)
                sp.dma_start(m.scr_sample.rearrange("s b c -> b s c"), sample_rows[:]).then_inc(sample_stored, 16)
                sp.wait_ge(lower_stored, 16)
                sp.dma_start(sys_n[:].rearrange("p t j -> p (t j)"), m.scr_lower).then_inc(sys_loaded, 16)
                sp.wait_ge(sample_stored, 16)
                for half in range(2):
                    sp.dma_start(sv[half::2, :, :], m.scr_sample[0:5].rearrange("s b (h n) -> (b h) s n", n=N)).then_inc(sample_loaded, 16)
                sp.dma_start(sval[:], m.scr_sample[5].rearrange("b (h two v) -> (b h two) v", two=2, v=32)).then_inc(sample_loaded, 16)
                sp.wait_ge(outer_done, 4)
                sp.dma_start(m.new_wkv_s, st.rearrange("p v k -> p (v k)")).then_inc(sample_state_stored, 16)
                sp.wait_ge(reduced, 2)
                sp.dma_start(m.scr_y.rearrange("b (h two v) -> (b h two) v", two=2, v=32), s_y[:]).then_inc(y_stored, 16)
                sp.wait_ge(y_stored, 16)
                sp.dma_start(m.y_sample_rows[:], m.scr_y).then_inc(y_loaded, 16)
                sp.wait_ge(solved, 1)
                sp.dma_start(m.scr_solved, sol_t[:].rearrange("p j t -> p (j t)")).then_inc(sol_stored, 16)
                sp.wait_ge(sol_stored, 16)
                sp.wait_ge(inverse_cleared, 1)
                for c in range(CM):
                    sp.dma_start(m.inverse[L * c:L * (c + 1), :, L * c:L * (c + 1)],
                                 m.scr_solved.rearrange("(s c) (j t) -> c j s t", c=CM, j=L)[c]).then_inc(sol_loaded, 16)
                sp.wait_ge(sol_loaded, 16 * CM)
                sp.wait_ge(y_loaded, 16)
                sp.wait_ge(sample_state_stored, 16)

            @block.scalar
            def _(act):
                for s in range(6):
                    act.wait_ge(sample_turned, s + 1)
                    nc.scalar.copy(sample_rows[:, s, :], psv[0:B, s % 2, :]).then_inc(sample_copied, 1)
                act.wait_ge(centred, 1)
                for i in range(CT):
                    last = nc.scalar.activation(sq[:, i, :], m.conv[:, i, :], ACT.Square)
                last.then_inc(squared, 1)
                act.wait_ge(var_done, 1)
                nc.scalar.activation(scale[:], big[:, 1, 0:TT], ACT.Sqrt, bias=m.eps_ln[:]).then_inc(rooted, 1)
                act.wait_ge(scaled, 1)
                for i in range(CT):
                    last = nc.scalar.activation(sq[:, i, :], m.conv[:, i, :], ACT.Sigmoid,
                                                scale=m.params[:, i, par("conv_ln_g"):par("conv_ln_g") + 1],
                                                bias=m.params[:, i, par("conv_ln_b"):par("conv_ln_b") + 1])
                last.then_inc(gated, 1)

            @block.gpsimd
            def _(pool):
                ch = Chain(pool, m.pool_step, m.pool_count)
                keys = lambda s: sv[:, s, :].unsqueeze(1).broadcast_to([P, 32, N])
                values = lambda ap: ap.unsqueeze(2).broadcast_to([P, 32, N])
                nc.gpsimd.memset(m.inverse[:], 0.0).then_inc(inverse_cleared, 1)
                pool.wait_ge(state_loaded, 16)
                pool.wait_ge(sample_loaded, 48)
                nc.gpsimd.tensor_tensor(st_p, st, keys(1), ALU.mult).then_inc(outer_done, 1)
                ch.link(nc.gpsimd.tensor_tensor(st_q, values(sval[:]), keys(3), ALU.mult))
                ch.link(nc.gpsimd.tensor_tensor(st, st, keys(0), ALU.mult))
                ch.link(nc.gpsimd.tensor_tensor(st, st, st_q, ALU.add))
                pool.wait_ge(reduced, 1)
                nc.gpsimd.tensor_tensor(st_q, values(s_a[:]), keys(2), ALU.mult).then_inc(outer_done, 1)
                pool.wait_ge(outer_done, 2)
                nc.gpsimd.tensor_tensor(st, st, st_q, ALU.add).then_inc(outer_done, 1)
                pool.wait_ge(outer_done, 3)
                nc.gpsimd.tensor_tensor(st_p, st, keys(4), ALU.mult).then_inc(outer_done, 1)

            @block.vector
            def _(dve):
                ch = Chain(dve, m.vector_step, m.vector_count)
                for g in range(2 * TM):
                    dve.wait_ge(pairs_done, g + 1)
                    sets = slice(H * (g // 2) + g % 2, H * (g // 2) + H, 2)
                    for c in range(CM):
                        r = slice(L * c, L * (c + 1))
                        last = nc.vector.tensor_tensor(lower[r, sets, :], pa[r, g % 2, :, L * c:L * (c + 1)],
                                                       m.below[r, :].unsqueeze(1).broadcast_to([L, 4, L]), ALU.mult)
                    last.then_inc(pairs_taken, 1)
                ch.link(nc.vector.memset(sol_t[:], 0.0))
                ch.link(nc.vector.memset(sol_t[:].rearrange("p j t -> p (j t)")[:, 0:L * L:L + 1], 1.0))
                dve.wait_ge(mean_done, 1)
                for i in range(CT):
                    last = nc.vector.tensor_tensor(m.conv[:, i, :], m.conv[:, i, :], big[:, 0, 0:TT], ALU.subtract)
                last.then_inc(centred, 1)
                dve.wait_ge(sys_loaded, 16)
                for t in range(1, L):
                    if t == 4:
                        dve.wait_ge(rooted, 1)
                        ch.link(nc.vector.reciprocal(scale[:], scale[:]))
                        for i in range(CT):
                            last = nc.vector.tensor_tensor(m.conv[:, i, :], m.conv[:, i, :], scale[:], ALU.mult)
                        last.then_inc(scaled, 1)
                    if t == 20:
                        dve.wait_ge(scaled, 1)
                        dve.wait_ge(gated, 1)
                        for i in range(CT):
                            ch.link(nc.vector.tensor_scalar(m.conv[:, i, :], m.conv[:, i, :],
                                                            m.params[:, i, par("conv_ln_g"):par("conv_ln_g") + 1],
                                                            m.params[:, i, par("conv_ln_b"):par("conv_ln_b") + 1], ALU.mult, ALU.add))
                            nc.vector.tensor_tensor(m.conv[:, i, :], m.conv[:, i, :], sq[:, i, :], ALU.mult)
                    if t == 6:
                        dve.wait_ge(outer_done, 1)
                        nc.vector.tensor_reduce(s_a[:], st_p, AX, ALU.add).then_inc(reduced, 1)
                    if t == 28:
                        dve.wait_ge(outer_done, 4)
                        nc.vector.tensor_reduce(s_y[:], st_p, AX, ALU.add).then_inc(reduced, 1)
                    pr = prod[:, 0:t * t].rearrange("p (j s) -> p j s", j=t)
                    ch.link(nc.vector.tensor_tensor(pr, sol_t[:, 0:t, 0:t], sys_n[:, t, 0:t].unsqueeze(1).broadcast_to([P, t, t]), ALU.mult))
                    last = nc.vector.tensor_reduce(sol_t[:, 0:t, t], pr, AX, ALU.add)
                    if t < L - 1:
                        ch.link(last)
                last.then_inc(solved, 1)


def recur(nc, m, ctx_out):
    with ExitStack() as ctx:
        def sb(name, shape, dt=F32):
            return ctx.enter_context(nc.sbuf_tensor(name, shape, dt))

        def ps(name, shape, dt=F32):
            return ctx.enter_context(nc.psum_tensor(name, shape, dt))

        def sem(name):
            return ctx_out.enter_context(nc.semaphore(name))

        inside = m.zs[:].rearrange("p s t -> p (s t)")[:, 0:2 * H * 3 * P].rearrange("p (b h a t) -> p b h a t", b=2, h=H, a=3)
        pushed = sb("pushed", [P, DC])
        w2 = sb("w2", [P, 2, DC])
        w1_t = sb("w1_t", [P, 2, CT, P])
        u = sb("u", [P, 2, DC])
        state = sb("state", [P, 2, CT, N])
        y = sb("y", [P, 2, DC])
        y_sq = sb("y_sq", [P, DC])
        o = sb("o", [P, 2, DC])
        stat = sb("stat", [P, 4, H])
        gn_g = sb("gn_g", [P, DC])
        gn_b = sb("gn_b", [P, DC])
        state_rows = sb("state_rows", [N, H, N])
        pin = ps("pin", [P, 2, 512])
        pw = ps("pw", [P, 2, 512])
        pu = ps("pu", [P, 2, 2, CT, N])
        pst = ps("pst", [P, CT, P])
        py = ps("py", [P, 512])

        gn_loaded = sem("gn_loaded")
        inside_done = sem("inside_done")
        inside_taken = sem("inside_taken")
        push_done = sem("push_done")
        push_taken = sem("push_taken")
        w2_done = sem("w2_done")
        w2_taken = sem("w2_taken")
        w1_done = sem("w1_done")
        w1_taken = sem("w1_taken")
        u_done = sem("u_done")
        u_taken = sem("u_taken")
        state_done = sem("state_done")
        state_ready = sem("state_ready")
        y_state_done = sem("y_state_done")
        y_done = sem("y_done")
        y_taken = sem("y_taken")
        y_state_taken = sem("y_state_taken")
        rooted = sem("gn_rooted")
        gn_var_ready = sem("gn_var_ready")
        gn_squared = sem("gn_squared")
        centred = sem("gn_centred")
        o_ready = sem("o_ready")
        o_turned = sem("o_turned")
        o_taken = sem("o_taken")
        final_turned = sem("final_turned")
        final_ready = sem("final_ready")
        final_stored = sem("final_stored")

        def rows(h):
            return slice(N * (h % 2), N * (h % 2) + N)

        with nc.Block() as block:
            @block.gpsimd
            def _(pool):
                for spent in m.spent:
                    pool.sem_clear(spent)

            @block.sync
            def _(sp):
                sp.dma_start(gn_g[:], m.vec["gn_g"].broadcast_to([P, DC])).then_inc(gn_loaded, 16)
                sp.dma_start(gn_b[:], m.vec["gn_b"].broadcast_to([P, DC])).then_inc(gn_loaded, 16)
                sp.wait_ge(final_ready, 2)
                sp.dma_start(m.new_wkv_p.rearrange("h v k -> v h k"), state_rows[:]).then_inc(final_stored, 16)
                sp.wait_ge(final_stored, 16)

            @block.tensor
            def _(pe):
                def products(j, h):
                    g = H * j + h
                    if g >= 2:
                        pe.wait_ge(inside_taken, g - 1)
                    c = slice(j * P, (j + 1) * P)
                    nc.tensor.matmul(pin[:, g % 2, 0:2 * P], m.k_grown[rows(h), h // 2, c],
                                     m.read_decayed[rows(h), h // 2, j].rearrange("p a t -> p (a t)"), start=True, stop=True)
                    nc.tensor.matmul(pin[:, g % 2, 2 * P:3 * P], m.b_grown[rows(h), h // 2, c],
                                     m.read_decayed[rows(h), h // 2, j, 1, :], start=True, stop=True).then_inc(inside_done, 1)

                def push(j):
                    pe.wait_ge(inside_taken, H * (j + 1))
                    if j >= 1:
                        pe.wait_ge(w2_taken, j)
                    for h in range(H):
                        last = nc.tensor.matmul(pw[:, 0, h * N:(h + 1) * N], inside[:, j % 2, h, 0, :], m.v_rows[:, j, h * N:(h + 1) * N],
                                                start=True, stop=True)
                    last.then_inc(push_done, 1)
                    if j >= 1:
                        pe.wait_ge(w1_taken, j)
                    for h in range(H):
                        last = nc.tensor.matmul(pw[rows(h), 1, (h // 2) * P:(h // 2 + 1) * P], m.a_rows[:, j, h * N:(h + 1) * N],
                                                m.inverse[:, H * j + h, :], start=True, stop=True)
                    last.then_inc(w1_done, 1)
                    pe.wait_ge(push_taken, j + 1)
                    for h in range(H):
                        last = nc.tensor.matmul(pw[:, 0, h * N:(h + 1) * N], m.inverse[:, H * j + h, :], pushed[:, h * N:(h + 1) * N],
                                                start=True, stop=True)
                    last.then_inc(w2_done, 1)

                for h in range(H):
                    products(0, h)
                push(0)
                for j in range(TM):
                    for c in range(CM):
                        n = CM * j + c
                        q = slice(L * c, L * (c + 1))
                        pe.wait_ge(w1_taken, j + 1)
                        pe.wait_ge(state_ready, n + 1)
                        if n >= 1:
                            pe.wait_ge(u_taken, n)
                        if c == 0 and j >= 1:
                            pe.wait_ge(y_state_taken, j)
                        for h in range(H):
                            last = nc.tensor.matmul(pu[q, h % 2, 0, h // 2, :], w1_t[rows(h), j % 2, h // 2, q],
                                                    state[rows(h), n % 2, h // 2, :], start=True, stop=True)
                        last.then_inc(u_done, 1)
                        if j + 1 < TM:
                            for h in (2 * c, 2 * c + 1):
                                products(j + 1, h)
                        pe.wait_ge(u_taken, n + 1)
                        for h in range(H):
                            hc = slice(h * N, (h + 1) * N)
                            nc.tensor.matmul(pst[rows(h), h // 2, 0:N], m.b_rows[q, j, hc], u[q, j % 2, hc], start=True, stop=False)
                            last = nc.tensor.matmul(pst[rows(h), h // 2, 0:N], m.k_rows[q, j, hc], m.v_rows[q, j, hc],
                                                    start=False, stop=True)
                        last.then_inc(state_done, 1)
                        for h in range(H):
                            last = nc.tensor.matmul(pu[q, h % 2, 1, h // 2, :], m.read_decayed[rows(h), h // 2, j, 1, q],
                                                    state[rows(h), n % 2, h // 2, :], start=True, stop=True)
                        last.then_inc(y_state_done, 1)
                    if j >= 1:
                        pe.wait_ge(y_taken, j)
                    for h in range(H):
                        hc = slice(h * N, (h + 1) * N)
                        nc.tensor.matmul(py[:, hc], inside[:, j % 2, h, 1, :], m.v_rows[:, j, hc], start=True, stop=False)
                        last = nc.tensor.matmul(py[:, hc], inside[:, j % 2, h, 2, :], u[:, j % 2, hc], start=False, stop=True)
                    last.then_inc(y_done, 1)
                    if j + 1 < TM:
                        push(j + 1)
                pe.wait_ge(state_ready, NCH + 1)
                pe.wait_ge(u_taken, NCH)
                pe.wait_ge(y_state_taken, TM)
                for h in range(H):
                    last = nc.tensor.transpose(pu[0:N, h % 2, 0, h // 2, :], state[rows(h), NCH % 2, h // 2, :], m.ident[rows(h), rows(h)])
                last.then_inc(final_turned, 1)
                for i, (t0, n) in enumerate(TOK_TILES):
                    pe.wait_ge(o_ready, i + 1)
                    pe.wait_ge(w1_taken, TM)
                    if i >= 1:
                        pe.wait_ge(o_taken, i)
                    for k in range(CT):
                        last = nc.tensor.transpose(pw[:, 1, k * P:k * P + n], o[0:n, i % 2, k * P:(k + 1) * P], m.ident[0:n, 0:n])
                    last.then_inc(o_turned, 1)

            @block.scalar
            def _(act):
                def copy_pushed(j):
                    act.wait_ge(push_done, j + 1)
                    nc.scalar.copy(pushed[:], pw[:, 0, :]).then_inc(push_taken, 1)
                    act.wait_ge(w1_done, j + 1)
                    nc.scalar.copy(w1_t[:, j % 2, :, :], pw[:, 1, :].rearrange("p (i t) -> p i t", i=CT)).then_inc(w1_taken, 1)
                    act.wait_ge(w2_done, j + 1)
                    nc.scalar.copy(w2[:, j % 2, :], pw[:, 0, :]).then_inc(w2_taken, 1)

                def norm_part(i, n):
                    act.wait_ge(centred, i + 1)
                    nc.scalar.activation(y_sq[0:n, :], y[0:n, i % 2, :], ACT.Square).then_inc(gn_squared, 1)
                    act.wait_ge(gn_var_ready, i + 1)
                    nc.scalar.activation(stat[0:n, 2, :], stat[0:n, 1, :], ACT.Sqrt, scale=1.0 / N, bias=m.eps_gn[0:n, :]).then_inc(rooted, 1)

                copy_pushed(0)
                for j in range(TM):
                    act.wait_ge(y_state_done, CM * (j + 1))
                    if j >= 2:
                        act.wait_ge(o_ready, j - 1)
                    nc.scalar.copy(y[:, j % 2, :].rearrange("p (i two c) -> p two i c", two=2, c=N), pu[:, :, 1, :, :]).then_inc(y_state_taken, 1)
                    if j + 1 < TM:
                        copy_pushed(j + 1)
                    if j >= 1:
                        norm_part(j - 1, P)
                act.wait_ge(final_turned, 1)
                nc.scalar.copy(state_rows[:].rearrange("v (i two) k -> v two i k", two=2), pu[0:N, :, 0, :, :]).then_inc(final_ready, 2)

                def copy_out(i):
                    t0, n = TOK_TILES[i]
                    act.wait_ge(o_turned, i + 1)
                    nc.scalar.copy(m.o_t[:, :, t0:t0 + n],
                                   pw[:, 1, :].rearrange("p (k t) -> p k t", k=CT)[:, :, 0:n]).then_inc(o_taken, 1)

                norm_part(TM - 1, P)
                for i in range(TM - 2):
                    copy_out(i)
                norm_part(TM, B)
                for i in range(TM - 2, NT):
                    copy_out(i)

            @block.vector
            def _(dve):
                ch = Chain(dve, m.vector_step, m.vector_count)

                def mask(j, h):
                    g = H * j + h
                    dve.wait_ge(inside_done, g + 1)
                    if j >= 2:
                        dve.wait_ge(y_done, j - 1)
                    nc.vector.tensor_tensor(inside[:, j % 2, h, :, :], pin[:, g % 2, 0:3 * P].rearrange("p (a t) -> p a t", a=3),
                                            m.inside_mask[:], ALU.mult).then_inc(inside_taken, 1)

                def group_norm(i, n):
                    b = i % 2
                    yv = y[0:n, b, :].rearrange("p (h c) -> p h c", h=H)
                    per_head = lambda ap: ap.unsqueeze(2).broadcast_to([n, H, N])
                    if i < TM:
                        dve.wait_ge(y_state_taken, i + 1)
                        dve.wait_ge(y_done, i + 1)
                        nc.vector.tensor_tensor(y[:, b, :], y[:, b, :], py[:], ALU.add).then_inc(y_taken, 1)
                        dve.wait_ge(y_taken, i + 1)
                    else:
                        ch.link(nc.vector.tensor_copy(y[0:B, b, :], m.y_sample_rows[:]))
                    ch.link(nc.vector.tensor_reduce(stat[0:n, 0, :], yv, AX, ALU.add))
                    ch.link(nc.vector.tensor_scalar(stat[0:n, 0, :], stat[0:n, 0, :], 1.0 / N, None, ALU.mult))
                    nc.vector.tensor_tensor(yv, yv, per_head(stat[0:n, 0, :]), ALU.subtract).then_inc(centred, 1)
                    dve.wait_ge(gn_squared, i + 1)
                    nc.vector.tensor_reduce(stat[0:n, 1, :], y_sq[0:n, :].rearrange("p (h c) -> p h c", h=H), AX, ALU.add).then_inc(gn_var_ready, 1)
                    dve.wait_ge(rooted, i + 1)
                    ch.link(nc.vector.reciprocal(stat[0:n, 3, :], stat[0:n, 2, :]))
                    ch.link(nc.vector.tensor_tensor(yv, yv, per_head(stat[0:n, 3, :]), ALU.mult))
                    ch.link(nc.vector.tensor_tensor(y[0:n, b, :], y[0:n, b, :], gn_g[0:n, :], ALU.mult))
                    if i >= 2:
                        dve.wait_ge(o_turned, i - 1)
                    ov = o[0:n, b, :].rearrange("p (h c) -> p h c", h=H)
                    ch.link(nc.vector.tensor_tensor(ov, m.v_rows[0:n, i, :].rearrange("p (h c) -> p h c", h=H), per_head(m.bonus[0:n, i, :]), ALU.mult))
                    ch.link(nc.vector.tensor_tensor(y[0:n, b, :], y[0:n, b, :], gn_b[0:n, :], ALU.add))
                    ch.link(nc.vector.tensor_tensor(o[0:n, b, :], o[0:n, b, :], y[0:n, b, :], ALU.add))
                    nc.vector.tensor_tensor(o[0:n, b, :], o[0:n, b, :], m.gate[0:n, i, :], ALU.mult).then_inc(o_ready, 1)

                nc.vector.memset(state[:, 0, :, :], 0.0).then_inc(state_ready, 1)
                dve.wait_ge(gn_loaded, 32)
                for h in range(H):
                    mask(0, h)
                for j in range(TM):
                    for c in range(CM):
                        n = CM * j + c
                        q = slice(L * c, L * (c + 1))
                        dve.wait_ge(w2_taken, j + 1)
                        dve.wait_ge(u_done, n + 1)
                        by_parity = lambda ap: ap.rearrange("p (i two c) -> p two i c", two=2, c=N)
                        nc.vector.tensor_tensor(by_parity(u[q, j % 2, :]), pu[q, :, 0, :, :], by_parity(w2[q, j % 2, :]),
                                                ALU.add).then_inc(u_taken, 1)
                        if j + 1 < TM:
                            for h in (2 * c, 2 * c + 1):
                                mask(j + 1, h)
                        if n >= 1:
                            dve.wait_ge(y_state_done, n)
                        dve.wait_ge(state_ready, n + 1)
                        ch.link(nc.vector.tensor_tensor(state[:, (n + 1) % 2, :, :], state[:, n % 2, :, :],
                                                        m.chunk_decay[:, :, n:n + 1].broadcast_to([P, CT, N]), ALU.mult))
                        dve.wait_ge(state_done, n + 1)
                        nc.vector.tensor_tensor(state[:, (n + 1) % 2, :, :], state[:, (n + 1) % 2, :, :], pst[:, :, 0:N],
                                                ALU.add).then_inc(state_ready, 1)
                    if j >= 1:
                        group_norm(j - 1, P)
                group_norm(TM - 1, P)
                group_norm(TM, B)


def mix(nc, m, ctx_out):
    BIG = 1e30
    GONE = -3e38
    with ExitStack() as ctx:
        def sb(name, shape, dt=F32):
            return ctx.enter_context(nc.sbuf_tensor(name, shape, dt))

        def ps(name, shape, dt=F32):
            return ctx.enter_context(nc.psum_tensor(name, shape, dt))

        def sem(name):
            return ctx_out.enter_context(nc.semaphore(name))

        w_out = sb("w_out_sb", [P, KD, D])
        x_rows = sb("x_rows5", [P, 2, D])
        x1 = sb("x1", [P, NT, D])
        x1_t = sb("x1_t", [P, KD, TT])
        ln_g = sb("ln1_g", [P, D])
        ln_b = sb("ln1_b", [P, D])
        router_w = sb("router_w_sb", [P, KD, E])
        router_b = sb("router_b", [P, E])
        sh_w = sb("sh_w", [P, 2, KD, FE])
        sh_d = sb("sh_d", [P, 2, D])
        sh_sig = sb("sh_sig", [P, TT])
        sh_h = sb("sh_h", [P, 2, TT])
        stats = sb("stats", [P, 2, 6])
        aggr = sb("aggr", [P, 4])
        scores = sb("scores", [P, NT, E])
        sel = sb("sel", [P, NT, E])
        top = sb("top", [P, NT * G, 8])
        grp = sb("grp", [P, NT, G])
        gt = sb("gt", [P, NT, G, G])
        eq = sb("eq", [P, NT, G, G])
        keep = sb("keep", [P, NT, G])
        hit = sb("hit", [P, NT, E])
        gsum = sb("gsum", [P, NT])
        before = sb("before", [P, P])
        zero_rows = sb("zero_rows", [CAP, D])
        first = sb("first", [P, G, G])
        f0 = sb("f0", [P, 2, D])
        jobs3 = sb("jobs3", [P, m.EXTRA, E])
        cnt = sb("cnt", [P, 4, E])
        ph = ps("ph", [P, 2, 1024])
        pt = ps("pt5", [P, 2, 512])
        plog = ps("plog", [P, NT, E])
        ppos = ps("ppos", [P, NT + 1, E])

        loaded = sem("mix_loaded")
        x_loaded = [sem(f"x_again{i}") for i in range(2)]
        mixed = sem("mixed")
        mixed_taken = sem("mixed_taken")
        var_ready = sem("var_ready")
        rooted = sem("ln1_rooted")
        x1_ready = sem("x1_ready")
        x1_turned = sem("x1_turned")
        x1_t_ready = sem("x1_t_ready")
        x1_stored = sem("x1_stored")
        logits_done = sem("logits_done")
        scores_ready = sem("scores_ready")
        hits_ready = sem("hits_ready")
        positions_done = sem("positions_done")
        routing_consts = sem("routing_consts")
        sh_done = sem("sh_done")
        sh_sig_ready = sem("sh_sig_ready")
        sh_h_ready = sem("sh_h_ready")
        f_done = sem("f_done")
        f_taken = sem("f_taken")
        f_stored = [sem(f"f_stored{i}") for i in range(2)]
        x_used = sem("x_used")
        zeros_ready = sem("zero_rows_ready")

        with nc.Block() as block:
            @block.sync
            def _(sp):
                for i in range(2):
                    sp.dma_start(x_rows[:, i, :], m.x_prompt[i * P:(i + 1) * P, :]).then_inc(x_loaded[i], 16)
                sp.dma_start(w_out[:], m.w_out.rearrange("(k p) n -> p k n", p=P)).then_inc(loaded, 16)
                sp.dma_start(ln_g[:], m.vec["ln1_g"].broadcast_to([P, D])).then_inc(loaded, 16)
                sp.dma_start(ln_b[:], m.vec["ln1_b"].broadcast_to([P, D])).then_inc(loaded, 16)
                sp.dma_start(router_w[:], m.router_w.rearrange("(k p) n -> p k n", p=P)).then_inc(loaded, 16)
                sp.dma_start(router_b[:], m.vec["router_bias"].broadcast_to([P, E])).then_inc(loaded, 16)
                sp.dma_start(sh_w[:, 0], m.sh_gate.rearrange("(k p) n -> p k n", p=P)).then_inc(loaded, 16)
                sp.dma_start(sh_w[:, 1], m.sh_up.rearrange("(k p) n -> p k n", p=P)).then_inc(loaded, 16)
                sp.dma_start(sh_d[:], m.sh_down.rearrange("(k p) n -> p k n", p=P)).then_inc(loaded, 16)
                for i in range(2, NT):
                    t0, n = TOK_TILES[i]
                    sp.wait_ge(x_used, i - 1)
                    src = m.x_prompt[t0:t0 + n, :] if i < TM else m.x_sample
                    sp.dma_start(x_rows[0:n, i % 2, :], src).then_inc(x_loaded[i % 2], 16)
                for i, (t0, n) in enumerate(TOK_TILES):
                    sp.wait_ge(x1_ready, i + 1)
                    sp.dma_start(m.scr_x1[t0:t0 + n, :], x1[0:n, i, :]).then_inc(x1_stored, 16)
                for i, (t0, n) in enumerate(TOK_TILES):
                    sp.wait_ge(f_taken, 2 * (i + 1))
                    sp.dma_start(m.scr_f[t0:t0 + n, :], f0[0:n, i % 2, :]).then_inc(f_stored[i % 2], 16)
                sp.wait_ge(zeros_ready, 1)
                sp.dma_start(m.scr_f[TT:TT + CAP, :], zero_rows[:]).then_inc(x1_stored, 16)
                sp.wait_ge(x1_stored, 16 * (NT + 1))
                sp.wait_ge(f_stored[0], 16 * 3)
                sp.wait_ge(f_stored[1], 16 * 2)

            @block.tensor
            def _(pe):
                pe.wait_ge(loaded, 16 * 8)
                def turn(i):
                    t0, n = TOK_TILES[i]
                    pe.wait_ge(x1_ready, i + 1)
                    for half in range(2):
                        g = 2 * i + half
                        if g >= 2:
                            pe.wait_ge(x1_t_ready, g - 1)
                        for k in range(4):
                            d0 = (4 * half + k) * P
                            last = nc.tensor.transpose(pt[:, half, k * P:k * P + n], x1[0:n, i, d0:d0 + P], m.ident[0:n, 0:n])
                        last.then_inc(x1_turned, 1)
                for i, (t0, n) in enumerate(TOK_TILES):
                    if i >= 2:
                        pe.wait_ge(mixed_taken, i - 1)
                    for c in range(2):
                        for k in range(KD):
                            lhs = m.conv[:, k, t0:t0 + n] if k < CT else m.o_t[:, k - CT, t0:t0 + n]
                            last = nc.tensor.matmul(ph[0:n, i % 2, c * 512:(c + 1) * 512], lhs, w_out[:, k, c * 512:(c + 1) * 512],
                                                    start=(k == 0), stop=(k == KD - 1))
                    last.then_inc(mixed, 1)
                    if i >= 1:
                        turn(i - 1)
                turn(NT - 1)
                pe.wait_ge(x1_t_ready, 2 * NT)
                for i, (t0, n) in enumerate(TOK_TILES):
                    for k in range(KD):
                        last = nc.tensor.matmul(plog[0:n, i, :], x1_t[:, k, t0:t0 + n], router_w[:, k, :], start=(k == 0), stop=(k == KD - 1))
                last.then_inc(logits_done, 1)
                pe.wait_ge(mixed_taken, NT)
                for j in range(2):
                    if j >= 1:
                        pe.wait_ge(sh_h_ready, j)
                    for part in range(2):
                        for k in range(KD):
                            for c0, c1 in ((0, T), (T, TT)):
                                last = nc.tensor.matmul(ph[:, part, c0:c1], sh_w[:, part, k, j * P:(j + 1) * P], x1_t[:, k, c0:c1],
                                                        start=(k == 0), stop=(k == KD - 1))
                        last.then_inc(sh_done, 1)
                pe.wait_ge(sh_h_ready, 2)
                pe.wait_ge(hits_ready, 1)
                pe.wait_ge(routing_consts, 2)
                for i in range(NT):
                    for j in range(i + 1):
                        last = nc.tensor.matmul(ppos[:, i, :], before[:] if j == i else m.ones[:], hit[:, j, :], start=(j == 0), stop=(j == i))
                for j in range(NT):
                    last = nc.tensor.matmul(ppos[:, NT, :], m.ones[:], hit[:, j, :], start=(j == 0), stop=(j == NT - 1))
                last.then_inc(positions_done, 1)
                for i, (t0, n) in enumerate(TOK_TILES):
                    if i >= 2:
                        pe.wait_ge(f_taken, 2 * (i - 1))
                    for c in range(2):
                        for j in range(2):
                            last = nc.tensor.matmul(ph[0:n, i % 2, c * 512:(c + 1) * 512], sh_h[:, j, t0:t0 + n], sh_d[:, j, c * 512:(c + 1) * 512],
                                                    start=(j == 0), stop=(j == 1))
                    last.then_inc(f_done, 1)

            @block.scalar
            def _(act):
                for i, (t0, n) in enumerate(TOK_TILES):
                    act.wait_ge(var_ready, i + 1)
                    nc.scalar.activation(aggr[0:n, 2:3], aggr[0:n, 1:2], ACT.Sqrt, bias=m.eps_ln[0:n, :]).then_inc(rooted, 1)
                    for half in range(2):
                        act.wait_ge(x1_turned, 2 * i + half + 1)
                        nc.scalar.copy(x1_t[:, 4 * half:4 * half + 4, t0:t0 + n],
                                       pt[:, half, :].rearrange("p (k t) -> p k t", k=4)[:, :, 0:n]).then_inc(x1_t_ready, 1)
                act.wait_ge(routing_consts, 1)
                act.wait_ge(logits_done, 1)
                nc.scalar.activation(scores[:, 0:TM, :], plog[:, 0:TM, :], ACT.Sigmoid)
                nc.scalar.activation(scores[0:B, TM, :], plog[0:B, TM, :], ACT.Sigmoid).then_inc(scores_ready, 1)
                for j in range(2):
                    act.wait_ge(sh_done, 2 * j + 1)
                    if j >= 1:
                        act.wait_ge(sh_h_ready, j)
                    nc.scalar.activation(sh_sig[:], ph[:, 0, 0:TT], ACT.Sigmoid).then_inc(sh_sig_ready, 1)

            @block.gpsimd
            def _(pool):
                nc.gpsimd.memset(scores[:, TM, :], 0.0).then_inc(routing_consts, 1)
                ch = Chain(pool, m.pool_step, m.pool_count)
                nc.gpsimd.memset(zero_rows[:], 0.0).then_inc(zeros_ready, 1)
                nc.gpsimd.memset(before[:], 1.0)
                ch.link(nc.gpsimd.memset(first[:], 1.0))
                nc.gpsimd.affine_select(out=before[:], in_=before[:], compare_op=ALU.is_gt, fill=0.0, base=0,
                                        pattern=[[1, P]], channel_multiplier=-1)
                nc.gpsimd.affine_select(out=first[:], in_=first[:], compare_op=ALU.is_gt, fill=0.0, base=0,
                                        pattern=[[1, G], [-1, G]], channel_multiplier=0).then_inc(routing_consts, 1)

            @block.vector
            def _(dve):
                ch = Chain(dve, m.vector_step, m.vector_count)

                def layer_norm(i, n):
                    r = x_rows[0:n, i % 2, :]
                    dve.wait_ge(x_loaded[i % 2], 16 * (i // 2 + 1))
                    dve.wait_ge(mixed, i + 1)
                    for c in range(2):
                        cs = slice(c * 512, (c + 1) * 512)
                        last = nc.vector.scalar_tensor_tensor(x1[0:n, i, cs], r[:, cs], ALPHA, ph[0:n, i % 2, cs], ALU.mult, ALU.add)
                    last.then_inc(mixed_taken, 1)
                    dve.wait_ge(mixed_taken, i + 1)
                    for c in range(2):
                        last = nc.vector.bn_stats(stats[0:n, c, :], x1[0:n, i, c * 512:(c + 1) * 512])
                    last.then_inc(x_used, 1)
                    dve.wait_ge(x_used, i + 1)
                    nc.vector.bn_aggr(aggr[0:n, 0:2], stats[0:n, :, :]).then_inc(var_ready, 1)
                    dve.wait_ge(var_ready, i + 1)
                    dve.wait_ge(rooted, i + 1)
                    ch.link(nc.vector.reciprocal(aggr[0:n, 3:4], aggr[0:n, 2:3]))
                    ch.link(nc.vector.tensor_scalar(x1[0:n, i, :], x1[0:n, i, :], aggr[0:n, 0:1], aggr[0:n, 3:4], ALU.subtract, ALU.mult))
                    ch.link(nc.vector.tensor_tensor(x1[0:n, i, :], x1[0:n, i, :], ln_g[0:n, :], ALU.mult))
                    nc.vector.tensor_tensor(x1[0:n, i, :], x1[0:n, i, :], ln_b[0:n, :], ALU.add).then_inc(x1_ready, 1)

                dve.wait_ge(loaded, 16 * 8)
                for i, (_, n) in enumerate(TOK_TILES):
                    layer_norm(i, n)
                dve.wait_ge(scores_ready, 1)
                dve.wait_ge(routing_consts, 2)
                ch.link(nc.vector.tensor_tensor(sel[:], scores[:], router_b[:].unsqueeze(1).broadcast_to([P, NT, E]), ALU.add))
                sel_g = sel[:].rearrange("p i (g e) -> p (i g) e", g=G)
                for g in range(NT * G):
                    last = nc.vector.max(top[:, g, :], sel_g[:, g, :])
                ch.link(last)
                grp_f = grp[:].rearrange("p i g -> p (i g)")
                ch.link(nc.vector.tensor_tensor(grp_f, top[:, :, 0], top[:, :, 1], ALU.add))
                me = grp[:].unsqueeze(3).broadcast_to([P, NT, G, G])
                other = grp[:].unsqueeze(2).broadcast_to([P, NT, G, G])
                nc.vector.tensor_tensor(gt[:], other, me, ALU.is_gt)
                ch.link(nc.vector.tensor_tensor(eq[:], other, me, ALU.is_equal))
                ch.link(nc.vector.tensor_tensor(eq[:], eq[:], first[:].unsqueeze(1).broadcast_to([P, NT, G, G]), ALU.mult))
                ch.link(nc.vector.tensor_tensor(gt[:], gt[:], eq[:], ALU.add))
                ch.link(nc.vector.tensor_reduce(grp[:], gt[:], AX, ALU.add))
                ch.link(nc.vector.tensor_scalar(keep[:], grp[:], float(KG), None, ALU.is_lt))
                keep_f = keep[:].rearrange("p i g -> p (i g)").unsqueeze(2).broadcast_to([P, NT * G, E // G])
                ch.link(nc.vector.tensor_tensor(sel_g, sel_g, keep_f, ALU.mult))
                ch.link(nc.vector.tensor_scalar(grp[:], keep[:], 1.0, BIG, ALU.subtract, ALU.mult))
                ch.link(nc.vector.tensor_tensor(sel_g, sel_g, grp_f.unsqueeze(2).broadcast_to([P, NT * G, E // G]), ALU.add))
                for i in range(NT):
                    last = nc.vector.max(top[:, i, :], sel[:, i, :])
                ch.link(last)
                for i in range(NT):
                    last = nc.vector.match_replace(hit[:, i, :], top[:, i, :], sel[:, i, :], GONE)
                ch.link(last)
                ch.link(nc.vector.tensor_scalar(hit[:], hit[:], GONE / 2, None, ALU.is_lt))
                nc.vector.tensor_tensor(hit[:], hit[:], m.is_token[:].unsqueeze(2).broadcast_to([P, NT, E]), ALU.mult).then_inc(hits_ready, 1)
                dve.wait_ge(hits_ready, 1)
                ch.link(nc.vector.tensor_tensor(scores[:], scores[:], hit[:], ALU.mult))
                ch.link(nc.vector.tensor_reduce(gsum[:], scores[:], AX, ALU.add))
                ch.link(nc.vector.tensor_scalar(gsum[:], gsum[:], 1e-20, None, ALU.add))
                ch.link(nc.vector.reciprocal(gsum[:], gsum[:]))
                by_tile = lambda ap: ap.rearrange("p i e -> p e i")
                ch.link(nc.vector.tensor_tensor(scores[:], scores[:], gsum[:].unsqueeze(2).broadcast_to([P, NT, E]), ALU.mult))
                ch.link(nc.vector.tensor_scalar(m.table[:, :, :, 1], by_tile(scores[:]), ROUTED_SCALE, None, ALU.mult))
                nc.vector.tensor_copy(m.table[:, :, :, 0], m.token_id[:].unsqueeze(1).broadcast_to([P, E, NT]))
                ch.link(nc.vector.memset(m.table[:, :, :, 2], 1.0))
                for j in range(2):
                    dve.wait_ge(sh_sig_ready, j + 1)
                    ch.link(nc.vector.tensor_tensor(sh_sig[:], sh_sig[:], ph[:, 0, 0:TT], ALU.mult))
                    dve.wait_ge(sh_done, 2 * j + 2)
                    nc.vector.tensor_tensor(sh_h[:, j, :], sh_sig[:], ph[:, 1, 0:TT], ALU.mult).then_inc(sh_h_ready, 1)
                dve.wait_ge(positions_done, 1)
                ch.link(nc.vector.scalar_tensor_tensor(sel[:], ppos[:, 0:NT, :], 1.0, hit[:], ALU.add, ALU.mult))
                ch.link(nc.vector.tensor_scalar(m.position[:], by_tile(sel[:]), 1.0, None, ALU.subtract))
                nc.vector.memset(cnt[:, 1:4, :], 0.0)
                ch.link(nc.vector.tensor_copy(cnt[:, 0, :], ppos[:, NT, :]))
                for b in range(1, m.MAX_JOBS):
                    ch.link(nc.vector.tensor_scalar(cnt[:, 2, :], cnt[:, 0, :], float(b * CAP), None, ALU.is_gt))
                    ch.link(nc.vector.tensor_tensor(cnt[:, 1, :], cnt[:, 1, :], cnt[:, 2, :], ALU.add))
                ch.link(nc.vector.tensor_tensor_scan(cnt[:, 2, :], m.ones[:, 0:E], cnt[:, 1, :], 0.0, ALU.mult, ALU.add))
                jk = m.job_index[:].unsqueeze(2).broadcast_to([P, m.EXTRA, E])
                ch.link(nc.vector.tensor_tensor(jobs3[:], cnt[:, 2, :].unsqueeze(1).broadcast_to([P, m.EXTRA, E]), jk, ALU.is_le))
                ch.link(nc.vector.tensor_reduce(m.job_expert[:], jobs3[:], AX, ALU.add))
                ch.link(nc.vector.tensor_tensor(jobs3[:], jobs3[:], cnt[:, 1, :].unsqueeze(1).broadcast_to([P, m.EXTRA, E]), ALU.mult))
                ch.link(nc.vector.tensor_reduce(m.job_base[:], jobs3[:], AX, ALU.add))
                ch.link(nc.vector.tensor_tensor(m.job_base[:], m.job_index[:], m.job_base[:], ALU.subtract))
                ch.link(nc.vector.tensor_scalar(m.job_base[:], m.job_base[:], 1.0, float(CAP), ALU.add, ALU.mult))
                nc.vector.tensor_copy(m.job_table[:, 1:], m.job_expert[0:1, :])
                ch.link(nc.vector.tensor_copy(m.job_table[:, 0:1], cnt[0:1, 2, E - 1:E]))
                for i, (t0, n) in enumerate(TOK_TILES):
                    dve.wait_ge(f_done, i + 1)
                    if i >= 2:
                        dve.wait_ge(f_stored[i % 2], 16 * (i // 2))
                    for c in range(2):
                        cs = slice(c * 512, (c + 1) * 512)
                        nc.vector.scalar_tensor_tensor(f0[0:n, i % 2, cs], x1[0:n, i, cs], ALPHA, ph[0:n, i % 2, cs],
                                                       ALU.mult, ALU.add).then_inc(f_taken, 1)


def experts(nc, m, ctx_out):
    NB = 4
    with ExitStack() as ctx:
        def sb(name, shape, dt=F32):
            return ctx.enter_context(nc.sbuf_tensor(name, shape, dt))

        def ps(name, shape, dt=F32):
            return ctx.enter_context(nc.psum_tensor(name, shape, dt))

        def sem(name):
            return ctx_out.enter_context(nc.semaphore(name))

        w_gate = m.w_gate + [sb(f"w_gate{i}", [P, KD, FE]) for i in range(len(m.w_gate), NB)]
        w_up = m.w_up + [sb(f"w_up{i}", [P, KD, FE]) for i in range(len(m.w_up), NB)]
        w_down = m.w_down + [sb(f"w_down{i}", [P, 2, D]) for i in range(len(m.w_down), NB)]
        member = sb("member", [P, 2, NT, CAP])
        entry = sb("entry", [CAP, 2, 3])
        row_in = sb("row_in", [CAP, 2], U32)
        row_out = sb("row_out", [CAP, 4], U32)
        weight = sb("weight", [CAP, 4])
        empty = sb("empty", [CAP, 2])
        x_list = sb("x_list", [CAP, 2, D])
        x_list_t = sb("x_list_t", [P, 2, KD, CAP])
        sig = sb("sig", [P, 2, 2, CAP])
        hid = sb("hid", [P, 2, 2, CAP])
        y_list = sb("y_list", [CAP, 2, D])
        moved = sb("moved", [P, NT])
        pl = ps("pl", [P, 2, 512])
        px = ps("px", [P, 2, 512])
        pgu = ps("pgu", [P, 2, 512])
        pyl = ps("pyl", [P, 2, 512])

        member_ready = sem("member_ready")
        list_done = sem("list_done")
        entry_ready = sem("entry_ready")
        rows_ready = sem("rows_ready")
        gathered = [sem(f"gathered{i}") for i in range(2)]
        added = [sem(f"added{i}") for i in range(2)]
        gate_loaded = [sem(f"gate_loaded{i}") for i in range(NB)]
        up_loaded = [sem(f"up_loaded{i}") for i in range(NB)]
        down_loaded = [sem(f"down_loaded{i}") for i in range(NB)]
        x_turned = sem("x_list_turned")
        x_ready = sem("x_list_ready")
        gu_done = sem("gu_done")
        sig_ready = sem("sig_ready")
        hid_ready = sem("hid_ready")
        y_done = sem("y_list_done")
        y_act = sem("y_act_ready")
        y_dve = sem("y_dve_ready")
        silu_ready = sem("silu_ready")
        waits_over = sem("waits_over")
        LOOPS = E // NB - 1
        KA = 512 // CAP if 512 // CAP < KD else KD // 2

        class Job:

            def __init__(self, turn, s):
                self.q = NB * turn + s
                self.s = s % NB
                self.b = s % 2
                self.pair = 2 * turn + s // 2
                self.before = 2 * turn + (s + 1) // 2
                self.turn = turn + s // NB

        def load(sp, job):
            q, s = job.q, job.s
            pick = lambda w: w[bass.ds(q, 1)].rearrange("o p n -> p (o n)")
            sp.dma_start(w_gate[s][:].rearrange("p k f -> p (k f)"), pick(m.exp_gate)).then_inc(gate_loaded[s], 16)
            sp.dma_start(w_up[s][:].rearrange("p k f -> p (k f)"), pick(m.exp_up)).then_inc(up_loaded[s], 16)
            sp.dma_start(w_down[s][:], m.exp_down[bass.ds(q, 1)].rearrange("o p j d -> p (o j) d")).then_inc(down_loaded[s], 16)

        def build_member(dve, job, first=False):
            q, s = job.q, job.s
            if not first:
                dve.wait_ge(list_done, q - 1)
            src = m.position[:, bass.ds(q, 1), :].rearrange("p o i -> p (o i)")
            nc.vector.tensor_tensor(member[:, s % 2], m.slot_index[:].unsqueeze(1).broadcast_to([P, NT, CAP]),
                                    src.unsqueeze(2).broadcast_to([P, NT, CAP]), ALU.is_equal).then_inc(member_ready, 1)

        def make_list(pe, job, first=False):
            q, s = job.q, job.s
            pe.wait_ge(member_ready, q + 1)
            if not first:
                pe.wait_ge(entry_ready, q - 1)
            for i in range(NT):
                last = nc.tensor.matmul(pl[0:CAP, s % 2, 0:3], member[:, s % 2, i, :],
                                        m.table[:, bass.ds(q, 1), i, :].rearrange("p o c -> p (o c)"),
                                        start=(i == 0), stop=(i == NT - 1))
            last.then_inc(list_done, 1)

        def read_list(dve, job, first=False, late=True):
            q, s = job.q, job.s
            b = s % 2
            dve.wait_ge(list_done, q + 1)
            nc.vector.tensor_copy(entry[:, b, :], pl[0:CAP, b, 0:3]).then_inc(entry_ready, 1)
            dve.wait_ge(entry_ready, q + 1)
            if not first:
                dve.wait_ge(gathered[b], 16 * job.pair)
            if late:
                dve.wait_ge(added[b], 16 * (job.pair - 1))
            nc.vector.tensor_copy(row_in[:, b:b + 1], entry[:, b, 0:1]).then_inc(rows_ready, 1)
            nc.vector.tensor_copy(weight[:, s:s + 1], entry[:, b, 1:2])
            nc.vector.tensor_scalar(empty[:, b:b + 1], entry[:, b, 2:3], -1.0, 1.0, ALU.mult, ALU.add).then_inc(rows_ready, 1)
            dve.wait_ge(rows_ready, 3 * q + 2)
            nc.vector.scalar_tensor_tensor(row_out[:, s:s + 1], empty[:, b:b + 1], m.spare_row[0:CAP, :], entry[:, b, 0:1],
                                           ALU.mult, ALU.add).then_inc(rows_ready, 1)

        def gather(pool, job, first=False):
            q, s = job.q, job.s
            pool.wait_ge(rows_ready, 3 * q + 3)
            if not first:
                pool.wait_ge(x_turned, 2 * q - 2)
            pool.sem_inc(waits_over)
            nc.gpsimd.indirect_dma_start(x_list[:, s % 2, :], None, m.scr_x1,
                                         bass.IndirectOffsetOnAxis(ap=row_in[:, s % 2:s % 2 + 1], axis=0)).then_inc(gathered[s % 2], 16)

        def turn_list(pe, job, first=False):
            q, s = job.q, job.s
            pe.wait_ge(gathered[s % 2], 16 * job.pair + 16)
            if not first:
                pe.wait_ge(x_ready, 2 * q)
            v = x_list[:, s % 2, :].rearrange("t (p k) -> t k p", k=KD)
            for k in range(KD):
                bank, at = (0, k) if k < KA else (1, k - KA)
                last = nc.tensor.transpose(px[:, bank, at * CAP:(at + 1) * CAP], v[:, k, :], m.ident[0:CAP, 0:CAP])
                if k in (KA - 1, KD - 1):
                    last.then_inc(x_turned, 1)

        def copy_turned(act, job, first=False):
            q, s = job.q, job.s
            for bank, (k0, k1) in enumerate(((0, KA), (KA, KD))):
                act.wait_ge(x_turned, 2 * q + bank + 1)
                if not first and bank == 0:
                    act.wait_ge(gu_done, q - 1)
                nc.scalar.copy(x_list_t[:, s % 2, k0:k1, :],
                               px[:, bank, 0:(k1 - k0) * CAP].rearrange("p (k t) -> p k t", t=CAP)).then_inc(x_ready, 1)

        def gate_up(pe, job, first=False):
            q, s = job.q, job.s
            pe.wait_ge(x_ready, 2 * q + 2)
            if not first:
                pe.wait_ge(hid_ready, q - 1)
            for part, w in enumerate((w_gate, w_up)):
                pe.wait_ge((gate_loaded, up_loaded)[part][s], 16 * job.turn + 16)
                for j in range(2):
                    for k in range(KD):
                        last = nc.tensor.matmul(pgu[:, s % 2, (2 * part + j) * CAP:(2 * part + j + 1) * CAP],
                                                w[s][:, k, j * P:(j + 1) * P], x_list_t[:, s % 2, k, :],
                                                start=(k == 0), stop=(k == KD - 1))
            last.then_inc(gu_done, 1)

        def gate_act(act, job):
            q, s = job.q, job.s
            act.wait_ge(gu_done, q + 1)
            nc.scalar.activation(sig[:, s % 2].rearrange("p j t -> p (j t)"), pgu[:, s % 2, 0:2 * CAP], ACT.Sigmoid).then_inc(sig_ready, 1)

        def gate_mul(dve, job):
            q, s = job.q, job.s
            g = sig[:, s % 2].rearrange("p j t -> p (j t)")
            h = hid[:, s % 2].rearrange("p j t -> p (j t)")
            dve.wait_ge(sig_ready, q + 1)
            nc.vector.tensor_tensor(g, g, pgu[:, s % 2, 0:2 * CAP], ALU.mult).then_inc(silu_ready, 1)
            dve.wait_ge(silu_ready, q + 1)
            nc.vector.tensor_tensor(h, g, pgu[:, s % 2, 2 * CAP:4 * CAP], ALU.mult).then_inc(hid_ready, 1)

        def down(pe, job, first=False):
            q, s = job.q, job.s
            pe.wait_ge(hid_ready, q + 1)
            pe.wait_ge(down_loaded[s], 16 * job.turn + 16)
            for c in range(2):
                if not first:
                    pe.wait_ge((y_act, y_dve)[c], q)
                for j in range(2):
                    last = nc.tensor.matmul(pyl[0:CAP, c, :], hid[:, s % 2, j, :], w_down[s][:, j, c * 512:(c + 1) * 512],
                                            start=(j == 0), stop=(j == 1))
                last.then_inc(y_done, 1)

        def weigh_act(act, job, first=False):
            q, s = job.q, job.s
            act.wait_ge(y_done, 2 * q + 1)
            act.wait_ge(rows_ready, 3 * q + 3)
            if not first:
                act.wait_ge(added[s % 2], 16 * job.pair)
            nc.scalar.activation(y_list[:, s % 2, 0:512], pyl[0:CAP, 0, :], ACT.Copy, scale=weight[:, s:s + 1]).then_inc(y_act, 1)

        def weigh_dve(dve, job, first=False):
            q, s = job.q, job.s
            dve.wait_ge(y_done, 2 * q + 2)
            if not first:
                dve.wait_ge(added[s % 2], 16 * job.pair)
            nc.vector.tensor_scalar(y_list[:, s % 2, 512:1024], pyl[0:CAP, 1, :], weight[:, s:s + 1], None, ALU.mult).then_inc(y_dve, 1)

        def add_rows(pool, job, first=False):
            q, s = job.q, job.s
            pool.wait_ge(y_act, q + 1)
            pool.wait_ge(y_dve, q + 1)
            if not first:
                pool.wait_ge(added[(s + 1) % 2], 16 * job.before)
            pool.sem_inc(waits_over)
            nc.gpsimd.indirect_dma_start(m.scr_f, bass.IndirectOffsetOnAxis(ap=row_out[:, s:s + 1], axis=0), y_list[:, s % 2, :], None,
                                         compute_op=ALU.add).then_inc(added[s % 2], 16)

        LOOPS = E // NB - 1

        with nc.Block() as block:
            @block.sync
            def _(sp):
                for s in range(NB):
                    load(sp, Job(0, s))
                with sp.Fori(1, E // NB) as turn:
                    for s in range(NB):
                        sp.wait_ge(y_done, 2 * (NB * turn + s - NB + 1))
                        load(sp, Job(turn, s))

            @block.tensor
            def _(pe):
                def step(turn, s, list2=True, turn1=True, first_gu=False, first_down=False):
                    gate_up(pe, Job(turn, s), first=first_gu)
                    if list2:
                        make_list(pe, Job(turn, s + 2))
                    if turn1:
                        turn_list(pe, Job(turn, s + 1))
                    down(pe, Job(turn, s), first=first_down)

                for s in range(2):
                    make_list(pe, Job(0, s), first=True)
                turn_list(pe, Job(0, 0), first=True)
                for s in range(NB):
                    step(0, s, first_gu=(s < 2), first_down=(s == 0))
                with pe.Fori(1, LOOPS) as turn:
                    for s in range(NB):
                        step(turn, s)
                for s in range(NB):
                    step(LOOPS, s, list2=(s + 2 < NB), turn1=(s + 1 < NB))

            @block.vector
            def _(dve):
                def step(turn, s, first=False, read2=True, build3=True, late=True):
                    gate_mul(dve, Job(turn, s))
                    if read2:
                        read_list(dve, Job(turn, s + 2), late=late)
                    if build3:
                        build_member(dve, Job(turn, s + 3))
                    weigh_dve(dve, Job(turn, s), first=first)

                for s in range(2):
                    build_member(dve, Job(0, s), first=True)
                for s in range(2):
                    read_list(dve, Job(0, s), first=True, late=False)
                build_member(dve, Job(0, 2))
                for s in range(NB):
                    step(0, s, first=(s < 2), late=(s + 2 >= NB))
                with dve.Fori(1, LOOPS) as turn:
                    for s in range(NB):
                        step(turn, s)
                for s in range(NB):
                    step(LOOPS, s, read2=(s + 2 < NB), build3=(s + 3 < NB))

            @block.scalar
            def _(act):
                def step(turn, s, first=False, copy1=True, first_copy=False):
                    gate_act(act, Job(turn, s))
                    if copy1:
                        copy_turned(act, Job(turn, s + 1), first=first_copy)
                    weigh_act(act, Job(turn, s), first=first)

                copy_turned(act, Job(0, 0), first=True)
                for s in range(NB):
                    step(0, s, first=(s < 2), first_copy=(s == 0))
                with act.Fori(1, LOOPS) as turn:
                    for s in range(NB):
                        step(turn, s)
                for s in range(NB):
                    step(LOOPS, s, copy1=(s + 1 < NB))

            @block.gpsimd
            def _(pool):
                def step(turn, s, first=False, gather2=True):
                    if gather2:
                        gather(pool, Job(turn, s + 2))
                    add_rows(pool, Job(turn, s), first=first)

                for s in range(2):
                    gather(pool, Job(0, s), first=True)
                for s in range(NB):
                    step(0, s, first=(s == 0))
                with pool.Fori(1, LOOPS) as turn:
                    for s in range(NB):
                        step(turn, s)
                for s in range(NB):
                    step(LOOPS, s, gather2=(s + 2 < NB))
                for b in range(2):
                    pool.wait_ge(added[b], 16 * (E // 2))


def overflow(nc, m, ctx_out):
    with ExitStack() as ctx:
        def sb(name, shape, dt=F32):
            return ctx.enter_context(nc.sbuf_tensor(name, shape, dt))

        def ps(name, shape, dt=F32):
            return ctx.enter_context(nc.psum_tensor(name, shape, dt))

        def sem(name):
            return ctx_out.enter_context(nc.semaphore(name))

        w_gu = sb("w_gu", [P, 2, KD, FE])
        w_down = sb("w_down_o", [P, 2, D])
        place = sb("place", [P, NT])
        member = sb("member_o", [P, NT, CAP])
        entry = sb("entry_o", [CAP, 3])
        row_in = sb("row_in_o", [CAP, 1], U32)
        row_out = sb("row_out_o", [CAP, 1], U32)
        empty = sb("empty_o", [CAP, 1])
        x_list = sb("x_list_o", [CAP, D])
        x_list_t = sb("x_list_t_o", [P, KD, CAP])
        sig = sb("sig_o", [P, 2 * CAP])
        hid = sb("hid_o", [P, 2, CAP])
        y_list = sb("y_list_o", [CAP, D])
        pl = ps("pl_o", [P, 512])
        px = ps("px_o", [P, 2, 512])
        pgu = ps("pgu_o", [P, 512])
        pyl = ps("pyl_o", [P, 2, 512])
        KA = 512 // CAP if 512 // CAP < KD else KD // 2
        weights_loaded = sem("o_weights_loaded")
        member_ready = sem("o_member_ready")
        list_done = sem("o_list_done")
        rows_ready = sem("o_rows_ready")
        gathered = sem("o_gathered")
        x_turned = sem("o_x_turned")
        x_ready = sem("o_x_ready")
        gu_done = sem("o_gu_done")
        sig_ready = sem("o_sig_ready")
        hid_ready = sem("o_hid_ready")
        y_done = sem("o_y_done")
        y_ready = sem("o_y_ready")
        added = sem("o_added")
        waits_over = sem("o_waits_over")

        def each_job(eng, body, expert=True):
            n = eng.value_load(m.job_table[0:1, 0:1], min_val=0, max_val=m.EXTRA)
            with eng.If(n > 0):
                with eng.Fori(0, m.EXTRA) as k:
                    with eng.If(k < n):
                        ex = eng.value_load(m.job_table[0:1, bass.ds(k + 1, 1)], min_val=0, max_val=E - 1) if expert else None
                        body(k, ex)

        with nc.Block() as block:
            @block.sync
            def _(sp):
                def body(k, ex):
                    sp.wait_ge(y_done, k)
                    pick = lambda w: w[bass.ds(ex, 1)].rearrange("o p n -> p (o n)")
                    sp.dma_start(w_gu[:, 0].rearrange("p k f -> p (k f)"), pick(m.exp_gate)).then_inc(weights_loaded, 16)
                    sp.dma_start(w_gu[:, 1].rearrange("p k f -> p (k f)"), pick(m.exp_up)).then_inc(weights_loaded, 16)
                    sp.dma_start(w_down[:], m.exp_down[bass.ds(ex, 1)].rearrange("o p j d -> p (o j) d")).then_inc(weights_loaded, 16)
                each_job(sp, body)

            @block.vector
            def _(dve):
                def body(k, ex):
                    dve.wait_ge(added, 16 * k)
                    nc.vector.tensor_scalar(place[:], m.position[:, bass.ds(ex, 1), :].rearrange("p o i -> p (o i)"),
                                            m.job_base[:, bass.ds(k, 1)], None, ALU.subtract).then_inc(member_ready, 1)
                    dve.wait_ge(member_ready, 2 * k + 1)
                    nc.vector.tensor_tensor(member[:], m.slot_index[:].unsqueeze(1).broadcast_to([P, NT, CAP]),
                                            place[:].unsqueeze(2).broadcast_to([P, NT, CAP]), ALU.is_equal).then_inc(member_ready, 1)
                    dve.wait_ge(list_done, k + 1)
                    nc.vector.tensor_copy(entry[:], pl[0:CAP, 0:3]).then_inc(rows_ready, 1)
                    dve.wait_ge(rows_ready, 4 * k + 1)
                    nc.vector.tensor_copy(row_in[:], entry[:, 0:1]).then_inc(rows_ready, 1)
                    nc.vector.tensor_scalar(empty[:], entry[:, 2:3], -1.0, 1.0, ALU.mult, ALU.add).then_inc(rows_ready, 1)
                    dve.wait_ge(rows_ready, 4 * k + 3)
                    nc.vector.scalar_tensor_tensor(row_out[:], empty[:], m.spare_row[0:CAP, :], entry[:, 0:1],
                                                   ALU.mult, ALU.add).then_inc(rows_ready, 1)
                    dve.wait_ge(sig_ready, k + 1)
                    nc.vector.tensor_tensor(sig[:], sig[:], pgu[:, 0:2 * CAP], ALU.mult).then_inc(hid_ready, 1)
                    dve.wait_ge(hid_ready, 2 * k + 1)
                    nc.vector.tensor_tensor(hid[:].rearrange("p j t -> p (j t)"), sig[:], pgu[:, 2 * CAP:4 * CAP], ALU.mult).then_inc(hid_ready, 1)
                    dve.wait_ge(y_done, k + 1)
                    for c in range(2):
                        last = nc.vector.tensor_scalar(y_list[:, c * 512:(c + 1) * 512], pyl[0:CAP, c, :], entry[:, 1:2], None, ALU.mult)
                    last.then_inc(y_ready, 1)
                each_job(dve, body)

            @block.tensor
            def _(pe):
                def body(k, ex):
                    pe.wait_ge(member_ready, 2 * k + 2)
                    for i in range(NT):
                        last = nc.tensor.matmul(pl[0:CAP, 0:3], member[:, i, :], m.table[:, bass.ds(ex, 1), i, :].rearrange("p o c -> p (o c)"),
                                                start=(i == 0), stop=(i == NT - 1))
                    last.then_inc(list_done, 1)
                    pe.wait_ge(gathered, 16 * k + 16)
                    v = x_list[:].rearrange("t (p k) -> t k p", k=KD)
                    for kk in range(KD):
                        bank, at = (0, kk) if kk < KA else (1, kk - KA)
                        last = nc.tensor.transpose(px[:, bank, at * CAP:(at + 1) * CAP], v[:, kk, :], m.ident[0:CAP, 0:CAP])
                    last.then_inc(x_turned, 1)
                    pe.wait_ge(x_ready, k + 1)
                    pe.wait_ge(weights_loaded, 48 * k + 48)
                    for part in range(2):
                        for j in range(2):
                            for kk in range(KD):
                                last = nc.tensor.matmul(pgu[:, (2 * part + j) * CAP:(2 * part + j + 1) * CAP],
                                                        w_gu[:, part, kk, j * P:(j + 1) * P], x_list_t[:, kk, :],
                                                        start=(kk == 0), stop=(kk == KD - 1))
                    last.then_inc(gu_done, 1)
                    pe.wait_ge(hid_ready, 2 * k + 2)
                    for c in range(2):
                        for j in range(2):
                            last = nc.tensor.matmul(pyl[0:CAP, c, :], hid[:, j, :], w_down[:, j, c * 512:(c + 1) * 512],
                                                    start=(j == 0), stop=(j == 1))
                    last.then_inc(y_done, 1)
                each_job(pe, body)

            @block.scalar
            def _(act):
                def body(k, ex):
                    act.wait_ge(x_turned, k + 1)
                    for bank, (k0, k1) in enumerate(((0, KA), (KA, KD))):
                        last = nc.scalar.copy(x_list_t[:, k0:k1, :], px[:, bank, 0:(k1 - k0) * CAP].rearrange("p (k t) -> p k t", t=CAP))
                    last.then_inc(x_ready, 1)
                    act.wait_ge(gu_done, k + 1)
                    nc.scalar.activation(sig[:], pgu[:, 0:2 * CAP], ACT.Sigmoid).then_inc(sig_ready, 1)
                each_job(act, body, expert=False)

            @block.gpsimd
            def _(pool):
                def body(k, ex):
                    pool.wait_ge(rows_ready, 4 * k + 4)
                    pool.sem_inc(waits_over)
                    nc.gpsimd.indirect_dma_start(x_list[:], None, m.scr_x1,
                                                 bass.IndirectOffsetOnAxis(ap=row_in[:], axis=0)).then_inc(gathered, 16)
                    pool.wait_ge(y_ready, k + 1)
                    pool.sem_inc(waits_over)
                    nc.gpsimd.indirect_dma_start(m.scr_f, bass.IndirectOffsetOnAxis(ap=row_out[:], axis=0), y_list[:], None,
                                                 compute_op=ALU.add).then_inc(added, 16)
                    pool.wait_ge(added, 16 * k + 16)
                each_job(pool, body, expert=False)


def finish(nc, m, ctx_out):
    with ExitStack() as ctx:
        def sb(name, shape, dt=F32):
            return ctx.enter_context(nc.sbuf_tensor(name, shape, dt))

        def sem(name):
            return ctx_out.enter_context(nc.semaphore(name))

        f = sb("f", [P, NT, D])
        ln_g = sb("ln2_g", [P, D])
        ln_b = sb("ln2_b", [P, D])
        stats = sb("stats7", [P, NT, 2, 6])
        aggr = sb("aggr7", [P, NT, 4])
        f_loaded = [sem(f"f_loaded{i}") for i in range(NT)]
        ln_loaded = sem("ln2_loaded")
        stats_ready = sem("stats_ready")
        var_ready = sem("var7_ready")
        rooted = sem("ln2_rooted")
        y_ready = sem("y_ready")
        y_stored = sem("out_stored")
        with nc.Block() as block:
            @block.sync
            def _(sp):
                for i, (t0, n) in enumerate(TOK_TILES):
                    sp.dma_start(f[0:n, i, :], m.scr_f[t0:t0 + n, :]).then_inc(f_loaded[i], 16)
                sp.dma_start(ln_g[:], m.vec["ln2_g"].broadcast_to([P, D])).then_inc(ln_loaded, 16)
                sp.dma_start(ln_b[:], m.vec["ln2_b"].broadcast_to([P, D])).then_inc(ln_loaded, 16)
                for i, (t0, n) in enumerate(TOK_TILES):
                    sp.wait_ge(y_ready, i + 1)
                    dst = m.y_prompt[t0:t0 + n, :] if i < TM else m.y_sample
                    sp.dma_start(dst, f[0:n, i, :]).then_inc(y_stored, 16)
                sp.wait_ge(y_stored, 16 * NT)

            @block.scalar
            def _(act):
                for i, (_, n) in enumerate(TOK_TILES):
                    act.wait_ge(var_ready, i + 1)
                    nc.scalar.activation(aggr[0:n, i, 2:3], aggr[0:n, i, 1:2], ACT.Sqrt, bias=m.eps_ln[0:n, :]).then_inc(rooted, 1)

            @block.vector
            def _(dve):
                ch = Chain(dve, m.vector_step, m.vector_count)
                dve.wait_ge(ln_loaded, 32)
                for i, (_, n) in enumerate(TOK_TILES):
                    x = f[0:n, i, :]
                    dve.wait_ge(f_loaded[i], 16)
                    for c in range(2):
                        last = nc.vector.bn_stats(stats[0:n, i, c, :], x[:, c * 512:(c + 1) * 512])
                    last.then_inc(stats_ready, 1)
                    dve.wait_ge(stats_ready, i + 1)
                    nc.vector.bn_aggr(aggr[0:n, i, 0:2], stats[0:n, i, :, :]).then_inc(var_ready, 1)
                    dve.wait_ge(var_ready, i + 1)
                    dve.wait_ge(rooted, i + 1)
                    ch.link(nc.vector.reciprocal(aggr[0:n, i, 3:4], aggr[0:n, i, 2:3]))
                    ch.link(nc.vector.tensor_scalar(x, x, aggr[0:n, i, 0:1], aggr[0:n, i, 3:4], ALU.subtract, ALU.mult))
                    ch.link(nc.vector.tensor_tensor(x, x, ln_g[0:n, :], ALU.mult))
                    nc.vector.tensor_tensor(x, x, ln_b[0:n, :], ALU.add).then_inc(y_ready, 1)


def constants(nc, m, ready):
    def build(pool):
        ch = Chain(pool, m.pool_step, m.pool_count)
        g = nc.gpsimd
        g.memset(m.eps_ln[:], LN_EPS)
        g.memset(m.eps_gn[:], GN_EPS)
        g.memset(m.ones[:], 1.0)
        g.memset(m.ones_mean[:], 1.0 / DC)
        ch.link(g.memset(m.ident[:], 0.0))
        g.affine_select(out=m.ident[:], in_=m.ident[:], compare_op=ALU.not_equal, fill=1.0, base=0,
                        pattern=[[-1, P]], channel_multiplier=1).then_inc(ready, 1)
        g.memset(m.head_ones[:], 1.0)
        g.memset(m.below[:], 1.0)
        g.memset(m.is_token[:], 1.0)
        g.memset(m.chunk_keep[:], 1.0)
        ch.link(g.memset(m.inside_mask[:], 1.0))
        heads = m.head_ones[:].rearrange("p (h c) -> p h c", c=N)
        ch.link(g.affine_select(out=heads, in_=heads, compare_op=ALU.is_ge, fill=0.0, base=0, pattern=[[-N, 2], [0, N]], channel_multiplier=1))
        ch.link(g.affine_select(out=heads, in_=heads, compare_op=ALU.is_ge, fill=0.0, base=N - 1, pattern=[[N, 2], [0, N]], channel_multiplier=-1))
        for c in range(CM):
            r = m.below[L * c:L * (c + 1), :]
            ch.link(g.affine_select(out=r, in_=r, compare_op=ALU.is_gt, fill=0.0, base=0, pattern=[[-1, L]], channel_multiplier=1))
        for part in range(3):
            v = m.inside_mask[:, part, :].rearrange("p (c t) -> p c t", t=L)
            ch.link(g.affine_select(out=v, in_=v, compare_op=ALU.is_ge, fill=0.0, base=0, pattern=[[-L, CM], [0, L]], channel_multiplier=1))
            ch.link(g.affine_select(out=v, in_=v, compare_op=ALU.is_ge, fill=0.0, base=L - 1, pattern=[[L, CM], [0, L]], channel_multiplier=-1))
            ch.link(g.affine_select(out=m.inside_mask[:, part, :], in_=m.inside_mask[:, part, :],
                                    compare_op=ALU.is_gt if part == 0 else ALU.is_ge, fill=0.0, base=0,
                                    pattern=[[1, P]], channel_multiplier=-1))
        g.memset(m.chunk_keep[:, 0:T:L], 0.0)
        g.affine_select(out=m.is_token[:, TM:], in_=m.is_token[:, TM:], compare_op=ALU.is_ge, fill=0.0, base=B - 1,
                        pattern=[[0, 1]], channel_multiplier=-1)
        wide = dict(allow_small_or_imprecise_dtypes=True)
        g.iota(m.token_id[:], pattern=[[P, NT]], base=0, channel_multiplier=1, **wide)
        g.iota(m.slot_index[:], pattern=[[1, CAP]], base=0, channel_multiplier=0, **wide)
        g.iota(m.job_index[:], pattern=[[1, m.EXTRA]], base=0, channel_multiplier=0, **wide)
        g.iota(m.spare_row[:], pattern=[[0, 1]], base=TT, channel_multiplier=1, **wide)
    return build


class Shared:
    pass


def kernel_program(nc, a, outs):
    m = Shared()
    flat = "l k n -> (l k) n"
    m.x_prompt = a["x_prompt"].rearrange("b t d -> (b t) d")
    m.x_sample = a["x_sample"].rearrange("b t d -> (b t) d")
    m.state_conv = a["state_conv"].rearrange("l b w c -> (l b) w c")
    m.state_shift = a["state_shift"].rearrange("l b c -> (l b) c")
    m.state_wkv = a["state_wkv"].rearrange("l b h (two v) k -> (l b h two) (v k)", two=2)
    m.w_in = a["w_in"].rearrange(flat)
    m.conv_w = a["conv_w"].rearrange("l w c -> (l w) c")
    m.mu_shift = a["mu_shift"]
    m.vec = {n: a[n] if n != "r_k" else a[n].rearrange("l h n -> l (h n)")
             for n in PARAMS + ["gn_g", "gn_b", "ln1_g", "ln1_b", "ln2_g", "ln2_b", "router_bias"]}
    m.w_up, m.a_up, m.g_up = (a[n].rearrange(flat) for n in ("w_up", "a_up", "g_up"))
    m.w_out, m.router_w = (a[n].rearrange(flat) for n in ("w_out", "router_w"))
    m.sh_gate, m.sh_up, m.sh_down = (a[n].rearrange(flat) for n in ("sh_gate", "sh_up", "sh_down"))
    m.exp_gate = a["exp_gate"].rearrange("l e (p k) f -> (l e) p (k f)", p=P)
    m.exp_up = a["exp_up"].rearrange("l e (p k) f -> (l e) p (k f)", p=P)
    m.exp_down = a["exp_down"].rearrange("l e (j p) d -> (l e) p j d", p=P)
    m.y_prompt = outs[0].rearrange("b t d -> (b t) d")
    m.y_sample = outs[1].rearrange("b t d -> (b t) d")
    m.new_conv_p = outs[2].rearrange("l b w c -> (l b w) c")
    m.new_shift_p = outs[3].rearrange("l b c -> (l b) c")
    m.new_wkv_p = outs[4].rearrange("l b h v k -> (l b h) v k")
    m.new_conv_s = outs[5].rearrange("l b w c -> (l b) w c")
    m.new_shift_s = outs[6].rearrange("l b c -> (l b) c")
    m.new_wkv_s = outs[7].rearrange("l b h (two v) k -> (l b h two) (v k)", two=2)
    m.scr_lower = nc.dram_tensor("scr_lower", (P, L * L), F32).ap()
    m.scr_solved = nc.dram_tensor("scr_solved", (P, L * L), F32).ap()
    m.scr_sample = nc.dram_tensor("scr_sample", (6, B, DC), F32).ap()
    m.scr_y = nc.dram_tensor("scr_y", (B, DC), F32).ap()
    m.scr_x1 = nc.dram_tensor("scr_x1", (TT, D), F32).ap()
    m.scr_f = nc.dram_tensor("scr_f", (TT + CAP, D), F32).ap()
    m.MAX_JOBS = -(-TT // CAP)
    m.EXTRA = TT * K // CAP
    with ExitStack() as top:
        def sb(name, shape, dt=F32):
            return top.enter_context(nc.sbuf_tensor(name, shape, dt))

        m.vector_step = top.enter_context(nc.semaphore("vector_step"))
        m.vector_count = [0]
        m.pool_step = top.enter_context(nc.semaphore("pool_step"))
        m.pool_count = [0]
        first_sems = ExitStack()
        m.spent = []
        m.ident = sb("ident", [P, P])
        m.ones = sb("ones", [P, P])
        m.eps_ln = sb("eps_ln", [P, 1])
        m.eps_gn = sb("eps_gn", [P, 1])
        m.is_token = sb("is_token", [P, NT])
        m.token_id = sb("token_id", [P, NT])
        m.slot_index = sb("slot_index", [P, CAP])
        m.job_index = sb("job_index", [P, m.EXTRA])
        m.job_expert = sb("job_expert", [P, m.EXTRA])
        m.job_base = sb("job_base", [P, m.EXTRA])
        m.job_table = sb("job_table", [1, m.EXTRA + 1], U32)
        m.spare_row = sb("spare_row", [P, 1])
        m.position = sb("position", [P, E, NT])
        m.table = sb("table", [P, E, NT, 3])
        with ExitStack() as late:
            def sb2(name, shape, dt=F32):
                return late.enter_context(nc.sbuf_tensor(name, shape, dt))

            m.conv = sb2("conv", [P, CT, TT])
            m.o_t = sb2("o_t", [P, CT, TT])
            with ExitStack() as mid:
                def sb3(name, shape, dt=F32):
                    return mid.enter_context(nc.sbuf_tensor(name, shape, dt))

                m.ones_mean = sb3("ones_mean", [P, P])
                m.head_ones = sb3("head_ones", [P, P])
                m.below = sb3("below", [P, L])
                m.inside_mask = sb3("inside_mask", [P, 3, P])
                m.chunk_keep = sb3("chunk_keep", [P, T])
                m.params = sb3("params", [P, CT, NPAR])
                m.zs = sb3("zs", [P, NSH, TT])
                project(nc, m, first_sems)
                m.v_rows = sb3("v_rows", [P, NT, DC])
                m.gate = sb3("gate", [P, NT, DC])
                m.bonus = sb3("bonus", [P, NT, H])
                m.a_rows = sb3("a_rows", [P, TM, DC])
                m.b_rows = sb3("b_rows", [P, TM, DC])
                m.k_rows = sb3("k_rows", [P, TM, DC])
                m.read_decayed = sb3("read_decayed", [P, CT, TM, 2, P])
                m.b_grown = sb3("b_grown", [P, CT, T])
                m.k_grown = sb3("k_grown", [P, CT, T])
                m.chunk_decay = sb3("chunk_decay", [P, CT, NCH])
                m.sample_vec = sb3("sample_vec", [P, 6, CT, B])
                m.y_sample_rows = sb3("y_sample_rows", [B, DC])
                time_prepare(nc, m, first_sems)
                m.inverse = sb3("inverse", [P, TM * H, P])
                solve_chunks(nc, m, first_sems)
                recur(nc, m, top)
            first_sems.close()
            mix(nc, m, top)
        m.w_gate, m.w_up, m.w_down = [], [], []
        experts(nc, m, top)
        overflow(nc, m, top)
        finish(nc, m, top)


_INS = ["x_prompt", "x_sample", "state_conv", "state_shift", "state_wkv", "w_in", "mu_shift", "conv_w", "conv_b",
        "conv_ln_g", "conv_ln_b", "w0", "w_up", "a0", "a_up", "g_up", "k_k", "k_a", "r_k", "gn_g", "gn_b", "w_out",
        "ln1_g", "ln1_b", "router_w", "router_bias", "exp_gate", "exp_up", "exp_down", "sh_gate", "sh_up", "sh_down",
        "ln2_g", "ln2_b"]
_OUTS = [(1, T, D), (B, 1, D), (1, 1, CW - 1, DC), (1, 1, DS), (1, 1, H, N, N), (1, B, CW - 1, DC), (1, B, DS),
         (1, B, H, N, N)]


def kernel(**inputs):
    import numpy as _np
    import concourse.bacc as _bacc
    from concourse import mybir as _mybir
    from concourse.bass_utils import run_bass_kernel_spmd as _run

    nc = _bacc.Bacc("TRN2", target_bir_lowering=False, num_devices=1)
    arrays, aps = {}, {}
    for name in _INS:
        x = _np.ascontiguousarray(inputs[name])
        arrays[f"in_{name}_dram"] = x
        aps[name] = nc.dram_tensor(f"in_{name}_dram", x.shape, _mybir.dt.from_np(x.dtype), kind="ExternalInput").ap()
    outs = [nc.dram_tensor(f"out_{i}_dram", shape, _mybir.dt.float32, kind="ExternalOutput").ap()
            for i, shape in enumerate(_OUTS)]
    kernel_program(nc, aps, outs)
    r = _run(nc, [arrays], core_ids=[0])
    return tuple(r.results[0][f"out_{i}_dram"] for i in range(len(_OUTS)))
```

```python
from contextlib import ExitStack

import concourse.bass as bass
from concourse import mybir

F32 = mybir.dt.float32
U32 = mybir.dt.uint32
BF16 = mybir.dt.bfloat16
ALU = mybir.AluOpType
ACT = mybir.ActivationFunctionType
AX = mybir.AxisListType.X

P = 128
D = 1024
KD = D // P
T = 512
B = 8
TT = T + B
TM = T // P
DC = 512
CT = DC // P
CW = 31
H = 8
N = 64
LW = 64
LA = 64
LG = 160
DS = 3 * 512 + LW + LA + LG
L = 32
NCH = T // L
CM = P // L
E = 64
FE = 256
K = 8
G = 8
KG = 4
CAP = 96
NB = 4
EXPERT_FLOATS = 3 * KD * FE
ALPHA = 2.0 ** 0.25
LN_EPS = 1e-5
GN_EPS = 64e-5
ROUTED_SCALE = 2.5
DECAY_SCALE = 0.6065306597126334
TOK_TILES = [(i * P, P) for i in range(TM)] + [(T, B)]
NT = len(TOK_TILES)

CONV_TILES = [(kind, i, off + i * P, P) for i in range(CT) for kind, off in (("glu_a", 0), ("glu_gate", DC))]
_RW = 2 * DC
SHIFT_TILES = [("lora", 0, _RW + 1536, P), ("gate0", 0, _RW + 1664, P)] \
    + [(kind, i, _RW + j * 512 + i * P, P) for i in range(CT) for j, kind in enumerate("rkv")] \
    + [("gate1", 0, _RW + 1792, 32)]
COL_TILES = CONV_TILES + SHIFT_TILES
NCOL = len(COL_TILES)
NCONV = len(CONV_TILES)
NSH = len(SHIFT_TILES)
LORA, GATE0, GATE1 = 0, 1, NSH - 1


def shift_index(kind, i):
    return 2 + 3 * i + "rkv".index(kind)


PARAMS = ["conv_b", "conv_ln_g", "conv_ln_b", "w0", "a0", "k_k", "k_a", "r_k"]
NPAR = CW + len(PARAMS)


def par(name):
    return CW + PARAMS.index(name)


class Chain:

    def __init__(self, eng, sem, state):
        self.eng, self.sem, self.state = eng, sem, state

    def link(self, ins):
        self.state[0] += 1
        ins.then_inc(self.sem, 1)
        self.eng.wait_ge(self.sem, self.state[0])


def cols(i):
    t0, n = TOK_TILES[i]
    return slice(t0, t0 + n)


def place(m, at, *shape):
    size = 1
    for n in shape:
        size *= n
    assert at + size <= NB * EXPERT_FLOATS
    names = "abcde"[:len(shape)]
    flat = m.w_exp[:, at:at + size]
    return flat.rearrange(f"p ({' '.join(names)}) -> p {' '.join(names)}", **dict(zip(names, shape)))


def project(nc, m, ctx_out):
    WB = 6
    ZB = 3
    with ExitStack() as ctx:
        def sb(name, shape, dt=F32):
            return ctx.enter_context(nc.sbuf_tensor(name, shape, dt))

        def ps(name, shape, dt=F32):
            return ctx.enter_context(nc.psum_tensor(name, shape, dt))

        def sem(name):
            m.spent.append(ctx_out.enter_context(nc.semaphore(name)))
            return m.spent[-1]

        x_rows = sb("x_rows", [P, NT, D])
        x_t = place(m, 0, KD, TT)
        w_col = place(m, KD * TT, WB, KD, P)
        staged = sb("staged", [P, ZB, T + 1])
        glu_stage = sb("glu_stage", [P, 2, T])
        u_pad = sb("u_pad", [P, CT, CW - 1 + T])
        z_last = sb("z_last", [P, NSH, 1 + B])
        z_diff = sb("z_diff", [P, 2, T])
        z_sample = sb("z_sample", [P, NCOL, B])
        gate_sample = sb("gate_sample", [P, CT, B])
        u_sample = sb("u_sample", [P, CT, B])
        zd_sample = sb("zd_sample", [P, NSH, B])
        par_rows = sb("par_rows", [NPAR, DC])
        shift_rows = sb("shift_rows", [B + 1, DS])
        conv_rows = sb("conv_rows", [120, 2, DC])
        shift_t = sb("shift_t", [P, NSH, B + 1])
        conv_state = sb("conv_state", [P, CT, B * (CW - 1)])
        conv_prod = sb("conv_prod", [P, CT, B * (CW - 1)])
        conv_sum = sb("conv_sum", [P, CT, B])
        tail_rows = sb("tail_rows", [38, DC])
        tail_in = sb("tail_in", [P, CT, 38])
        shift_out = sb("shift_out", [1 + B, DS])
        pt = ps("pt", [P, 2, 512])
        pz = ps("pz", [P, 3, 512])
        pzs = ps("pzs", [P, NCOL, B])
        pm = ps("pm", [P, 2, 512])

        x_loaded = sem("x_loaded")
        small_loaded = sem("small_loaded")
        w_loaded = [sem(f"w_loaded{i}") for i in range(WB)]
        consts_ready = sem("consts_ready")
        xt_turned = sem("xt_turned")
        xt_ready = sem("xt_ready")
        small_turned = sem("small_turned")
        small_ready = sem("small_ready")
        tile_projected = sem("tile_projected")
        tile_taken = sem("tile_taken")
        staged_used = sem("staged_used")
        glu_used = sem("glu_used")
        sample_taken = sem("sample_taken")
        sample_gated = sem("sample_gated")
        tails_ready = sem("tails_ready")
        tails_turned = sem("tails_turned")
        tails_copied = sem("tails_copied")
        state_stored = sem("state_stored")
        zeros_ready = sem("zeros_ready")
        XT_GROUPS = 2 * TM + 1
        SMALL = 4

        with nc.Block() as block:
            @block.sync
            def _(sp):
                for i, (t0, n) in enumerate(TOK_TILES):
                    src = m.x_prompt[t0:t0 + n, :] if i < TM else m.x_sample
                    sp.dma_start(x_rows[0:n, i, :], src).then_inc(x_loaded, 16)
                for c, (_, _, c0, w) in enumerate(COL_TILES):
                    if c >= WB:
                        sp.wait_ge(tile_projected, c - WB + 1)
                    sp.dma_start(w_col[:, c % WB, :, 0:w],
                                 m.w_in[:, c0:c0 + w].rearrange("(k p) n -> p k n", p=P)).then_inc(w_loaded[c % WB], 16)
                sp.wait_ge(tails_copied, 2)
                sp.dma_start(m.new_conv_p, tail_rows[0:30, :]).then_inc(state_stored, 16)
                sp.dma_start(m.new_conv_s[:, CW - 2, :], tail_rows[30:38, :]).then_inc(state_stored, 16)
                sp.wait_ge(tails_copied, 6)
                sp.dma_start(m.new_shift_p, shift_out[0:1, :]).then_inc(state_stored, 16)
                sp.dma_start(m.new_shift_s, shift_out[1:1 + B, :]).then_inc(state_stored, 16)
                sp.wait_ge(state_stored, 16 * 5)

            @block.scalar
            def _(act):
                act.dma_start(par_rows[0:CW, :], m.conv_w).then_inc(small_loaded, 16)
                for name in PARAMS:
                    act.dma_start(par_rows[par(name):par(name) + 1, :], m.vec[name]).then_inc(small_loaded, 16)
                act.dma_start(shift_rows[0:B, :], m.state_shift).then_inc(small_loaded, 16)
                act.dma_start(shift_rows[B:B + 1, :], m.mu_shift).then_inc(small_loaded, 16)
                for j in range(2):
                    act.dma_start(conv_rows[:, j, :],
                                  m.state_conv[4 * j:4 * j + 4].rearrange("b w c -> (b w) c")).then_inc(small_loaded, 16)
                act.dma_start(m.new_conv_s[:, 0:CW - 2, :], m.state_conv[:, 1:CW - 1, :]).then_inc(state_stored, 16)
                for g in range(XT_GROUPS):
                    act.wait_ge(xt_turned, g + 1)
                    if g < 2 * TM:
                        i, k0 = g // 2, 4 * (g % 2)
                        nc.scalar.copy(x_t[:, k0:k0 + 4, cols(i)],
                                       pt[:, g % 2, :].rearrange("p (k t) -> p k t", k=4)).then_inc(xt_ready, 1)
                    else:
                        nc.scalar.copy(x_t[:, :, cols(TM)],
                                       pt[:, g % 2, 0:KD * B].rearrange("p (k t) -> p k t", k=KD)).then_inc(xt_ready, 1)
                act.wait_ge(zeros_ready, 3)
                for c, (kind, i, _, w) in enumerate(COL_TILES):
                    act.wait_ge(tile_projected, c + 1)
                    z = pz[0:w, c % 3, :]
                    if kind == "glu_a":
                        if i >= 1:
                            act.wait_ge(glu_used, i)
                        nc.scalar.copy(glu_stage[:, 0, :], z).then_inc(tile_taken, 1)
                    elif kind == "glu_gate":
                        nc.scalar.activation(glu_stage[:, 1, :], z, ACT.Sigmoid).then_inc(tile_taken, 1)
                    else:
                        s = c - NCONV
                        if s >= ZB:
                            act.wait_ge(staged_used, s - ZB + 1)
                        nc.scalar.copy(z_last[0:w, s, 0:1], z[:, T - 1:T])
                        nc.scalar.copy(staged[0:w, s % ZB, 1:T + 1], z).then_inc(tile_taken, 1)
                nc.scalar.copy(z_sample[:, 0:NCOL - 1, :], pzs[:, 0:NCOL - 1, :])
                nc.scalar.copy(z_sample[0:32, NCOL - 1, :], pzs[0:32, NCOL - 1, :]).then_inc(sample_taken, 1)
                nc.scalar.activation(gate_sample[:], pzs[:, 1:NCONV:2, :], ACT.Sigmoid).then_inc(sample_gated, 1)

            @block.tensor
            def _(pe):
                pe.wait_ge(consts_ready, 1)
                for g in range(XT_GROUPS):
                    i = g // 2
                    pe.wait_ge(x_loaded, 16 * NT)
                    if g >= 2:
                        pe.wait_ge(xt_ready, g - 1)
                    if g < 2 * TM:
                        for k in range(4):
                            d0 = (4 * (g % 2) + k) * P
                            last = nc.tensor.transpose(pt[:, g % 2, k * P:(k + 1) * P], x_rows[:, i, d0:d0 + P], m.ident[:])
                    else:
                        for k in range(KD):
                            last = nc.tensor.transpose(pt[:, g % 2, k * B:(k + 1) * B],
                                                       x_rows[0:B, TM, k * P:(k + 1) * P], m.ident[0:B, 0:B])
                    last.then_inc(xt_turned, 1)
                pe.wait_ge(small_loaded, 16 * (1 + len(PARAMS) + 4))
                for i in range(CT):
                    last = nc.tensor.transpose(pm[:, 0, i * NPAR:(i + 1) * NPAR], par_rows[:, i * P:(i + 1) * P],
                                               m.ident[0:NPAR, 0:NPAR])
                last.then_inc(small_turned, 1)
                for s, (_, _, c0, w) in enumerate(SHIFT_TILES):
                    last = nc.tensor.transpose(pm[0:w, 1, s * (B + 1):(s + 1) * (B + 1)],
                                               shift_rows[:, c0 - _RW:c0 - _RW + w], m.ident[0:B + 1, 0:B + 1])
                last.then_inc(small_turned, 1)
                for h in range(2):
                    pe.wait_ge(small_ready, h + 1)
                    for i in range(2):
                        for j in range(2):
                            last = nc.tensor.transpose(pm[:, h, (2 * i + j) * 120:(2 * i + j + 1) * 120],
                                                       conv_rows[:, j, (2 * h + i) * P:(2 * h + i + 1) * P],
                                                       m.ident[0:120, 0:120])
                    last.then_inc(small_turned, 1)
                pe.wait_ge(xt_ready, XT_GROUPS)
                for c, (_, _, _, w) in enumerate(COL_TILES):
                    pe.wait_ge(w_loaded[c % WB], 16 * (c // WB + 1))
                    if c >= 3:
                        pe.wait_ge(tile_taken, c - 2)
                    for k in range(KD):
                        nc.tensor.matmul(pz[0:w, c % 3, :], w_col[:, c % WB, k, 0:w], x_t[:, k, 0:T],
                                         start=(k == 0), stop=(k == KD - 1))
                        last = nc.tensor.matmul(pzs[0:w, c, :], w_col[:, c % WB, k, 0:w], x_t[:, k, T:TT],
                                                start=(k == 0), stop=(k == KD - 1))
                    last.then_inc(tile_projected, 1)
                pe.wait_ge(tails_ready, 1)
                for i in range(CT):
                    last = nc.tensor.transpose(pm[0:38, 0, i * P:(i + 1) * P], tail_in[:, i, :], m.ident[:])
                last.then_inc(tails_turned, 1)
                pe.wait_ge(tails_ready, 2)
                for q in range(4):
                    if q >= 1:
                        pe.wait_ge(tails_copied, q + 1)
                    for s in range(4 * q, min(4 * q + 4, NSH)):
                        w = SHIFT_TILES[s][3]
                        last = nc.tensor.transpose(pm[0:1 + B, 1 - q % 2, (s % 4) * P:(s % 4) * P + w],
                                                   z_last[0:w, s, :], m.ident[0:w, 0:w])
                    last.then_inc(tails_turned, 1)

            @block.vector
            def _(dve):
                ch = Chain(dve, m.vector_step, m.vector_count)
                nc.vector.memset(u_pad[:, :, 0:CW - 1], 0.0).then_inc(zeros_ready, 1)
                for b in range(ZB):
                    last = nc.vector.memset(staged[:, b, 0:1], 0.0)
                last.then_inc(zeros_ready, 1)
                nc.vector.memset(shift_t[:], 0.0).then_inc(zeros_ready, 1)
                dve.wait_ge(zeros_ready, 3)
                dve.wait_ge(small_turned, 1)
                ch.link(nc.vector.tensor_copy(m.params[:], pm[:, 0, 0:CT * NPAR].rearrange("p (i n) -> p i n", i=CT)))
                dve.wait_ge(small_turned, 2)
                nc.vector.tensor_copy(shift_t[:, 0:NSH - 1, :], pm[:, 1, 0:(NSH - 1) * (B + 1)].rearrange("p (i n) -> p i n", n=B + 1))
                nc.vector.tensor_copy(shift_t[0:32, NSH - 1, :], pm[0:32, 1, (NSH - 1) * (B + 1):NSH * (B + 1)]).then_inc(small_ready, 2)
                for h in range(2):
                    dve.wait_ge(small_turned, 3 + h)
                    nc.vector.tensor_copy(conv_state[:, 2 * h:2 * h + 2, :],
                                          pm[:, h, 0:480].rearrange("p (i n) -> p i n", i=2)).then_inc(small_ready, 1)
                dve.wait_ge(small_ready, 4)
                for i in range(CT):
                    dve.wait_ge(tile_taken, 2 * i + 2)
                    nc.vector.tensor_tensor(u_pad[:, i, CW - 1:CW - 1 + T], glu_stage[:, 0, :], glu_stage[:, 1, :],
                                            ALU.mult).then_inc(glu_used, 1)
                    dve.wait_ge(glu_used, i + 1)
                    ch.link(nc.vector.tensor_scalar(m.conv[:, i, 0:T], u_pad[:, i, 0:T], m.params[:, i, 0:1],
                                                    m.params[:, i, par("conv_b"):par("conv_b") + 1], ALU.mult, ALU.add))
                    for j in range(1, CW):
                        ch.link(nc.vector.scalar_tensor_tensor(m.conv[:, i, 0:T], u_pad[:, i, j:j + T],
                                                               m.params[:, i, j:j + 1], m.conv[:, i, 0:T], ALU.mult, ALU.add))
                for s, (_, _, _, w) in enumerate(SHIFT_TILES):
                    dve.wait_ge(tile_taken, NCONV + s + 1)
                    st = staged[0:w, s % ZB, :]
                    ch.link(nc.vector.tensor_tensor(z_diff[0:w, s % 2, :], st[:, 0:T], st[:, 1:T + 1], ALU.subtract))
                    nc.vector.scalar_tensor_tensor(m.zs[0:w, s, 0:T], z_diff[0:w, s % 2, :], shift_t[0:w, s, B:B + 1],
                                                   st[:, 1:T + 1], ALU.mult, ALU.add).then_inc(staged_used, 1)
                dve.wait_ge(sample_taken, 1)
                nc.vector.tensor_copy(z_last[:, 0:NSH - 1, 1:], z_sample[:, NCONV:NCOL - 1, :])
                nc.vector.tensor_copy(z_last[0:32, NSH - 1, 1:], z_sample[0:32, NCOL - 1, :])
                for sl, w in ((slice(0, NSH - 1), P), (slice(NSH - 1, NSH), 32)):
                    zc = slice(NCONV + sl.start, NCONV + sl.stop)
                    n = sl.stop - sl.start
                    ch.link(nc.vector.tensor_tensor(zd_sample[0:w, sl, :], shift_t[0:w, sl, 0:B], z_sample[0:w, zc, :], ALU.subtract))
                    ch.link(nc.vector.tensor_tensor(zd_sample[0:w, sl, :], zd_sample[0:w, sl, :],
                                                    shift_t[0:w, sl, B:B + 1].broadcast_to([w, n, B]), ALU.mult))
                    ch.link(nc.vector.tensor_tensor(m.zs[0:w, sl, T:TT], zd_sample[0:w, sl, :], z_sample[0:w, zc, :], ALU.add))
                glu = z_sample[:, 0:NCONV, :].rearrange("p (i two) b -> p i two b", two=2)
                dve.wait_ge(sample_gated, 1)
                ch.link(nc.vector.tensor_tensor(u_sample[:], glu[:, :, 0, :], gate_sample[:], ALU.mult))
                ch.link(nc.vector.tensor_tensor(conv_prod[:].rearrange("p i (b j) -> p i b j", b=B),
                                                conv_state[:].rearrange("p i (b j) -> p i b j", b=B),
                                                m.params[:, :, 0:CW - 1].unsqueeze(2).broadcast_to([P, CT, B, CW - 1]), ALU.mult))
                ch.link(nc.vector.tensor_reduce(conv_sum[:], conv_prod[:].rearrange("p i (b j) -> p i b j", b=B), AX, ALU.add))
                ch.link(nc.vector.tensor_tensor(m.conv[:, :, T:TT], u_sample[:],
                                                m.params[:, :, CW - 1:CW].broadcast_to([P, CT, B]), ALU.mult))
                ch.link(nc.vector.tensor_tensor(conv_sum[:], conv_sum[:],
                                                m.params[:, :, par("conv_b"):par("conv_b") + 1].broadcast_to([P, CT, B]), ALU.add))
                ch.link(nc.vector.tensor_tensor(m.conv[:, :, T:TT], m.conv[:, :, T:TT], conv_sum[:], ALU.add))
                nc.vector.tensor_copy(tail_in[:, :, 0:30], u_pad[:, :, T:T + CW - 1])
                nc.vector.tensor_copy(tail_in[:, :, 30:38], u_sample[:]).then_inc(tails_ready, 2)
                dve.wait_ge(tails_turned, 1)
                nc.vector.tensor_copy(tail_rows[:], pm[0:38, 0, :]).then_inc(tails_copied, 2)
                for q in range(4):
                    dve.wait_ge(tails_turned, q + 2)
                    for s in range(4 * q, min(4 * q + 4, NSH)):
                        _, _, c0, w = SHIFT_TILES[s]
                        last = nc.vector.tensor_copy(shift_out[:, c0 - _RW:c0 - _RW + w],
                                                     pm[0:1 + B, 1 - q % 2, (s % 4) * P:(s % 4) * P + w])
                    last.then_inc(tails_copied, 1)

            @block.gpsimd
            def _(pool):
                constants(nc, m, consts_ready)(pool)



def time_prepare(nc, m, ctx_out):
    with ExitStack() as ctx:
        def sb(name, shape, dt=F32):
            return ctx.enter_context(nc.sbuf_tensor(name, shape, dt))

        def ps(name, shape, dt=F32):
            return ctx.enter_context(nc.psum_tensor(name, shape, dt))

        def sem(name):
            m.spent.append(ctx_out.enter_context(nc.semaphore(name)))
            return m.spent[-1]

        lora_w = sb("lora_w", [P, DC])
        g_up0 = sb("g_up0", [P, DC])
        g_up1 = sb("g_up1", [32, DC])
        wd_tanh = sb("wd_tanh", [LW, TT])
        gd_sig = place(m, m.BESIDE_ROWS, 2, TT)
        decay = place(m, m.BESIDE_ZS, CT, TT)
        rate = place(m, m.BESIDE_ZS + CT * TT, CT, TT)
        sq = sb("sq", [P, TT])
        norm = sb("norm", [P, TT])
        kk = sb("kk", [P, TT])
        k2 = sb("k2", [P, TT])
        kb = sb("kb", [P, TT])
        tmp = sb("tmp", [P, TT])
        rk = sb("rk", [P, TT])
        cum = sb("cum", [P, T])
        cum_before = sb("cum_before", [P, T])
        cum_end = sb("cum_end", [P, T])
        e_before = sb("e_before", [P, T])
        e_after = sb("e_after", [P, T])
        e_inverse = sb("e_inverse", [P, T])
        e_end = sb("e_end", [P, T])
        b_end = sb("b_end", [P, T])
        k_end = sb("k_end", [P, T])
        big = ps("big", [P, 2, 1024])
        turn = ps("turn", [P, 2, 512])
        pg = ps("pg", [P, 512])
        pb = ps("pb", [P, NT * H])

        w_in2 = sem("lora_loaded")
        tanh_ready = sem("tanh_ready")
        lora_done = sem("lora_done")
        lora_taken = sem("lora_taken")
        sq_ready = sem("sq_ready")
        ss_done = sem("ss_done")
        norm_root = sem("norm_root")
        cum_ready = sem("cum_ready")
        exp_ready = sem("exp_ready")
        bonus_in = sem("bonus_in")
        bonus_done = sem("bonus_done")
        scaled_ready = sem("scaled_ready")
        turned = sem("turned")
        turned_taken = sem("turned_taken")
        gate_done = sem("gate_done")
        gate_taken = sem("gate_taken")
        kk_used = sem("kk_used")
        NTURN = 5

        with nc.Block() as block:
            @block.sync
            def _(sp):
                sp.dma_start(lora_w[0:LW, :], m.w_up).then_inc(w_in2, 16)
                sp.dma_start(lora_w[LW:P, :], m.a_up).then_inc(w_in2, 16)
                sp.dma_start(g_up0[:], m.g_up[0:P, :]).then_inc(w_in2, 16)
                sp.dma_start(g_up1[:], m.g_up[P:LG, :]).then_inc(w_in2, 16)

            @block.tensor
            def _(pe):
                pe.wait_ge(w_in2, 64)
                pe.wait_ge(tanh_ready, 1)
                for j in range(2 * CT):
                    i, rows = j // 2, slice(0, LW) if j % 2 == 0 else slice(LW, P)
                    src = wd_tanh[:, :] if j % 2 == 0 else m.zs[LW:P, LORA, :]
                    if j >= 2:
                        pe.wait_ge(lora_taken, j - 1)
                    for c0, c1 in ((0, T), (T, TT)):
                        last = nc.tensor.matmul(big[:, j % 2, c0:c1], lora_w[rows, i * P:(i + 1) * P], src[:, c0:c1],
                                                start=True, stop=True)
                    last.then_inc(lora_done, 1)
                pe.wait_ge(tanh_ready, 2)
                for i, (t0, n) in enumerate(TOK_TILES):
                    if i >= 1:
                        pe.wait_ge(gate_taken, i)
                    nc.tensor.matmul(pg[0:n, :], gd_sig[:, 0, t0:t0 + n], g_up0[:], start=True, stop=False)
                    nc.tensor.matmul(pg[0:n, :], gd_sig[0:32, 1, t0:t0 + n], g_up1[:], start=False, stop=True).then_inc(gate_done, 1)
                pe.wait_ge(lora_taken, 2 * CT)
                for i in range(CT):
                    pe.wait_ge(sq_ready, i + 1)
                    for c0, c1 in ((0, T), (T, TT)):
                        last = nc.tensor.matmul(big[:, 0, c0:c1], m.head_ones[:], sq[:, c0:c1], start=True, stop=True)
                    last.then_inc(ss_done, 1)
                    pe.wait_ge(bonus_in, i + 1)
                    for j, (t0, n) in enumerate(TOK_TILES):
                        last = nc.tensor.matmul(pb[0:n, j * H + 2 * i:j * H + 2 * i + 2], rk[:, t0:t0 + n], m.head_ones[:, 0:P:N],
                                                start=True, stop=True)
                    last.then_inc(bonus_done, 1)
                    for q in range(NTURN):
                        g = NTURN * i + q
                        if g >= 2:
                            pe.wait_ge(turned_taken, g - 1)
                        if q < 4:
                            if q == 0:
                                pe.wait_ge(scaled_ready, i + 1)
                            for j in range(TM):
                                src = (m.read_decayed[:, i, j, 0, :], b_end[:, cols(j)], k_end[:, cols(j)],
                                       m.zs[:, shift_index("v", i), cols(j)])[q]
                                last = nc.tensor.transpose(turn[:, g % 2, j * P:(j + 1) * P], src, m.ident[:])
                        else:
                            last = nc.tensor.transpose(turn[0:B, g % 2, 0:P], m.zs[:, shift_index("v", i), T:TT], m.ident[:])
                        last.then_inc(turned, 1)

            @block.scalar
            def _(act):
                nc.scalar.activation(wd_tanh[:], m.zs[0:LW, LORA, :], ACT.Tanh).then_inc(tanh_ready, 1)
                nc.scalar.activation(gd_sig[:, 0, :], m.zs[:, GATE0, :], ACT.Sigmoid)
                nc.scalar.activation(gd_sig[0:32, 1, :], m.zs[0:32, GATE1, :], ACT.Sigmoid).then_inc(tanh_ready, 1)
                for j in range(2 * CT):
                    i = j // 2
                    act.wait_ge(lora_done, j + 1)
                    dst, bias = (decay, "w0") if j % 2 == 0 else (rate, "a0")
                    nc.scalar.activation(dst[:, i, :], big[:, j % 2, 0:TT], ACT.Sigmoid,
                                         bias=m.params[:, i, par(bias):par(bias) + 1]).then_inc(lora_taken, 1)
                for i, (_, n) in enumerate(TOK_TILES):
                    act.wait_ge(gate_done, i + 1)
                    nc.scalar.copy(m.gate[0:n, i, :], pg[0:n, :]).then_inc(gate_taken, 1)
                for i in range(CT):
                    if i >= 1:
                        act.wait_ge(ss_done, i)
                    nc.scalar.activation(sq[:], m.zs[:, shift_index("k", i), :], ACT.Square,
                                         scale=m.params[:, i, par("k_k"):par("k_k") + 1]).then_inc(sq_ready, 1)
                    act.wait_ge(ss_done, i + 1)
                    if i >= 1:
                        act.wait_ge(kk_used, i)
                    nc.scalar.activation(norm[:], big[:, 0, 0:TT], ACT.Sqrt).then_inc(norm_root, 1)
                    act.wait_ge(cum_ready, i + 1)
                    if i >= 1:
                        act.wait_ge(scaled_ready, i)
                    nc.scalar.activation(e_before[:], cum_before[:], ACT.Exp, scale=-DECAY_SCALE)
                    nc.scalar.activation(e_after[:], cum[:], ACT.Exp, scale=-DECAY_SCALE)
                    nc.scalar.activation(e_inverse[:], cum[:], ACT.Exp, scale=DECAY_SCALE)
                    nc.scalar.activation(e_end[:], cum_end[:], ACT.Exp, scale=DECAY_SCALE)
                    nc.scalar.activation(m.chunk_decay[:, i, :], cum[:, L - 1:T:L], ACT.Exp, scale=-DECAY_SCALE)
                    nc.scalar.activation(m.sample_vec[:, 0, i, :], decay[:, i, T:TT], ACT.Exp, scale=-DECAY_SCALE).then_inc(exp_ready, 1)
                    for q in range(NTURN):
                        g = NTURN * i + q
                        act.wait_ge(turned, g + 1)
                        if q < 4:
                            nc.scalar.copy((m.a_rows, m.b_rows, m.k_rows, m.v_rows)[q][:, 0:TM, i * P:(i + 1) * P],
                                           turn[:, g % 2, :].rearrange("p (j c) -> p j c", j=TM)).then_inc(turned_taken, 1)
                        else:
                            nc.scalar.copy(m.v_rows[0:B, TM, i * P:(i + 1) * P], turn[0:B, g % 2, 0:P]).then_inc(turned_taken, 1)

            @block.vector
            def _(dve):
                ch = Chain(dve, m.vector_step, m.vector_count)
                for i in range(CT):
                    r = m.zs[:, shift_index("r", i), :]
                    k = m.zs[:, shift_index("k", i), :]
                    v = m.zs[:, shift_index("v", i), :]
                    if i == 0:
                        dve.wait_ge(lora_taken, 2 * CT)
                    if i >= 1:
                        dve.wait_ge(exp_ready, i)
                        dve.wait_ge(scaled_ready, i)
                    nc.vector.tensor_scalar(kk[:], k, m.params[:, i, par("k_k"):par("k_k") + 1], None, ALU.mult)
                    nc.vector.tensor_scalar(tmp[:], rate[:, i, :], 1.0, m.params[:, i, par("k_a"):par("k_a") + 1],
                                            ALU.subtract, ALU.mult)
                    ch.link(nc.vector.tensor_tensor_scan(cum[:], m.chunk_keep[:], decay[:, i, 0:T], 0.0, ALU.mult, ALU.add))
                    nc.vector.tensor_tensor(cum_before[:], cum[:], decay[:, i, 0:T], ALU.subtract)
                    nc.vector.tensor_tensor(cum_end[:].rearrange("p (c l) -> p c l", l=L), cum[:].rearrange("p (c l) -> p c l", l=L),
                                            cum[:, L - 1:T:L].unsqueeze(2).broadcast_to([P, NCH, L]), ALU.subtract).then_inc(cum_ready, 1)
                    ch.link(nc.vector.scalar_tensor_tensor(k2[:], tmp[:], 1.0, k, ALU.add, ALU.mult))
                    if i >= 1:
                        dve.wait_ge(bonus_done, i)
                    nc.vector.scalar_tensor_tensor(rk[:], r, m.params[:, i, par("r_k"):par("r_k") + 1], k2[:],
                                                   ALU.mult, ALU.mult).then_inc(bonus_in, 1)
                    dve.wait_ge(norm_root, i + 1)
                    ch.link(nc.vector.tensor_scalar(tmp[:], norm[:], 1e-12, None, ALU.max))
                    ch.link(nc.vector.reciprocal(tmp[:], tmp[:]))
                    ch.link(nc.vector.tensor_tensor(kk[:], kk[:], tmp[:], ALU.mult))
                    nc.vector.tensor_copy(m.sample_vec[:, 1, i, :], kk[:, T:TT]).then_inc(kk_used, 1)
                    ch.link(nc.vector.scalar_tensor_tensor(kb[:], kk[:], -1.0, rate[:, i, :], ALU.mult, ALU.mult))
                    nc.vector.tensor_copy(m.sample_vec[:, 2, i, :], kb[:, T:TT])
                    nc.vector.tensor_copy(m.sample_vec[:, 3, i, :], k2[:, T:TT])
                    nc.vector.tensor_copy(m.sample_vec[:, 4, i, :], r[:, T:TT])
                    nc.vector.tensor_copy(m.sample_vec[:, 5, i, :], v[:, T:TT])
                    dve.wait_ge(exp_ready, i + 1)
                    if i >= 1:
                        dve.wait_ge(turned, NTURN * (i - 1) + 3)
                    tiles = lambda ap: ap.rearrange("p (j t) -> p j t", j=TM)
                    nc.vector.tensor_tensor(m.read_decayed[:, i, :, 0, :], tiles(kk[:, 0:T]), tiles(e_before[:]), ALU.mult)
                    nc.vector.tensor_tensor(b_end[:], kb[:, 0:T], e_end[:], ALU.mult)
                    nc.vector.tensor_tensor(k_end[:], k2[:, 0:T], e_end[:], ALU.mult)
                    nc.vector.tensor_tensor(m.read_decayed[:, i, :, 1, :], tiles(r[:, 0:T]), tiles(e_after[:]), ALU.mult)
                    nc.vector.tensor_tensor(m.b_grown[:, i, :], kb[:, 0:T], e_inverse[:], ALU.mult)
                    nc.vector.tensor_tensor(m.k_grown[:, i, :], k2[:, 0:T], e_inverse[:], ALU.mult).then_inc(scaled_ready, 1)
                dve.wait_ge(bonus_done, CT)
                nc.vector.tensor_copy(m.bonus[:, 0:TM, :], pb[:, 0:TM * H].rearrange("p (j h) -> p j h", h=H))
                nc.vector.tensor_copy(m.bonus[0:B, TM, :], pb[0:B, TM * H:])

def solve_chunks(nc, m, ctx_out):
    SETS = TM * H
    with ExitStack() as ctx:
        def sb(name, shape, dt=F32):
            return ctx.enter_context(nc.sbuf_tensor(name, shape, dt))

        def ps(name, shape, dt=F32):
            return ctx.enter_context(nc.psum_tensor(name, shape, dt))

        def sem(name):
            m.spent.append(ctx_out.enter_context(nc.semaphore(name)))
            return m.spent[-1]

        lower = sb("lower", [P, SETS, L])
        sys_n = place(m, m.BESIDE_ZS, L, L)
        sol_t = place(m, m.BESIDE_ZS + L * L, L, L)
        prod = sb("prod", [P, L * L])
        sample_rows = sb("sample_rows", [B, 6, DC])
        sv = sb("sv", [P, 5, N])
        sval = sb("sval", [P, 32])
        free = m.zs[:].rearrange("p s t -> p (s t)")
        st, st_p, st_q = (free[:, i * 32 * N:(i + 1) * 32 * N].rearrange("p (v k) -> p v k", k=N) for i in range(3))
        s_a = sb("s_a", [P, 32])
        s_y = sb("s_y", [P, 32])
        sq = place(m, m.BESIDE_ZS + 2 * L * L, CT, TT)
        scale = sb("ln_scale", [P, TT])
        pa = ps("pa", [P, 2, 4, P])
        big = ps("big3", [P, 2, 1024])
        psv = ps("psv", [P, 2, 512])

        pairs_done = sem("pairs_done")
        pairs_taken = sem("pairs_taken")
        lower_stored = sem("lower_stored")
        sys_loaded = sem("sys_loaded")
        solved = sem("solved")
        inverse_cleared = sem("inverse_cleared")
        sol_stored = sem("sol_stored")
        sol_loaded = sem("sol_loaded")
        sample_turned = sem("sample_turned")
        sample_copied = sem("sample_copied")
        sample_stored = sem("sample_stored")
        sample_loaded = sem("sample_loaded")
        state_loaded = sem("state_loaded")
        outer_done = sem("outer_done")
        reduced = sem("reduced")
        y_stored = sem("y_stored")
        y_loaded = sem("y_loaded")
        mean_done = sem("mean_done")
        centred = sem("centred")
        squared = sem("squared")
        var_done = sem("var_done")
        rooted = sem("rooted")
        scaled = sem("scaled")
        gated = sem("gated")
        sample_state_stored = sem("sample_state_stored")

        with nc.Block() as block:
            @block.tensor
            def _(pe):
                for g in range(2 * TM):
                    j, odd = g // 2, g % 2
                    if g >= 2:
                        pe.wait_ge(pairs_taken, g - 1)
                    for h in range(odd, H, 2):
                        rows = slice(N * odd, N * odd + N)
                        last = nc.tensor.matmul(pa[:, odd, h // 2, :], m.read_decayed[rows, h // 2, j, 0, :],
                                                m.b_grown[rows, h // 2, j * P:(j + 1) * P], start=True, stop=True)
                    last.then_inc(pairs_done, 1)
                for s in range(6):
                    if s >= 2:
                        pe.wait_ge(sample_copied, s - 1)
                    for i in range(CT):
                        last = nc.tensor.transpose(psv[0:B, s % 2, i * P:(i + 1) * P], m.sample_vec[:, s, i, :], m.ident[:])
                    last.then_inc(sample_turned, 1)
                for c0, c1 in ((0, T), (T, TT)):
                    for i in range(CT):
                        last = nc.tensor.matmul(big[:, 0, c0:c1], m.ones_mean[:], m.conv[:, i, c0:c1], start=(i == 0), stop=(i == CT - 1))
                last.then_inc(mean_done, 1)
                pe.wait_ge(squared, 1)
                for c0, c1 in ((0, T), (T, TT)):
                    for i in range(CT):
                        last = nc.tensor.matmul(big[:, 1, c0:c1], m.ones_mean[:], sq[:, i, c0:c1], start=(i == 0), stop=(i == CT - 1))
                last.then_inc(var_done, 1)

            @block.sync
            def _(sp):
                sp.dma_start(st.rearrange("p v k -> p (v k)"), m.state_wkv).then_inc(state_loaded, 16)
                sp.wait_ge(pairs_taken, 2 * TM)
                sp.dma_start(m.scr_lower.rearrange("(s c) (t j) -> (c t) s j", c=CM, j=L), lower[:]).then_inc(lower_stored, 16)
                sp.wait_ge(sample_copied, 6)
                sp.dma_start(m.scr_sample.rearrange("s b c -> b s c"), sample_rows[:]).then_inc(sample_stored, 16)
                sp.wait_ge(lower_stored, 16)
                sp.dma_start(sys_n[:].rearrange("p t j -> p (t j)"), m.scr_lower).then_inc(sys_loaded, 16)
                sp.wait_ge(sample_stored, 16)
                for half in range(2):
                    sp.dma_start(sv[half::2, :, :], m.scr_sample[0:5].rearrange("s b (h n) -> (b h) s n", n=N)).then_inc(sample_loaded, 16)
                sp.dma_start(sval[:], m.scr_sample[5].rearrange("b (h two v) -> (b h two) v", two=2, v=32)).then_inc(sample_loaded, 16)
                sp.wait_ge(outer_done, 4)
                sp.dma_start(m.new_wkv_s, st.rearrange("p v k -> p (v k)")).then_inc(sample_state_stored, 16)
                sp.wait_ge(reduced, 2)
                sp.dma_start(m.scr_y.rearrange("b (h two v) -> (b h two) v", two=2, v=32), s_y[:]).then_inc(y_stored, 16)
                sp.wait_ge(y_stored, 16)
                sp.dma_start(m.y_sample_rows[:], m.scr_y).then_inc(y_loaded, 16)
                sp.wait_ge(solved, 1)
                sp.dma_start(m.scr_solved, sol_t[:].rearrange("p j t -> p (j t)")).then_inc(sol_stored, 16)
                sp.wait_ge(sol_stored, 16)
                sp.wait_ge(inverse_cleared, 1)
                for c in range(CM):
                    sp.dma_start(m.inverse[L * c:L * (c + 1), :, L * c:L * (c + 1)],
                                 m.scr_solved.rearrange("(s c) (j t) -> c j s t", c=CM, j=L)[c]).then_inc(sol_loaded, 16)
                sp.wait_ge(sol_loaded, 16 * CM)
                sp.wait_ge(y_loaded, 16)
                sp.wait_ge(sample_state_stored, 16)

            @block.scalar
            def _(act):
                for s in range(6):
                    act.wait_ge(sample_turned, s + 1)
                    nc.scalar.copy(sample_rows[:, s, :], psv[0:B, s % 2, :]).then_inc(sample_copied, 1)
                act.wait_ge(centred, 1)
                for i in range(CT):
                    last = nc.scalar.activation(sq[:, i, :], m.conv[:, i, :], ACT.Square)
                last.then_inc(squared, 1)
                act.wait_ge(var_done, 1)
                nc.scalar.activation(scale[:], big[:, 1, 0:TT], ACT.Sqrt, bias=m.eps_ln[:]).then_inc(rooted, 1)
                act.wait_ge(scaled, 1)
                for i in range(CT):
                    last = nc.scalar.activation(sq[:, i, :], m.conv[:, i, :], ACT.Sigmoid,
                                                scale=m.params[:, i, par("conv_ln_g"):par("conv_ln_g") + 1],
                                                bias=m.params[:, i, par("conv_ln_b"):par("conv_ln_b") + 1])
                last.then_inc(gated, 1)

            @block.gpsimd
            def _(pool):
                ch = Chain(pool, m.pool_step, m.pool_count)
                keys = lambda s: sv[:, s, :].unsqueeze(1).broadcast_to([P, 32, N])
                values = lambda ap: ap.unsqueeze(2).broadcast_to([P, 32, N])
                nc.gpsimd.memset(m.inverse[:], 0.0).then_inc(inverse_cleared, 1)
                pool.wait_ge(state_loaded, 16)
                pool.wait_ge(sample_loaded, 48)
                nc.gpsimd.tensor_tensor(st_p, st, keys(1), ALU.mult).then_inc(outer_done, 1)
                ch.link(nc.gpsimd.tensor_tensor(st_q, values(sval[:]), keys(3), ALU.mult))
                ch.link(nc.gpsimd.tensor_tensor(st, st, keys(0), ALU.mult))
                ch.link(nc.gpsimd.tensor_tensor(st, st, st_q, ALU.add))
                pool.wait_ge(reduced, 1)
                nc.gpsimd.tensor_tensor(st_q, values(s_a[:]), keys(2), ALU.mult).then_inc(outer_done, 1)
                pool.wait_ge(outer_done, 2)
                nc.gpsimd.tensor_tensor(st, st, st_q, ALU.add).then_inc(outer_done, 1)
                pool.wait_ge(outer_done, 3)
                nc.gpsimd.tensor_tensor(st_p, st, keys(4), ALU.mult).then_inc(outer_done, 1)

            @block.vector
            def _(dve):
                ch = Chain(dve, m.vector_step, m.vector_count)
                for g in range(2 * TM):
                    dve.wait_ge(pairs_done, g + 1)
                    sets = slice(H * (g // 2) + g % 2, H * (g // 2) + H, 2)
                    for c in range(CM):
                        r = slice(L * c, L * (c + 1))
                        last = nc.vector.tensor_tensor(lower[r, sets, :], pa[r, g % 2, :, L * c:L * (c + 1)],
                                                       m.below[r, :].unsqueeze(1).broadcast_to([L, 4, L]), ALU.mult)
                    last.then_inc(pairs_taken, 1)
                ch.link(nc.vector.memset(sol_t[:], 0.0))
                ch.link(nc.vector.memset(sol_t[:].rearrange("p j t -> p (j t)")[:, 0:L * L:L + 1], 1.0))
                dve.wait_ge(mean_done, 1)
                for i in range(CT):
                    last = nc.vector.tensor_tensor(m.conv[:, i, :], m.conv[:, i, :], big[:, 0, 0:TT], ALU.subtract)
                last.then_inc(centred, 1)
                dve.wait_ge(sys_loaded, 16)
                for t in range(1, L):
                    if t == 4:
                        dve.wait_ge(rooted, 1)
                        ch.link(nc.vector.reciprocal(scale[:], scale[:]))
                        for i in range(CT):
                            last = nc.vector.tensor_tensor(m.conv[:, i, :], m.conv[:, i, :], scale[:], ALU.mult)
                        last.then_inc(scaled, 1)
                    if t == 20:
                        dve.wait_ge(scaled, 1)
                        dve.wait_ge(gated, 1)
                        for i in range(CT):
                            ch.link(nc.vector.tensor_scalar(m.conv[:, i, :], m.conv[:, i, :],
                                                            m.params[:, i, par("conv_ln_g"):par("conv_ln_g") + 1],
                                                            m.params[:, i, par("conv_ln_b"):par("conv_ln_b") + 1], ALU.mult, ALU.add))
                            nc.vector.tensor_tensor(m.conv[:, i, :], m.conv[:, i, :], sq[:, i, :], ALU.mult)
                    if t == 6:
                        dve.wait_ge(outer_done, 1)
                        nc.vector.tensor_reduce(s_a[:], st_p, AX, ALU.add).then_inc(reduced, 1)
                    if t == 28:
                        dve.wait_ge(outer_done, 4)
                        nc.vector.tensor_reduce(s_y[:], st_p, AX, ALU.add).then_inc(reduced, 1)
                    pr = prod[:, 0:t * t].rearrange("p (j s) -> p j s", j=t)
                    ch.link(nc.vector.tensor_tensor(pr, sol_t[:, 0:t, 0:t], sys_n[:, t, 0:t].unsqueeze(1).broadcast_to([P, t, t]), ALU.mult))
                    last = nc.vector.tensor_reduce(sol_t[:, 0:t, t], pr, AX, ALU.add)
                    if t < L - 1:
                        ch.link(last)
                last.then_inc(solved, 1)


def recur(nc, m, ctx_out):
    with ExitStack() as ctx:
        def sb(name, shape, dt=F32):
            return ctx.enter_context(nc.sbuf_tensor(name, shape, dt))

        def ps(name, shape, dt=F32):
            return ctx.enter_context(nc.psum_tensor(name, shape, dt))

        def sem(name):
            return ctx_out.enter_context(nc.semaphore(name))

        inside = m.zs[:].rearrange("p s t -> p (s t)")[:, 0:2 * H * 3 * P].rearrange("p (b h a t) -> p b h a t", b=2, h=H, a=3)
        pushed = sb("pushed", [P, DC])
        w2 = sb("w2", [P, 2, DC])
        w1_t = place(m, m.BESIDE_ROWS, 2, CT, P)
        u = sb("u", [P, 2, DC])
        state = sb("state", [P, 2, CT, N])
        y = sb("y", [P, 2, DC])
        y_sq = sb("y_sq", [P, DC])
        o = sb("o", [P, 3, DC])
        stat = sb("stat", [P, 4, H])
        gn_g = sb("gn_g", [P, DC])
        gn_b = sb("gn_b", [P, DC])
        state_rows = w2[0:N, TM % 2, :].rearrange("v (h k) -> v h k", h=H)
        pin = ps("pin", [P, 2, 512])
        pw = ps("pw", [P, 2, 512])
        pu = ps("pu", [P, 2, 2, CT, N])
        pst = ps("pst", [P, CT, P])
        py = ps("py", [P, 512])

        gn_loaded = sem("gn_loaded")
        inside_done = sem("inside_done")
        inside_taken = sem("inside_taken")
        push_done = sem("push_done")
        push_taken = sem("push_taken")
        w2_done = sem("w2_done")
        w2_taken = sem("w2_taken")
        w1_done = sem("w1_done")
        w1_taken = sem("w1_taken")
        u_done = sem("u_done")
        u_taken = sem("u_taken")
        state_done = sem("state_done")
        state_ready = sem("state_ready")
        y_state_done = sem("y_state_done")
        y_done = sem("y_done")
        y_taken = sem("y_taken")
        y_state_taken = sem("y_state_taken")
        rooted = sem("gn_rooted")
        gn_var_ready = sem("gn_var_ready")
        gn_squared = sem("gn_squared")
        centred = sem("gn_centred")
        normed = sem("gn_normed")
        o_ready = sem("o_ready")
        o_turned = sem("o_turned")
        o_taken = sem("o_taken")
        final_turned = sem("final_turned")
        final_ready = sem("final_ready")
        final_stored = sem("final_stored")

        BEFORE = ((), (1,), (4,), ())
        AFTER = ((0,), (2, 3), (5, 6, 7), ())

        def rows(h):
            return slice(N * (h % 2), N * (h % 2) + N)

        with nc.Block() as block:
            @block.gpsimd
            def _(pool):
                for spent in m.spent:
                    pool.sem_clear(spent)
                ch = Chain(pool, m.pool_step, m.pool_count)
                tt = nc.gpsimd.tensor_tensor
                pool.wait_ge(gn_loaded, 32)
                for i, (_, n) in enumerate(TOK_TILES):
                    yi, oi = y[0:n, i % 2, :], o[0:n, i % 3, :]
                    by_head = lambda ap: ap.rearrange("p (h c) -> p h c", h=H)
                    if i >= 3:
                        pool.wait_ge(o_turned, i - 2)
                    ch.link(tt(by_head(oi), by_head(m.v_rows[0:n, i, :]), m.bonus[0:n, i, :].unsqueeze(2).broadcast_to([n, H, N]), ALU.mult))
                    pool.wait_ge(normed, i + 1)
                    ch.link(tt(yi, yi, gn_g[0:n, :], ALU.mult))
                    ch.link(tt(yi, yi, gn_b[0:n, :], ALU.add))
                    ch.link(tt(oi, oi, yi, ALU.add))
                    tt(oi, oi, m.gate[0:n, i, :], ALU.mult).then_inc(o_ready, 1)

            @block.sync
            def _(sp):
                sp.dma_start(gn_g[:], m.vec["gn_g"].broadcast_to([P, DC])).then_inc(gn_loaded, 16)
                sp.dma_start(gn_b[:], m.vec["gn_b"].broadcast_to([P, DC])).then_inc(gn_loaded, 16)
                sp.dma_start(m.w_out_half[0][:], m.w_out[:, 0:512].rearrange("(k p) n -> p k n", p=P)).then_inc(m.w_out_loaded[0], 16)
                for i in range(2):
                    sp.dma_start(m.x_again[:, i, :], m.x_prompt[i * P:(i + 1) * P, :]).then_inc(m.x_again_loaded[i], 16)
                sp.wait_ge(final_ready, 2)
                sp.dma_start(m.new_wkv_p.rearrange("h v k -> v h k"), state_rows).then_inc(final_stored, 16)
                sp.wait_ge(final_stored, 16)

            @block.tensor
            def _(pe):
                def products(j, h):
                    g = H * j + h
                    if g >= 2:
                        pe.wait_ge(inside_taken, g - 1)
                    c = slice(j * P, (j + 1) * P)
                    nc.tensor.matmul(pin[:, g % 2, 0:2 * P], m.k_grown[rows(h), h // 2, c],
                                     m.read_decayed[rows(h), h // 2, j].rearrange("p a t -> p (a t)"), start=True, stop=True)
                    nc.tensor.matmul(pin[:, g % 2, 2 * P:3 * P], m.b_grown[rows(h), h // 2, c],
                                     m.read_decayed[rows(h), h // 2, j, 1, :], start=True, stop=True).then_inc(inside_done, 1)

                def push_first(j):
                    pe.wait_ge(inside_taken, H * (j + 1))
                    if j >= 1:
                        pe.wait_ge(w2_taken, j)
                    for h in range(H):
                        last = nc.tensor.matmul(pw[:, 0, h * N:(h + 1) * N], inside[:, j % 2, h, 0, :], m.v_rows[:, j, h * N:(h + 1) * N],
                                                start=True, stop=True)
                    last.then_inc(push_done, 1)
                    if j >= 1:
                        pe.wait_ge(w1_taken, j)
                    for h in range(H):
                        last = nc.tensor.matmul(pw[rows(h), 1, (h // 2) * P:(h // 2 + 1) * P], m.a_rows[:, j, h * N:(h + 1) * N],
                                                m.inverse[:, H * j + h, :], start=True, stop=True)
                    last.then_inc(w1_done, 1)

                def push_second(j):
                    pe.wait_ge(push_taken, j + 1)
                    for h in range(H):
                        last = nc.tensor.matmul(pw[:, 0, h * N:(h + 1) * N], m.inverse[:, H * j + h, :], pushed[:, h * N:(h + 1) * N],
                                                start=True, stop=True)
                    last.then_inc(w2_done, 1)

                def outputs_inside(j):
                    if j >= 1:
                        pe.wait_ge(y_taken, j)
                    for h in range(H):
                        hc = slice(h * N, (h + 1) * N)
                        nc.tensor.matmul(py[:, hc], inside[:, j % 2, h, 1, :], m.v_rows[:, j, hc], start=True, stop=False)
                        last = nc.tensor.matmul(py[:, hc], inside[:, j % 2, h, 2, :], u[:, j % 2, hc], start=False, stop=True)
                    last.then_inc(y_done, 1)

                for h in range(H):
                    products(0, h)
                push_first(0)
                push_second(0)
                for j in range(TM):
                    for c in range(CM):
                        n = CM * j + c
                        q = slice(L * c, L * (c + 1))
                        pe.wait_ge(w1_taken, j + 1)
                        pe.wait_ge(state_ready, n + 1)
                        if n >= 1:
                            pe.wait_ge(u_taken, n)
                        if c == 0 and j >= 1:
                            pe.wait_ge(y_state_taken, j)
                        for h in range(H):
                            last = nc.tensor.matmul(pu[q, h % 2, 0, h // 2, :], w1_t[rows(h), j % 2, h // 2, q],
                                                    state[rows(h), n % 2, h // 2, :], start=True, stop=True)
                        last.then_inc(u_done, 1)
                        for h in range(H):
                            hc = slice(h * N, (h + 1) * N)
                            nc.tensor.matmul(pst[rows(h), h // 2, N:], m.k_rows[q, j, hc], m.v_rows[q, j, hc], start=True, stop=True)
                        if c == 0 and j >= 1:
                            outputs_inside(j - 1)
                        if j + 1 < TM:
                            for h in BEFORE[c]:
                                products(j + 1, h)
                            if c == CM - 1:
                                push_first(j + 1)
                        pe.wait_ge(u_taken, n + 1)
                        for h in range(H):
                            hc = slice(h * N, (h + 1) * N)
                            last = nc.tensor.matmul(pst[rows(h), h // 2, 0:N], m.b_rows[q, j, hc], u[q, j % 2, hc], start=True, stop=True)
                        last.then_inc(state_done, 1)
                        for h in range(H):
                            last = nc.tensor.matmul(pu[q, h % 2, 1, h // 2, :], m.read_decayed[rows(h), h // 2, j, 1, q],
                                                    state[rows(h), n % 2, h // 2, :], start=True, stop=True)
                        last.then_inc(y_state_done, 1)
                        if j + 1 < TM:
                            for h in AFTER[c]:
                                products(j + 1, h)
                    if j + 1 < TM:
                        push_second(j + 1)
                outputs_inside(TM - 1)
                pe.wait_ge(state_ready, NCH + 1)
                pe.wait_ge(u_taken, NCH)
                pe.wait_ge(y_state_taken, TM)
                for h in range(H):
                    last = nc.tensor.transpose(pu[0:N, h % 2, 0, h // 2, :], state[rows(h), NCH % 2, h // 2, :], m.ident[rows(h), rows(h)])
                last.then_inc(final_turned, 1)
                for i, (t0, n) in enumerate(TOK_TILES):
                    pe.wait_ge(o_ready, i + 1)
                    pe.wait_ge(w1_taken, TM)
                    if i >= 1:
                        pe.wait_ge(o_taken, i)
                    for k in range(CT):
                        last = nc.tensor.transpose(pw[:, 1, k * P:k * P + n], o[0:n, i % 3, k * P:(k + 1) * P], m.ident[0:n, 0:n])
                    last.then_inc(o_turned, 1)

            @block.scalar
            def _(act):
                def copy_pushed(j):
                    act.wait_ge(push_done, j + 1)
                    nc.scalar.copy(pushed[:], pw[:, 0, :]).then_inc(push_taken, 1)
                    act.wait_ge(w1_done, j + 1)
                    nc.scalar.copy(w1_t[:, j % 2, :, :], pw[:, 1, :].rearrange("p (i t) -> p i t", i=CT)).then_inc(w1_taken, 1)

                def copy_w2(j):
                    act.wait_ge(w2_done, j + 1)
                    nc.scalar.copy(w2[:, j % 2, :], pw[:, 0, :]).then_inc(w2_taken, 1)

                def norm_part(i, n):
                    act.wait_ge(centred, i + 1)
                    nc.scalar.activation(y_sq[0:n, :], y[0:n, i % 2, :], ACT.Square).then_inc(gn_squared, 1)
                    act.wait_ge(gn_var_ready, i + 1)
                    nc.scalar.activation(stat[0:n, 2, :], stat[0:n, 1, :], ACT.Sqrt, scale=1.0 / N, bias=m.eps_gn[0:n, :]).then_inc(rooted, 1)

                copy_pushed(0)
                copy_w2(0)
                for j in range(TM):
                    if j >= 1:
                        norm_part(j - 1, P)
                    if j + 1 < TM:
                        copy_pushed(j + 1)
                    act.wait_ge(y_state_done, CM * (j + 1))
                    if j >= 2:
                        act.wait_ge(o_ready, j - 1)
                    nc.scalar.copy(y[:, j % 2, :].rearrange("p (i two c) -> p two i c", two=2, c=N), pu[:, :, 1, :, :]).then_inc(y_state_taken, 1)
                    if j + 1 < TM:
                        copy_w2(j + 1)
                act.wait_ge(final_turned, 1)
                nc.scalar.copy(state_rows.rearrange("v (i two) k -> v two i k", two=2), pu[0:N, :, 0, :, :]).then_inc(final_ready, 2)

                def copy_out(i):
                    t0, n = TOK_TILES[i]
                    act.wait_ge(o_turned, i + 1)
                    nc.scalar.copy(m.o_t[:, :, t0:t0 + n],
                                   pw[:, 1, :].rearrange("p (k t) -> p k t", k=CT)[:, :, 0:n]).then_inc(o_taken, 1)

                norm_part(TM - 1, P)
                for i in range(TM - 2):
                    copy_out(i)
                norm_part(TM, B)
                for i in range(TM - 2, NT):
                    copy_out(i)

            @block.vector
            def _(dve):
                ch = Chain(dve, m.vector_step, m.vector_count)

                def mask(j, h):
                    g = H * j + h
                    dve.wait_ge(inside_done, g + 1)
                    if j >= 2:
                        dve.wait_ge(y_done, j - 1)
                    nc.vector.tensor_tensor(inside[:, j % 2, h, :, :], pin[:, g % 2, 0:3 * P].rearrange("p (a t) -> p a t", a=3),
                                            m.inside_mask[:], ALU.mult).then_inc(inside_taken, 1)

                def centre(i, n):
                    b = i % 2
                    yv = y[0:n, b, :].rearrange("p (h c) -> p h c", h=H)
                    if i < TM:
                        dve.wait_ge(y_state_taken, i + 1)
                        dve.wait_ge(y_done, i + 1)
                        nc.vector.tensor_tensor(y[:, b, :], y[:, b, :], py[:], ALU.add).then_inc(y_taken, 1)
                        dve.wait_ge(y_taken, i + 1)
                    else:
                        dve.wait_ge(o_ready, i - 1)
                        ch.link(nc.vector.tensor_copy(y[0:B, b, :], m.y_sample_rows[:]))
                    ch.link(nc.vector.tensor_reduce(stat[0:n, 0, :], yv, AX, ALU.add))
                    ch.link(nc.vector.tensor_scalar(stat[0:n, 0, :], stat[0:n, 0, :], 1.0 / N, None, ALU.mult))
                    nc.vector.tensor_tensor(yv, yv, stat[0:n, 0, :].unsqueeze(2).broadcast_to([n, H, N]), ALU.subtract).then_inc(centred, 1)

                def normalise(i, n):
                    yv = y[0:n, i % 2, :].rearrange("p (h c) -> p h c", h=H)
                    dve.wait_ge(gn_squared, i + 1)
                    nc.vector.tensor_reduce(stat[0:n, 1, :], y_sq[0:n, :].rearrange("p (h c) -> p h c", h=H), AX, ALU.add).then_inc(gn_var_ready, 1)
                    dve.wait_ge(rooted, i + 1)
                    ch.link(nc.vector.reciprocal(stat[0:n, 3, :], stat[0:n, 2, :]))
                    nc.vector.tensor_tensor(yv, yv, stat[0:n, 3, :].unsqueeze(2).broadcast_to([n, H, N]), ALU.mult).then_inc(normed, 1)

                nc.vector.memset(state[:, 0, :, :], 0.0).then_inc(state_ready, 1)
                for h in range(H):
                    mask(0, h)
                for j in range(TM):
                    for c in range(CM):
                        n = CM * j + c
                        q = slice(L * c, L * (c + 1))
                        dve.wait_ge(w2_taken, j + 1)
                        dve.wait_ge(u_done, n + 1)
                        by_parity = lambda ap: ap.rearrange("p (i two c) -> p two i c", two=2, c=N)
                        nc.vector.tensor_tensor(by_parity(u[q, j % 2, :]), pu[q, :, 0, :, :], by_parity(w2[q, j % 2, :]),
                                                ALU.add).then_inc(u_taken, 1)
                        if n >= 1:
                            dve.wait_ge(y_state_done, n)
                        dve.wait_ge(state_ready, n + 1)
                        ch.link(nc.vector.tensor_tensor(state[:, (n + 1) % 2, :, :], state[:, n % 2, :, :],
                                                        m.chunk_decay[:, :, n:n + 1].broadcast_to([P, CT, N]), ALU.mult))
                        if j + 1 < TM:
                            for h in BEFORE[c]:
                                mask(j + 1, h)
                        dve.wait_ge(state_done, n + 1)
                        ch.link(nc.vector.tensor_tensor(state[:, (n + 1) % 2, :, :], state[:, (n + 1) % 2, :, :], pst[:, :, 0:N], ALU.add))
                        nc.vector.tensor_tensor(state[:, (n + 1) % 2, :, :], state[:, (n + 1) % 2, :, :], pst[:, :, N:],
                                                ALU.add).then_inc(state_ready, 1)
                        if j >= 1 and c == 1:
                            centre(j - 1, P)
                        if j >= 1 and c == 2:
                            normalise(j - 1, P)
                        if j + 1 < TM:
                            for h in AFTER[c]:
                                mask(j + 1, h)
                for i, n in ((TM - 1, P), (TM, B)):
                    centre(i, n)
                    normalise(i, n)


def mix(nc, m, ctx_out):
    BIG = 1e30
    GONE = -3e38
    with ExitStack() as ctx:
        def sb(name, shape, dt=F32):
            return ctx.enter_context(nc.sbuf_tensor(name, shape, dt))

        def ps(name, shape, dt=F32):
            return ctx.enter_context(nc.psum_tensor(name, shape, dt))

        def sem(name):
            return ctx_out.enter_context(nc.semaphore(name))

        w_out = m.w_out_half
        x_rows = m.x_again
        x1 = sb("x1", [P, NT, D])
        x1_t = sb("x1_t", [P, KD, TT])
        ln_g = place(m, m.UPPER + KD * 512, D)
        ln_b = place(m, m.UPPER + KD * 512 + D, D)
        router_w = sb("router_w_sb", [P, KD, E])
        router_b = sb("router_b", [P, E])
        sh_w = sb("sh_w", [P, 2, KD, FE])
        sh_d = sb("sh_d", [P, 2, D])
        sh_sig = sb("sh_sig", [P, TT])
        sh_h = sb("sh_h", [P, 2, TT])
        stats = sb("stats", [P, 2, 6])
        aggr = sb("aggr", [P, 4])
        scores = sb("scores", [P, NT, E])
        sel = sb("sel", [P, NT, E])
        top = sb("top", [P, NT * G, 8])
        grp = sb("grp", [P, NT, G])
        gt = sb("gt", [P, NT, G, G])
        eq = sb("eq", [P, NT, G, G])
        keep = sb("keep", [P, NT, G])
        hit = sb("hit", [P, NT, E])
        gsum = sb("gsum", [P, NT])
        before = sb("before", [P, P])
        first = sb("first", [P, G, G])
        f0 = sb("f0", [P, 2, D])
        jobs3 = x1_t[:].rearrange("p k t -> p (k t)")[:, 0:m.EXTRA * E].rearrange("p (j e) -> p j e", e=E)
        cnt = sb("cnt", [P, 4, E])
        ph = ps("ph", [P, 2, 1024])
        pt = ps("pt5", [P, 2, 512])
        plog = ps("plog", [P, NT, E])
        ppos = ps("ppos", [P, NT + 1, E])

        loaded = sem("mix_loaded")
        x_loaded = m.x_again_loaded
        ln_loaded = sem("ln1_loaded")
        sh_loaded = sem("sh_loaded")
        mixed = sem("mixed")
        mixed_taken = sem("mixed_taken")
        var_ready = sem("var_ready")
        rooted = sem("ln1_rooted")
        x1_ready = sem("x1_ready")
        x1_turned = sem("x1_turned")
        x1_t_ready = sem("x1_t_ready")
        x1_stored = sem("x1_stored")
        logits_done = sem("logits_done")
        scores_ready = sem("scores_ready")
        hits_ready = sem("hits_ready")
        positions_done = sem("positions_done")
        routing_consts = sem("routing_consts")
        sh_done = sem("sh_done")
        sh_sig_ready = sem("sh_sig_ready")
        sh_h_ready = sem("sh_h_ready")
        f_done = sem("f_done")
        f_taken = sem("f_taken")
        f_stored = [sem(f"f_stored{i}") for i in range(2)]
        x_used = sem("x_used")

        with nc.Block() as block:
            @block.sync
            def _(sp):
                sp.dma_start(w_out[1][:], m.w_out[:, 512:1024].rearrange("(k p) n -> p k n", p=P)).then_inc(m.w_out_loaded[1], 16)
                sp.dma_start(ln_g[:], m.vec["ln1_g"].broadcast_to([P, D])).then_inc(ln_loaded, 16)
                sp.dma_start(ln_b[:], m.vec["ln1_b"].broadcast_to([P, D])).then_inc(ln_loaded, 16)
                sp.dma_start(router_w[:], m.router_w.rearrange("(k p) n -> p k n", p=P)).then_inc(loaded, 16)
                sp.dma_start(router_b[:], m.vec["router_bias"].broadcast_to([P, E])).then_inc(loaded, 16)
                sp.dma_start(sh_w[:, 0], m.sh_gate.rearrange("(k p) n -> p k n", p=P)).then_inc(sh_loaded, 16)
                sp.dma_start(sh_w[:, 1], m.sh_up.rearrange("(k p) n -> p k n", p=P)).then_inc(sh_loaded, 16)
                sp.dma_start(sh_d[:], m.sh_down.rearrange("(k p) n -> p k n", p=P)).then_inc(sh_loaded, 16)
                for i in range(2, NT):
                    t0, n = TOK_TILES[i]
                    sp.wait_ge(x_used, i - 1)
                    src = m.x_prompt[t0:t0 + n, :] if i < TM else m.x_sample
                    sp.dma_start(x_rows[0:n, i % 2, :], src).then_inc(x_loaded[i % 2], 16)
                for job in range(2):
                    load_expert(sp, m, job, job)
                for i, (t0, n) in enumerate(TOK_TILES):
                    sp.wait_ge(x1_ready, i + 1)
                    sp.dma_start(m.scr_x1[t0:t0 + n, :], x1[0:n, i, :]).then_inc(x1_stored, 16)
                sp.dma_start(m.scr_f[TT:TT + CAP, :], x1[0:CAP, 0, :]).then_inc(x1_stored, 16)
                sp.dma_start(m.scr_x1[TT:TT + CAP, :], x1[0:CAP, 0, :]).then_inc(x1_stored, 16)
                for job in range(2, NB):
                    load_expert(sp, m, job, job)
                for i, (t0, n) in enumerate(TOK_TILES):
                    sp.wait_ge(f_taken, 2 * (i + 1))
                    sp.dma_start(m.scr_f[t0:t0 + n, :], f0[0:n, i % 2, :]).then_inc(f_stored[i % 2], 16)
                sp.wait_ge(x1_stored, 16 * (NT + 2))
                sp.wait_ge(f_stored[0], 16 * 3)
                sp.wait_ge(f_stored[1], 16 * 2)

            @block.tensor
            def _(pe):
                def turn(i):
                    t0, n = TOK_TILES[i]
                    pe.wait_ge(x1_ready, i + 1)
                    for half in range(2):
                        g = 2 * i + half
                        if g >= 2:
                            pe.wait_ge(x1_t_ready, g - 1)
                        for k in range(4):
                            d0 = (4 * half + k) * P
                            last = nc.tensor.transpose(pt[:, half, k * P:k * P + n], x1[0:n, i, d0:d0 + P], m.ident[0:n, 0:n])
                        last.then_inc(x1_turned, 1)
                for i, (t0, n) in enumerate(TOK_TILES):
                    if i >= 2:
                        pe.wait_ge(mixed_taken, i - 1)
                    for c in range(2):
                        if i == 0:
                            pe.wait_ge(m.w_out_loaded[c], 16)
                        for k in range(KD):
                            lhs = m.conv[:, k, t0:t0 + n] if k < CT else m.o_t[:, k - CT, t0:t0 + n]
                            last = nc.tensor.matmul(ph[0:n, i % 2, c * 512:(c + 1) * 512], lhs, w_out[c][:, k, :],
                                                    start=(k == 0), stop=(k == KD - 1))
                    last.then_inc(mixed, 1)
                    if i >= 1:
                        turn(i - 1)
                turn(NT - 1)
                pe.wait_ge(x1_t_ready, 2 * NT)
                pe.wait_ge(loaded, 16 * 2)
                for i, (t0, n) in enumerate(TOK_TILES):
                    for k in range(KD):
                        last = nc.tensor.matmul(plog[0:n, i, :], x1_t[:, k, t0:t0 + n], router_w[:, k, :], start=(k == 0), stop=(k == KD - 1))
                last.then_inc(logits_done, 1)
                pe.wait_ge(mixed_taken, NT)
                pe.wait_ge(sh_loaded, 16 * 3)
                for j in range(2):
                    if j >= 1:
                        pe.wait_ge(sh_h_ready, j)
                    for part in range(2):
                        for k in range(KD):
                            for c0, c1 in ((0, T), (T, TT)):
                                last = nc.tensor.matmul(ph[:, part, c0:c1], sh_w[:, part, k, j * P:(j + 1) * P], x1_t[:, k, c0:c1],
                                                        start=(k == 0), stop=(k == KD - 1))
                        last.then_inc(sh_done, 1)
                pe.wait_ge(sh_h_ready, 2)
                pe.wait_ge(hits_ready, 1)
                pe.wait_ge(routing_consts, 2)
                for i in range(NT):
                    for j in range(i + 1):
                        last = nc.tensor.matmul(ppos[:, i, :], before[:] if j == i else m.ones[:], hit[:, j, :], start=(j == 0), stop=(j == i))
                for j in range(NT):
                    last = nc.tensor.matmul(ppos[:, NT, :], m.ones[:], hit[:, j, :], start=(j == 0), stop=(j == NT - 1))
                last.then_inc(positions_done, 1)
                for i, (t0, n) in enumerate(TOK_TILES):
                    if i >= 2:
                        pe.wait_ge(f_taken, 2 * (i - 1))
                    for c in range(2):
                        for j in range(2):
                            last = nc.tensor.matmul(ph[0:n, i % 2, c * 512:(c + 1) * 512], sh_h[:, j, t0:t0 + n], sh_d[:, j, c * 512:(c + 1) * 512],
                                                    start=(j == 0), stop=(j == 1))
                    last.then_inc(f_done, 1)

            @block.scalar
            def _(act):
                for i, (t0, n) in enumerate(TOK_TILES):
                    act.wait_ge(var_ready, i + 1)
                    nc.scalar.activation(aggr[0:n, 2:3], aggr[0:n, 1:2], ACT.Sqrt, bias=m.eps_ln[0:n, :]).then_inc(rooted, 1)
                    for half in range(2):
                        act.wait_ge(x1_turned, 2 * i + half + 1)
                        nc.scalar.copy(x1_t[:, 4 * half:4 * half + 4, t0:t0 + n],
                                       pt[:, half, :].rearrange("p (k t) -> p k t", k=4)[:, :, 0:n]).then_inc(x1_t_ready, 1)
                act.wait_ge(routing_consts, 1)
                act.wait_ge(logits_done, 1)
                nc.scalar.activation(scores[:, 0:TM, :], plog[:, 0:TM, :], ACT.Sigmoid)
                nc.scalar.activation(scores[0:B, TM, :], plog[0:B, TM, :], ACT.Sigmoid).then_inc(scores_ready, 1)
                for j in range(2):
                    act.wait_ge(sh_done, 2 * j + 1)
                    if j >= 1:
                        act.wait_ge(sh_h_ready, j)
                    nc.scalar.activation(sh_sig[:], ph[:, 0, 0:TT], ACT.Sigmoid).then_inc(sh_sig_ready, 1)

            @block.gpsimd
            def _(pool):
                nc.gpsimd.memset(scores[:, TM, :], 0.0).then_inc(routing_consts, 1)
                ch = Chain(pool, m.pool_step, m.pool_count)
                nc.gpsimd.memset(before[:], 1.0)
                ch.link(nc.gpsimd.memset(first[:], 1.0))
                nc.gpsimd.affine_select(out=before[:], in_=before[:], compare_op=ALU.is_gt, fill=0.0, base=0,
                                        pattern=[[1, P]], channel_multiplier=-1)
                nc.gpsimd.affine_select(out=first[:], in_=first[:], compare_op=ALU.is_gt, fill=0.0, base=0,
                                        pattern=[[1, G], [-1, G]], channel_multiplier=0).then_inc(routing_consts, 1)

            @block.vector
            def _(dve):
                ch = Chain(dve, m.vector_step, m.vector_count)

                def layer_norm(i, n):
                    r = x_rows[0:n, i % 2, :]
                    dve.wait_ge(x_loaded[i % 2], 16 * (i // 2 + 1))
                    dve.wait_ge(mixed, i + 1)
                    for c in range(2):
                        cs = slice(c * 512, (c + 1) * 512)
                        last = nc.vector.scalar_tensor_tensor(x1[0:n, i, cs], r[:, cs], ALPHA, ph[0:n, i % 2, cs], ALU.mult, ALU.add)
                    last.then_inc(mixed_taken, 1)
                    dve.wait_ge(mixed_taken, i + 1)
                    for c in range(2):
                        last = nc.vector.bn_stats(stats[0:n, c, :], x1[0:n, i, c * 512:(c + 1) * 512])
                    last.then_inc(x_used, 1)
                    dve.wait_ge(x_used, i + 1)
                    nc.vector.bn_aggr(aggr[0:n, 0:2], stats[0:n, :, :]).then_inc(var_ready, 1)
                    dve.wait_ge(var_ready, i + 1)
                    dve.wait_ge(rooted, i + 1)
                    ch.link(nc.vector.reciprocal(aggr[0:n, 3:4], aggr[0:n, 2:3]))
                    ch.link(nc.vector.tensor_scalar(x1[0:n, i, :], x1[0:n, i, :], aggr[0:n, 0:1], aggr[0:n, 3:4], ALU.subtract, ALU.mult))
                    ch.link(nc.vector.tensor_tensor(x1[0:n, i, :], x1[0:n, i, :], ln_g[0:n, :], ALU.mult))
                    nc.vector.tensor_tensor(x1[0:n, i, :], x1[0:n, i, :], ln_b[0:n, :], ALU.add).then_inc(x1_ready, 1)

                dve.wait_ge(ln_loaded, 32)
                for i, (_, n) in enumerate(TOK_TILES):
                    layer_norm(i, n)
                dve.wait_ge(scores_ready, 1)
                dve.wait_ge(routing_consts, 2)
                dve.wait_ge(loaded, 16 * 2)
                ch.link(nc.vector.tensor_tensor(sel[:], scores[:], router_b[:].unsqueeze(1).broadcast_to([P, NT, E]), ALU.add))
                sel_g = sel[:].rearrange("p i (g e) -> p (i g) e", g=G)
                for g in range(NT * G):
                    last = nc.vector.max(top[:, g, :], sel_g[:, g, :])
                ch.link(last)
                grp_f = grp[:].rearrange("p i g -> p (i g)")
                ch.link(nc.vector.tensor_tensor(grp_f, top[:, :, 0], top[:, :, 1], ALU.add))
                me = grp[:].unsqueeze(3).broadcast_to([P, NT, G, G])
                other = grp[:].unsqueeze(2).broadcast_to([P, NT, G, G])
                nc.vector.tensor_tensor(gt[:], other, me, ALU.is_gt)
                ch.link(nc.vector.tensor_tensor(eq[:], other, me, ALU.is_equal))
                ch.link(nc.vector.tensor_tensor(eq[:], eq[:], first[:].unsqueeze(1).broadcast_to([P, NT, G, G]), ALU.mult))
                ch.link(nc.vector.tensor_tensor(gt[:], gt[:], eq[:], ALU.add))
                ch.link(nc.vector.tensor_reduce(grp[:], gt[:], AX, ALU.add))
                ch.link(nc.vector.tensor_scalar(keep[:], grp[:], float(KG), None, ALU.is_lt))
                keep_f = keep[:].rearrange("p i g -> p (i g)").unsqueeze(2).broadcast_to([P, NT * G, E // G])
                ch.link(nc.vector.tensor_tensor(sel_g, sel_g, keep_f, ALU.mult))
                ch.link(nc.vector.tensor_scalar(grp[:], keep[:], 1.0, BIG, ALU.subtract, ALU.mult))
                ch.link(nc.vector.tensor_tensor(sel_g, sel_g, grp_f.unsqueeze(2).broadcast_to([P, NT * G, E // G]), ALU.add))
                for i in range(NT):
                    last = nc.vector.max(top[:, i, :], sel[:, i, :])
                ch.link(last)
                for i in range(NT):
                    last = nc.vector.match_replace(hit[:, i, :], top[:, i, :], sel[:, i, :], GONE)
                ch.link(last)
                ch.link(nc.vector.tensor_scalar(hit[:], hit[:], GONE / 2, None, ALU.is_lt))
                nc.vector.tensor_tensor(hit[:], hit[:], m.is_token[:].unsqueeze(2).broadcast_to([P, NT, E]), ALU.mult).then_inc(hits_ready, 1)
                dve.wait_ge(hits_ready, 1)
                ch.link(nc.vector.tensor_tensor(scores[:], scores[:], hit[:], ALU.mult))
                ch.link(nc.vector.tensor_reduce(gsum[:], scores[:], AX, ALU.add))
                ch.link(nc.vector.tensor_scalar(gsum[:], gsum[:], 1e-20, None, ALU.add))
                ch.link(nc.vector.reciprocal(gsum[:], gsum[:]))
                by_tile = lambda ap: ap.rearrange("p i e -> p e i")
                ch.link(nc.vector.tensor_tensor(scores[:], scores[:], gsum[:].unsqueeze(2).broadcast_to([P, NT, E]), ALU.mult))
                ch.link(nc.vector.tensor_scalar(scores[:], scores[:], ROUTED_SCALE, None, ALU.mult))
                for part in range(3):
                    col = m.table[:, :, :, 3 + part]
                    ch.link(nc.vector.tensor_copy(col, by_tile(scores[:])))
                    if part < 2:
                        ch.link(nc.vector.tensor_tensor(scores[:], scores[:], col.rearrange("p e i -> p i e"), ALU.subtract))
                nc.vector.tensor_copy(m.table[:, :, :, 0], m.tile_index[:].unsqueeze(1).broadcast_to([P, E, NT]))
                nc.vector.tensor_copy(m.table[:, :, :, 1], m.partition_index[:].unsqueeze(1).broadcast_to([P, E, NT]))
                ch.link(nc.vector.memset(m.table[:, :, :, 2], 1.0))
                for j in range(2):
                    dve.wait_ge(sh_sig_ready, j + 1)
                    ch.link(nc.vector.tensor_tensor(sh_sig[:], sh_sig[:], ph[:, 0, 0:TT], ALU.mult))
                    dve.wait_ge(sh_done, 2 * j + 2)
                    nc.vector.tensor_tensor(sh_h[:, j, :], sh_sig[:], ph[:, 1, 0:TT], ALU.mult).then_inc(sh_h_ready, 1)
                dve.wait_ge(positions_done, 1)
                ch.link(nc.vector.scalar_tensor_tensor(sel[:], ppos[:, 0:NT, :], 1.0, hit[:], ALU.add, ALU.mult))
                ch.link(nc.vector.tensor_scalar(m.position[:], by_tile(sel[:]), 1.0, None, ALU.subtract))
                nc.vector.memset(cnt[:, 1:4, :], 0.0)
                ch.link(nc.vector.tensor_copy(cnt[:, 0, :], ppos[:, NT, :]))
                for b in range(1, m.MAX_JOBS):
                    ch.link(nc.vector.tensor_scalar(cnt[:, 2, :], cnt[:, 0, :], float(b * CAP), None, ALU.is_gt))
                    ch.link(nc.vector.tensor_tensor(cnt[:, 1, :], cnt[:, 1, :], cnt[:, 2, :], ALU.add))
                ch.link(nc.vector.tensor_tensor_scan(cnt[:, 2, :], m.ones[:, 0:E], cnt[:, 1, :], 0.0, ALU.mult, ALU.add))
                jk = m.job_index[:].unsqueeze(2).broadcast_to([P, m.EXTRA, E])
                ch.link(nc.vector.tensor_tensor(jobs3[:], cnt[:, 2, :].unsqueeze(1).broadcast_to([P, m.EXTRA, E]), jk, ALU.is_le))
                ch.link(nc.vector.tensor_reduce(m.job_expert[:], jobs3[:], AX, ALU.add))
                ch.link(nc.vector.tensor_tensor(jobs3[:], jobs3[:], cnt[:, 1, :].unsqueeze(1).broadcast_to([P, m.EXTRA, E]), ALU.mult))
                ch.link(nc.vector.tensor_reduce(m.job_base[:], jobs3[:], AX, ALU.add))
                ch.link(nc.vector.tensor_tensor(m.job_base[:], m.job_index[:], m.job_base[:], ALU.subtract))
                ch.link(nc.vector.tensor_scalar(m.job_base[:], m.job_base[:], 1.0, float(CAP), ALU.add, ALU.mult))
                nc.vector.tensor_copy(m.job_table[:, 1:], m.job_expert[0:1, :])
                ch.link(nc.vector.tensor_copy(m.job_table[:, 0:1], cnt[0:1, 2, E - 1:E]))
                for i, (t0, n) in enumerate(TOK_TILES):
                    dve.wait_ge(f_done, i + 1)
                    if i >= 2:
                        dve.wait_ge(f_stored[i % 2], 16 * (i // 2))
                    for c in range(2):
                        cs = slice(c * 512, (c + 1) * 512)
                        nc.vector.scalar_tensor_tensor(f0[0:n, i % 2, cs], x1[0:n, i, cs], ALPHA, ph[0:n, i % 2, cs],
                                                       ALU.mult, ALU.add).then_inc(f_taken, 1)


def load_expert(sp, m, q, s):
    pick = lambda w: w[bass.ds(q, 1)].rearrange("o p n -> p (o n)")
    sp.dma_start(m.expert_gate[s][:].rearrange("p k f -> p (k f)"), pick(m.exp_gate)).then_inc(m.gate_loaded[s], 16)
    sp.dma_start(m.expert_up[s][:].rearrange("p k f -> p (k f)"), pick(m.exp_up)).then_inc(m.up_loaded[s], 16)
    sp.dma_start(m.expert_down[s][:], m.exp_down[bass.ds(q, 1)].rearrange("o p j d -> p (o j) d")).then_inc(m.down_loaded[s], 16)


def experts(nc, m, ctx_out):
    STEPS = 2 * NB
    with ExitStack() as ctx:
        def sb(name, shape, dt=F32):
            return ctx.enter_context(nc.sbuf_tensor(name, shape, dt))

        def ps(name, shape, dt=F32):
            return ctx.enter_context(nc.psum_tensor(name, shape, dt))

        def sem(name):
            return ctx_out.enter_context(nc.semaphore(name))

        member = sb("member", [P, 2, NT, CAP], BF16)
        entry = sb("entry", [CAP, STEPS, 6])
        row = sb("row", [CAP, STEPS], U32)
        spare = sb("spare", [CAP, STEPS])
        token = sb("token", [CAP, STEPS])
        weight = sb("weight", [CAP, STEPS])
        x_list = sb("x_list", [CAP, NB, D])
        x_list_t = sb("x_list_t", [P, 2, KD, CAP])
        sig = sb("sig", [P, 2, 2, CAP])
        hid = sb("hid", [P, 2, 2, CAP])
        y_list = sb("y_list", [CAP, 2, D])
        moved = sb("moved", [P, NT])
        pl = ps("pl", [P, 2, 512])
        px = ps("px", [P, 2, 512])
        pgu = ps("pgu", [P, 2, 512])
        pyl = ps("pyl", [P, 2, 512])

        member_ready = sem("member_ready")
        list_done = sem("list_done")
        entry_ready = sem("entry_ready")
        rows_ready = sem("rows_ready")
        gathered = [sem(f"gathered{i}") for i in range(NB)]
        added = [sem(f"added{i}") for i in range(2)]
        x_turned = sem("x_list_turned")
        x_ready = sem("x_list_ready")
        gu_done = sem("gu_done")
        sig_ready = sem("sig_ready")
        hid_ready = sem("hid_ready")
        y_done = sem("y_list_done")
        y_act = sem("y_act_ready")
        y_dve = sem("y_dve_ready")
        silu_ready = sem("silu_ready")
        weight_ready = sem("weight_ready")
        waits_over = sem("waits_over")
        LOOPS = E // STEPS - 1
        AHEAD = NB
        KA = 512 // CAP if 512 // CAP < KD else KD // 2

        class Job:

            def __init__(self, turn, s):
                self.q = STEPS * turn + s
                self.s = s % NB
                self.l = s % STEPS
                self.pair = STEPS // 2 * turn + s // 2
                self.before = STEPS // 2 * turn + (s + 1) // 2
                self.turn = STEPS // NB * turn + s // NB

            def has_before(self, n):
                return not isinstance(self.q, int) or self.q >= n

        def build_member(dve, job):
            q, s = job.q, job.s
            if job.has_before(2):
                dve.wait_ge(list_done, q - 1)
            src = m.position[:, bass.ds(q, 1), :].rearrange("p o i -> p (o i)")
            nc.vector.tensor_tensor(member[:, s % 2], m.slot_index[:].unsqueeze(1).broadcast_to([P, NT, CAP]),
                                    src.unsqueeze(2).broadcast_to([P, NT, CAP]), ALU.is_equal).then_inc(member_ready, 1)

        def make_list(pe, job):
            q, s = job.q, job.s
            pe.wait_ge(member_ready, q + 1)
            if job.has_before(2):
                pe.wait_ge(entry_ready, q - 1)
            for i in range(NT):
                last = nc.tensor.matmul(pl[0:CAP, s % 2, 0:6], member[:, s % 2, i, :],
                                        m.table[:, bass.ds(q, 1), i, :].rearrange("p o c -> p (o c)"),
                                        start=(i == 0), stop=(i == NT - 1))
            last.then_inc(list_done, 1)

        def read_list(dve, job):
            q, s = job.q, job.l
            dve.wait_ge(list_done, q + 1)
            if job.has_before(STEPS):
                dve.wait_ge(added[s % 2], 16 * (job.pair - STEPS // 2 + 1))
            nc.vector.tensor_copy(entry[:, s, :], pl[0:CAP, s % 2, 0:6]).then_inc(entry_ready, 1)
            dve.wait_ge(entry_ready, q + 1)
            nc.vector.tensor_scalar(spare[:, s:s + 1], entry[:, s, 2:3], m.minus_spare[0:CAP, :], m.spare_row[0:CAP, :], ALU.mult, ALU.add)
            nc.vector.scalar_tensor_tensor(token[:, s:s + 1], entry[:, s, 0:1], float(P), entry[:, s, 1:2],
                                           ALU.mult, ALU.add).then_inc(rows_ready, 1)
            dve.wait_ge(rows_ready, 2 * q + 1)
            nc.vector.tensor_tensor(row[:, s:s + 1], spare[:, s:s + 1], token[:, s:s + 1], ALU.add).then_inc(rows_ready, 1)
            nc.vector.tensor_reduce(weight[:, s:s + 1], entry[:, s, 3:6], AX, ALU.add).then_inc(weight_ready, 1)

        def gather(pool, job):
            q, s = job.q, job.s
            pool.wait_ge(rows_ready, 2 * q + 2)
            if job.has_before(NB):
                pool.wait_ge(x_turned, 2 * (q - NB + 1))
            pool.sem_inc(waits_over)
            nc.gpsimd.indirect_dma_start(x_list[:, s, :], None, m.scr_x1,
                                         bass.IndirectOffsetOnAxis(ap=row[:, job.l:job.l + 1], axis=0)).then_inc(gathered[s], 16)

        def turn_list(pe, job):
            q, s = job.q, job.s
            pe.wait_ge(gathered[s], 16 * job.turn + 16)
            if job.has_before(1):
                pe.wait_ge(x_ready, 2 * q)
            v = x_list[:, s, :].rearrange("t (p k) -> t k p", k=KD)
            for k in range(KD):
                bank, at = (0, k) if k < KA else (1, k - KA)
                last = nc.tensor.transpose(px[:, bank, at * CAP:(at + 1) * CAP], v[:, k, :], m.ident[0:CAP, 0:CAP])
                if k in (KA - 1, KD - 1):
                    last.then_inc(x_turned, 1)

        def copy_turned(act, job):
            q, s = job.q, job.s
            for bank, (k0, k1) in enumerate(((0, KA), (KA, KD))):
                act.wait_ge(x_turned, 2 * q + bank + 1)
                if job.has_before(2) and bank == 0:
                    act.wait_ge(gu_done, q - 1)
                nc.scalar.copy(x_list_t[:, s % 2, k0:k1, :],
                               px[:, bank, 0:(k1 - k0) * CAP].rearrange("p (k t) -> p k t", t=CAP)).then_inc(x_ready, 1)

        def gate_up(pe, job):
            q, s = job.q, job.s
            pe.wait_ge(x_ready, 2 * q + 2)
            if job.has_before(2):
                pe.wait_ge(hid_ready, q - 1)
            for part, w in enumerate((m.expert_gate, m.expert_up)):
                pe.wait_ge((m.gate_loaded, m.up_loaded)[part][s], 16 * job.turn + 16)
                for j in range(2):
                    for k in range(KD):
                        last = nc.tensor.matmul(pgu[:, s % 2, (2 * part + j) * CAP:(2 * part + j + 1) * CAP],
                                                w[s][:, k, j * P:(j + 1) * P], x_list_t[:, s % 2, k, :],
                                                start=(k == 0), stop=(k == KD - 1))
            last.then_inc(gu_done, 1)

        def gate_act(act, job):
            q, s = job.q, job.s
            act.wait_ge(gu_done, q + 1)
            nc.scalar.activation(sig[:, s % 2].rearrange("p j t -> p (j t)"), pgu[:, s % 2, 0:2 * CAP], ACT.Sigmoid).then_inc(sig_ready, 1)

        def gate_mul(dve, job):
            q, s = job.q, job.s
            g = sig[:, s % 2].rearrange("p j t -> p (j t)")
            h = hid[:, s % 2].rearrange("p j t -> p (j t)")
            dve.wait_ge(sig_ready, q + 1)
            nc.vector.tensor_tensor(g, g, pgu[:, s % 2, 0:2 * CAP], ALU.mult).then_inc(silu_ready, 1)
            dve.wait_ge(silu_ready, q + 1)
            nc.vector.tensor_tensor(h, g, pgu[:, s % 2, 2 * CAP:4 * CAP], ALU.mult).then_inc(hid_ready, 1)

        def down(pe, job):
            q, s = job.q, job.s
            pe.wait_ge(hid_ready, q + 1)
            pe.wait_ge(m.down_loaded[s], 16 * job.turn + 16)
            for c in range(2):
                if job.has_before(1):
                    pe.wait_ge((y_act, y_dve)[c], q)
                for j in range(2):
                    last = nc.tensor.matmul(pyl[0:CAP, c, :], hid[:, s % 2, j, :], m.expert_down[s][:, j, c * 512:(c + 1) * 512],
                                            start=(j == 0), stop=(j == 1))
                last.then_inc(y_done, 1)

        def weigh_act(act, job):
            q, s = job.q, job.s
            act.wait_ge(y_done, 2 * q + 1)
            act.wait_ge(weight_ready, q + 1)
            if job.has_before(2):
                act.wait_ge(added[s % 2], 16 * job.pair)
            nc.scalar.activation(y_list[:, s % 2, 0:512], pyl[0:CAP, 0, :], ACT.Copy, scale=weight[:, job.l:job.l + 1]).then_inc(y_act, 1)

        def weigh_dve(dve, job):
            q, s = job.q, job.s
            dve.wait_ge(y_done, 2 * q + 2)
            dve.wait_ge(weight_ready, q + 1)
            if job.has_before(2):
                dve.wait_ge(added[s % 2], 16 * job.pair)
            nc.vector.tensor_scalar(y_list[:, s % 2, 512:1024], pyl[0:CAP, 1, :], weight[:, job.l:job.l + 1], None, ALU.mult).then_inc(y_dve, 1)

        def add_rows(pool, job):
            q, s = job.q, job.s
            pool.wait_ge(y_act, q + 1)
            pool.wait_ge(y_dve, q + 1)
            if job.has_before(1):
                pool.wait_ge(added[(s + 1) % 2], 16 * job.before)
            pool.sem_inc(waits_over)
            nc.gpsimd.indirect_dma_start(m.scr_f, bass.IndirectOffsetOnAxis(ap=row[:, job.l:job.l + 1], axis=0), y_list[:, s % 2, :], None,
                                         compute_op=ALU.add).then_inc(added[s % 2], 16)

        def each(eng, step):
            for s in range(STEPS):
                step(0, s, False)
            with eng.Fori(1, LOOPS) as turn:
                for s in range(STEPS):
                    step(turn, s, False)
            for s in range(STEPS):
                step(LOOPS, s, True)

        with nc.Block() as block:
            @block.sync
            def _(sp):
                with sp.Fori(1, E // NB) as turn:
                    for s in range(NB):
                        sp.wait_ge(y_done, 2 * (NB * turn + s - NB + 1))
                        load_expert(sp, m, NB * turn + s, s)

            @block.tensor
            def _(pe):
                def step(turn, s, last):
                    if not last or s + AHEAD < STEPS:
                        make_list(pe, Job(turn, s + AHEAD))
                    if not last or s + 1 < STEPS:
                        gate_up(pe, Job(turn, s + 1))
                    if not last or s + 2 < STEPS:
                        turn_list(pe, Job(turn, s + 2))
                    down(pe, Job(turn, s))

                for s in range(AHEAD):
                    make_list(pe, Job(0, s))
                for s in range(2):
                    turn_list(pe, Job(0, s))
                gate_up(pe, Job(0, 0))
                each(pe, step)

            @block.vector
            def _(dve):
                def step(turn, s, last):
                    if not last or s + AHEAD < STEPS:
                        read_list(dve, Job(turn, s + AHEAD))
                    if not last or s + 1 < STEPS:
                        gate_mul(dve, Job(turn, s + 1))
                    if not last or s + AHEAD + 1 < STEPS:
                        build_member(dve, Job(turn, s + AHEAD + 1))
                    weigh_dve(dve, Job(turn, s))

                build_member(dve, Job(0, 0))
                for s in range(AHEAD):
                    build_member(dve, Job(0, s + 1))
                    read_list(dve, Job(0, s))
                gate_mul(dve, Job(0, 0))
                each(dve, step)

            @block.scalar
            def _(act):
                def step(turn, s, last):
                    if not last or s + 1 < STEPS:
                        gate_act(act, Job(turn, s + 1))
                    if not last or s + 2 < STEPS:
                        copy_turned(act, Job(turn, s + 2))
                    weigh_act(act, Job(turn, s))

                for s in range(2):
                    copy_turned(act, Job(0, s))
                gate_act(act, Job(0, 0))
                each(act, step)

            @block.gpsimd
            def _(pool):
                def step(turn, s, last):
                    if not last or s + AHEAD < STEPS:
                        gather(pool, Job(turn, s + AHEAD))
                    add_rows(pool, Job(turn, s))

                for s in range(AHEAD):
                    gather(pool, Job(0, s))
                each(pool, step)
                for b in range(2):
                    pool.wait_ge(added[b], 16 * (E // 2))


def overflow(nc, m, ctx_out):
    with ExitStack() as ctx:
        def sb(name, shape, dt=F32):
            return ctx.enter_context(nc.sbuf_tensor(name, shape, dt))

        def ps(name, shape, dt=F32):
            return ctx.enter_context(nc.psum_tensor(name, shape, dt))

        def sem(name):
            return ctx_out.enter_context(nc.semaphore(name))

        w_gu = sb("w_gu", [P, 2, KD, FE])
        w_down = sb("w_down_o", [P, 2, D])
        place = sb("place", [P, NT])
        member = sb("member_o", [P, NT, CAP], BF16)
        entry = sb("entry_o", [CAP, 6])
        row = sb("row_o", [CAP, 1], U32)
        spare = sb("spare_o", [CAP, 1])
        token = sb("token_o", [CAP, 1])
        weight = sb("weight_o", [CAP, 1])
        x_list = sb("x_list_o", [CAP, D])
        x_list_t = sb("x_list_t_o", [P, KD, CAP])
        sig = sb("sig_o", [P, 2 * CAP])
        hid = sb("hid_o", [P, 2, CAP])
        y_list = sb("y_list_o", [CAP, D])
        pl = ps("pl_o", [P, 512])
        px = ps("px_o", [P, 2, 512])
        pgu = ps("pgu_o", [P, 512])
        pyl = ps("pyl_o", [P, 2, 512])
        KA = 512 // CAP if 512 // CAP < KD else KD // 2
        weights_loaded = sem("o_weights_loaded")
        member_ready = sem("o_member_ready")
        list_done = sem("o_list_done")
        rows_ready = sem("o_rows_ready")
        gathered = sem("o_gathered")
        x_turned = sem("o_x_turned")
        x_ready = sem("o_x_ready")
        gu_done = sem("o_gu_done")
        sig_ready = sem("o_sig_ready")
        hid_ready = sem("o_hid_ready")
        y_done = sem("o_y_done")
        y_ready = sem("o_y_ready")
        added = sem("o_added")
        waits_over = sem("o_waits_over")

        def each_job(eng, body, expert=True):
            n = eng.value_load(m.job_table[0:1, 0:1], min_val=0, max_val=m.EXTRA)
            with eng.If(n > 0):
                with eng.Fori(0, m.EXTRA) as k:
                    with eng.If(k < n):
                        ex = eng.value_load(m.job_table[0:1, bass.ds(k + 1, 1)], min_val=0, max_val=E - 1) if expert else None
                        body(k, ex)

        with nc.Block() as block:
            @block.sync
            def _(sp):
                def body(k, ex):
                    sp.wait_ge(y_done, k)
                    pick = lambda w: w[bass.ds(ex, 1)].rearrange("o p n -> p (o n)")
                    sp.dma_start(w_gu[:, 0].rearrange("p k f -> p (k f)"), pick(m.exp_gate)).then_inc(weights_loaded, 16)
                    sp.dma_start(w_gu[:, 1].rearrange("p k f -> p (k f)"), pick(m.exp_up)).then_inc(weights_loaded, 16)
                    sp.dma_start(w_down[:], m.exp_down[bass.ds(ex, 1)].rearrange("o p j d -> p (o j) d")).then_inc(weights_loaded, 16)
                each_job(sp, body)

            @block.vector
            def _(dve):
                def body(k, ex):
                    dve.wait_ge(added, 16 * k)
                    nc.vector.tensor_scalar(place[:], m.position[:, bass.ds(ex, 1), :].rearrange("p o i -> p (o i)"),
                                            m.job_base[:, bass.ds(k, 1)], None, ALU.subtract).then_inc(member_ready, 1)
                    dve.wait_ge(member_ready, 2 * k + 1)
                    nc.vector.tensor_tensor(member[:], m.slot_index[:].unsqueeze(1).broadcast_to([P, NT, CAP]),
                                            place[:].unsqueeze(2).broadcast_to([P, NT, CAP]), ALU.is_equal).then_inc(member_ready, 1)
                    dve.wait_ge(list_done, k + 1)
                    nc.vector.tensor_copy(entry[:], pl[0:CAP, 0:6]).then_inc(rows_ready, 1)
                    dve.wait_ge(rows_ready, 4 * k + 1)
                    nc.vector.tensor_reduce(weight[:], entry[:, 3:6], AX, ALU.add)
                    nc.vector.tensor_scalar(spare[:], entry[:, 2:3], m.minus_spare[0:CAP, :], m.spare_row[0:CAP, :],
                                            ALU.mult, ALU.add).then_inc(rows_ready, 1)
                    nc.vector.scalar_tensor_tensor(token[:], entry[:, 0:1], float(P), entry[:, 1:2], ALU.mult, ALU.add).then_inc(rows_ready, 1)
                    dve.wait_ge(rows_ready, 4 * k + 3)
                    nc.vector.tensor_tensor(row[:], spare[:], token[:], ALU.add).then_inc(rows_ready, 1)
                    dve.wait_ge(sig_ready, k + 1)
                    nc.vector.tensor_tensor(sig[:], sig[:], pgu[:, 0:2 * CAP], ALU.mult).then_inc(hid_ready, 1)
                    dve.wait_ge(hid_ready, 2 * k + 1)
                    nc.vector.tensor_tensor(hid[:].rearrange("p j t -> p (j t)"), sig[:], pgu[:, 2 * CAP:4 * CAP], ALU.mult).then_inc(hid_ready, 1)
                    dve.wait_ge(y_done, k + 1)
                    for c in range(2):
                        last = nc.vector.tensor_scalar(y_list[:, c * 512:(c + 1) * 512], pyl[0:CAP, c, :], weight[:], None, ALU.mult)
                    last.then_inc(y_ready, 1)
                each_job(dve, body)

            @block.tensor
            def _(pe):
                def body(k, ex):
                    pe.wait_ge(member_ready, 2 * k + 2)
                    for i in range(NT):
                        last = nc.tensor.matmul(pl[0:CAP, 0:6], member[:, i, :], m.table[:, bass.ds(ex, 1), i, :].rearrange("p o c -> p (o c)"),
                                                start=(i == 0), stop=(i == NT - 1))
                    last.then_inc(list_done, 1)
                    pe.wait_ge(gathered, 16 * k + 16)
                    v = x_list[:].rearrange("t (p k) -> t k p", k=KD)
                    for kk in range(KD):
                        bank, at = (0, kk) if kk < KA else (1, kk - KA)
                        last = nc.tensor.transpose(px[:, bank, at * CAP:(at + 1) * CAP], v[:, kk, :], m.ident[0:CAP, 0:CAP])
                    last.then_inc(x_turned, 1)
                    pe.wait_ge(x_ready, k + 1)
                    pe.wait_ge(weights_loaded, 48 * k + 48)
                    for part in range(2):
                        for j in range(2):
                            for kk in range(KD):
                                last = nc.tensor.matmul(pgu[:, (2 * part + j) * CAP:(2 * part + j + 1) * CAP],
                                                        w_gu[:, part, kk, j * P:(j + 1) * P], x_list_t[:, kk, :],
                                                        start=(kk == 0), stop=(kk == KD - 1))
                    last.then_inc(gu_done, 1)
                    pe.wait_ge(hid_ready, 2 * k + 2)
                    for c in range(2):
                        for j in range(2):
                            last = nc.tensor.matmul(pyl[0:CAP, c, :], hid[:, j, :], w_down[:, j, c * 512:(c + 1) * 512],
                                                    start=(j == 0), stop=(j == 1))
                    last.then_inc(y_done, 1)
                each_job(pe, body)

            @block.scalar
            def _(act):
                def body(k, ex):
                    act.wait_ge(x_turned, k + 1)
                    for bank, (k0, k1) in enumerate(((0, KA), (KA, KD))):
                        last = nc.scalar.copy(x_list_t[:, k0:k1, :], px[:, bank, 0:(k1 - k0) * CAP].rearrange("p (k t) -> p k t", t=CAP))
                    last.then_inc(x_ready, 1)
                    act.wait_ge(gu_done, k + 1)
                    nc.scalar.activation(sig[:], pgu[:, 0:2 * CAP], ACT.Sigmoid).then_inc(sig_ready, 1)
                each_job(act, body, expert=False)

            @block.gpsimd
            def _(pool):
                def body(k, ex):
                    pool.wait_ge(rows_ready, 4 * k + 4)
                    pool.sem_inc(waits_over)
                    nc.gpsimd.indirect_dma_start(x_list[:], None, m.scr_x1,
                                                 bass.IndirectOffsetOnAxis(ap=row[:], axis=0)).then_inc(gathered, 16)
                    pool.wait_ge(y_ready, k + 1)
                    pool.sem_inc(waits_over)
                    nc.gpsimd.indirect_dma_start(m.scr_f, bass.IndirectOffsetOnAxis(ap=row[:], axis=0), y_list[:], None,
                                                 compute_op=ALU.add).then_inc(added, 16)
                    pool.wait_ge(added, 16 * k + 16)
                each_job(pool, body, expert=False)


def finish(nc, m, ctx_out):
    with ExitStack() as ctx:
        def sb(name, shape, dt=F32):
            return ctx.enter_context(nc.sbuf_tensor(name, shape, dt))

        def sem(name):
            return ctx_out.enter_context(nc.semaphore(name))

        f = sb("f", [P, NT, D])
        ln_g = sb("ln2_g", [P, D])
        ln_b = sb("ln2_b", [P, D])
        stats = sb("stats7", [P, NT, 2, 6])
        aggr = sb("aggr7", [P, NT, 4])
        f_loaded = [sem(f"f_loaded{i}") for i in range(NT)]
        ln_loaded = sem("ln2_loaded")
        stats_ready = sem("stats_ready")
        var_ready = sem("var7_ready")
        rooted = sem("ln2_rooted")
        y_ready = sem("y_ready")
        y_stored = sem("out_stored")
        with nc.Block() as block:
            @block.sync
            def _(sp):
                for i, (t0, n) in enumerate(TOK_TILES):
                    sp.dma_start(f[0:n, i, :], m.scr_f[t0:t0 + n, :]).then_inc(f_loaded[i], 16)
                sp.dma_start(ln_g[:], m.vec["ln2_g"].broadcast_to([P, D])).then_inc(ln_loaded, 16)
                sp.dma_start(ln_b[:], m.vec["ln2_b"].broadcast_to([P, D])).then_inc(ln_loaded, 16)
                for i, (t0, n) in enumerate(TOK_TILES):
                    sp.wait_ge(y_ready, i + 1)
                    dst = m.y_prompt[t0:t0 + n, :] if i < TM else m.y_sample
                    sp.dma_start(dst, f[0:n, i, :]).then_inc(y_stored, 16)
                sp.wait_ge(y_stored, 16 * NT)

            @block.scalar
            def _(act):
                for i, (_, n) in enumerate(TOK_TILES):
                    act.wait_ge(var_ready, i + 1)
                    nc.scalar.activation(aggr[0:n, i, 2:3], aggr[0:n, i, 1:2], ACT.Sqrt, bias=m.eps_ln[0:n, :]).then_inc(rooted, 1)

            @block.vector
            def _(dve):
                ch = Chain(dve, m.vector_step, m.vector_count)
                dve.wait_ge(ln_loaded, 32)
                for i, (_, n) in enumerate(TOK_TILES):
                    x = f[0:n, i, :]
                    dve.wait_ge(f_loaded[i], 16)
                    for c in range(2):
                        last = nc.vector.bn_stats(stats[0:n, i, c, :], x[:, c * 512:(c + 1) * 512])
                    last.then_inc(stats_ready, 1)
                    dve.wait_ge(stats_ready, i + 1)
                    nc.vector.bn_aggr(aggr[0:n, i, 0:2], stats[0:n, i, :, :]).then_inc(var_ready, 1)
                    dve.wait_ge(var_ready, i + 1)
                    dve.wait_ge(rooted, i + 1)
                    ch.link(nc.vector.reciprocal(aggr[0:n, i, 3:4], aggr[0:n, i, 2:3]))
                    ch.link(nc.vector.tensor_scalar(x, x, aggr[0:n, i, 0:1], aggr[0:n, i, 3:4], ALU.subtract, ALU.mult))
                    ch.link(nc.vector.tensor_tensor(x, x, ln_g[0:n, :], ALU.mult))
                    nc.vector.tensor_tensor(x, x, ln_b[0:n, :], ALU.add).then_inc(y_ready, 1)


def constants(nc, m, ready):
    def build(pool):
        ch = Chain(pool, m.pool_step, m.pool_count)
        g = nc.gpsimd
        g.memset(m.eps_ln[:], LN_EPS)
        g.memset(m.eps_gn[:], GN_EPS)
        g.memset(m.ones[:], 1.0)
        g.memset(m.ones_mean[:], 1.0 / DC)
        ch.link(g.memset(m.ident[:], 0.0))
        g.affine_select(out=m.ident[:], in_=m.ident[:], compare_op=ALU.not_equal, fill=1.0, base=0,
                        pattern=[[-1, P]], channel_multiplier=1).then_inc(ready, 1)
        g.memset(m.head_ones[:], 1.0)
        g.memset(m.below[:], 1.0)
        g.memset(m.is_token[:], 1.0)
        g.memset(m.chunk_keep[:], 1.0)
        ch.link(g.memset(m.inside_mask[:], 1.0))
        heads = m.head_ones[:].rearrange("p (h c) -> p h c", c=N)
        ch.link(g.affine_select(out=heads, in_=heads, compare_op=ALU.is_ge, fill=0.0, base=0, pattern=[[-N, 2], [0, N]], channel_multiplier=1))
        ch.link(g.affine_select(out=heads, in_=heads, compare_op=ALU.is_ge, fill=0.0, base=N - 1, pattern=[[N, 2], [0, N]], channel_multiplier=-1))
        for c in range(CM):
            r = m.below[L * c:L * (c + 1), :]
            ch.link(g.affine_select(out=r, in_=r, compare_op=ALU.is_gt, fill=0.0, base=0, pattern=[[-1, L]], channel_multiplier=1))
        for part in range(3):
            v = m.inside_mask[:, part, :].rearrange("p (c t) -> p c t", t=L)
            ch.link(g.affine_select(out=v, in_=v, compare_op=ALU.is_ge, fill=0.0, base=0, pattern=[[-L, CM], [0, L]], channel_multiplier=1))
            ch.link(g.affine_select(out=v, in_=v, compare_op=ALU.is_ge, fill=0.0, base=L - 1, pattern=[[L, CM], [0, L]], channel_multiplier=-1))
            ch.link(g.affine_select(out=m.inside_mask[:, part, :], in_=m.inside_mask[:, part, :],
                                    compare_op=ALU.is_gt if part == 0 else ALU.is_ge, fill=0.0, base=0,
                                    pattern=[[1, P]], channel_multiplier=-1))
        g.memset(m.chunk_keep[:, 0:T:L], 0.0)
        g.affine_select(out=m.is_token[:, TM:], in_=m.is_token[:, TM:], compare_op=ALU.is_ge, fill=0.0, base=B - 1,
                        pattern=[[0, 1]], channel_multiplier=-1)
        wide = dict(allow_small_or_imprecise_dtypes=True)
        g.iota(m.tile_index[:], pattern=[[1, NT]], base=0, channel_multiplier=0, **wide)
        g.iota(m.partition_index[:], pattern=[[0, NT]], base=0, channel_multiplier=1, **wide)
        g.iota(m.minus_spare[:], pattern=[[0, 1]], base=-TT, channel_multiplier=-1, **wide)
        g.iota(m.slot_index[:], pattern=[[1, CAP]], base=0, channel_multiplier=0, **wide)
        g.iota(m.job_index[:], pattern=[[1, m.EXTRA]], base=0, channel_multiplier=0, **wide)
        g.iota(m.spare_row[:], pattern=[[0, 1]], base=TT, channel_multiplier=1, **wide)
    return build


class Shared:
    pass


def kernel_program(nc, a, outs):
    m = Shared()
    flat = "l k n -> (l k) n"
    m.x_prompt = a["x_prompt"].rearrange("b t d -> (b t) d")
    m.x_sample = a["x_sample"].rearrange("b t d -> (b t) d")
    m.state_conv = a["state_conv"].rearrange("l b w c -> (l b) w c")
    m.state_shift = a["state_shift"].rearrange("l b c -> (l b) c")
    m.state_wkv = a["state_wkv"].rearrange("l b h (two v) k -> (l b h two) (v k)", two=2)
    m.w_in = a["w_in"].rearrange(flat)
    m.conv_w = a["conv_w"].rearrange("l w c -> (l w) c")
    m.mu_shift = a["mu_shift"]
    m.vec = {n: a[n] if n != "r_k" else a[n].rearrange("l h n -> l (h n)")
             for n in PARAMS + ["gn_g", "gn_b", "ln1_g", "ln1_b", "ln2_g", "ln2_b", "router_bias"]}
    m.w_up, m.a_up, m.g_up = (a[n].rearrange(flat) for n in ("w_up", "a_up", "g_up"))
    m.w_out, m.router_w = (a[n].rearrange(flat) for n in ("w_out", "router_w"))
    m.sh_gate, m.sh_up, m.sh_down = (a[n].rearrange(flat) for n in ("sh_gate", "sh_up", "sh_down"))
    m.exp_gate = a["exp_gate"].rearrange("l e (p k) f -> (l e) p (k f)", p=P)
    m.exp_up = a["exp_up"].rearrange("l e (p k) f -> (l e) p (k f)", p=P)
    m.exp_down = a["exp_down"].rearrange("l e (j p) d -> (l e) p j d", p=P)
    m.y_prompt = outs[0].rearrange("b t d -> (b t) d")
    m.y_sample = outs[1].rearrange("b t d -> (b t) d")
    m.new_conv_p = outs[2].rearrange("l b w c -> (l b w) c")
    m.new_shift_p = outs[3].rearrange("l b c -> (l b) c")
    m.new_wkv_p = outs[4].rearrange("l b h v k -> (l b h) v k")
    m.new_conv_s = outs[5].rearrange("l b w c -> (l b) w c")
    m.new_shift_s = outs[6].rearrange("l b c -> (l b) c")
    m.new_wkv_s = outs[7].rearrange("l b h (two v) k -> (l b h two) (v k)", two=2)
    m.scr_lower = nc.dram_tensor("scr_lower", (P, L * L), F32).ap()
    m.scr_solved = nc.dram_tensor("scr_solved", (P, L * L), F32).ap()
    m.scr_sample = nc.dram_tensor("scr_sample", (6, B, DC), F32).ap()
    m.scr_y = nc.dram_tensor("scr_y", (B, DC), F32).ap()
    m.scr_x1 = nc.dram_tensor("scr_x1", (TT + CAP, D), F32).ap()
    m.scr_f = nc.dram_tensor("scr_f", (TT + CAP, D), F32).ap()
    m.MAX_JOBS = -(-TT // CAP)
    m.EXTRA = TT * K // CAP
    with ExitStack() as top:
        def sb(name, shape, dt=F32):
            return top.enter_context(nc.sbuf_tensor(name, shape, dt))

        m.vector_step = top.enter_context(nc.semaphore("vector_step"))
        m.vector_count = [0]
        m.pool_step = top.enter_context(nc.semaphore("pool_step"))
        m.pool_count = [0]
        first_sems = ExitStack()
        m.spent = []
        m.ident = sb("ident", [P, P])
        m.ones = sb("ones", [P, P])
        m.eps_ln = sb("eps_ln", [P, 1])
        m.eps_gn = sb("eps_gn", [P, 1])
        m.is_token = sb("is_token", [P, NT])
        m.tile_index = sb("tile_index", [P, NT])
        m.partition_index = sb("partition_index", [P, NT])
        m.slot_index = sb("slot_index", [P, CAP])
        m.job_index = sb("job_index", [P, m.EXTRA])
        m.job_expert = sb("job_expert", [P, m.EXTRA])
        m.job_base = sb("job_base", [P, m.EXTRA])
        m.job_table = sb("job_table", [1, m.EXTRA + 1], U32)
        m.spare_row = sb("spare_row", [P, 1])
        m.minus_spare = sb("minus_spare", [P, 1])
        m.position = sb("position", [P, E, NT])
        m.table = sb("table", [P, E, NT, 6], BF16)
        m.w_exp = sb("w_exp", [P, NB * EXPERT_FLOATS])
        at = lambda s, part: EXPERT_FLOATS * s + KD * FE * part
        m.expert_gate = [place(m, at(s, 0), KD, FE) for s in range(NB)]
        m.expert_up = [place(m, at(s, 1), KD, FE) for s in range(NB)]
        m.expert_down = [place(m, at(s, 2), 2, D) for s in range(NB)]
        m.UPPER = 2 * EXPERT_FLOATS
        m.BESIDE_ROWS = TM * DC * 3 + NT * DC + CT * T
        m.BESIDE_ZS = m.UPPER + NSH * TT
        m.zs = place(m, m.UPPER, NSH, TT)
        m.x_again = place(m, m.UPPER + 3 * KD * FE, 2, D)
        m.w_out_half = [place(m, m.UPPER + 4 * KD * FE, KD, 512), place(m, m.UPPER, KD, 512)]
        m.gate_loaded = [top.enter_context(nc.semaphore(f"gate_loaded{i}")) for i in range(NB)]
        m.up_loaded = [top.enter_context(nc.semaphore(f"up_loaded{i}")) for i in range(NB)]
        m.down_loaded = [top.enter_context(nc.semaphore(f"down_loaded{i}")) for i in range(NB)]
        m.w_out_loaded = [top.enter_context(nc.semaphore(f"w_out_loaded{i}")) for i in range(2)]
        m.x_again_loaded = [top.enter_context(nc.semaphore(f"x_again_loaded{i}")) for i in range(2)]
        with ExitStack() as late:
            def sb2(name, shape, dt=F32):
                return late.enter_context(nc.sbuf_tensor(name, shape, dt))

            m.conv = sb2("conv", [P, CT, TT])
            m.o_t = sb2("o_t", [P, CT, TT])
            with ExitStack() as mid:
                def sb3(name, shape, dt=F32):
                    return mid.enter_context(nc.sbuf_tensor(name, shape, dt))

                m.ones_mean = sb3("ones_mean", [P, P])
                m.head_ones = sb3("head_ones", [P, P])
                m.below = sb3("below", [P, L])
                m.inside_mask = sb3("inside_mask", [P, 3, P])
                m.chunk_keep = sb3("chunk_keep", [P, T])
                m.params = sb3("params", [P, CT, NPAR])
                project(nc, m, first_sems)
                m.v_rows = place(m, 0, NT, DC)
                m.gate = sb3("gate", [P, NT, DC])
                m.bonus = sb3("bonus", [P, NT, H])
                m.a_rows, m.b_rows, m.k_rows = (place(m, NT * DC + i * TM * DC, TM, DC) for i in range(3))
                m.read_decayed = sb3("read_decayed", [P, CT, TM, 2, P])
                m.b_grown = place(m, NT * DC + 3 * TM * DC, CT, T)
                m.k_grown = sb3("k_grown", [P, CT, T])
                m.chunk_decay = sb3("chunk_decay", [P, CT, NCH])
                m.sample_vec = sb3("sample_vec", [P, 6, CT, B])
                m.y_sample_rows = sb3("y_sample_rows", [B, DC])
                time_prepare(nc, m, first_sems)
                m.inverse = sb3("inverse", [P, TM * H, P])
                solve_chunks(nc, m, first_sems)
                recur(nc, m, top)
            first_sems.close()
            mix(nc, m, top)
        experts(nc, m, top)
        overflow(nc, m, top)
        finish(nc, m, top)


_INS = ["x_prompt", "x_sample", "state_conv", "state_shift", "state_wkv", "w_in", "mu_shift", "conv_w", "conv_b",
        "conv_ln_g", "conv_ln_b", "w0", "w_up", "a0", "a_up", "g_up", "k_k", "k_a", "r_k", "gn_g", "gn_b", "w_out",
        "ln1_g", "ln1_b", "router_w", "router_bias", "exp_gate", "exp_up", "exp_down", "sh_gate", "sh_up", "sh_down",
        "ln2_g", "ln2_b"]
_OUTS = [(1, T, D), (B, 1, D), (1, 1, CW - 1, DC), (1, 1, DS), (1, 1, H, N, N), (1, B, CW - 1, DC), (1, B, DS),
         (1, B, H, N, N)]


def kernel(**inputs):
    import numpy as _np
    import concourse.bacc as _bacc
    from concourse import mybir as _mybir
    from concourse.bass_utils import run_bass_kernel_spmd as _run

    nc = _bacc.Bacc("TRN2", target_bir_lowering=False, num_devices=1)
    arrays, aps = {}, {}
    for name in _INS:
        x = _np.ascontiguousarray(inputs[name])
        arrays[f"in_{name}_dram"] = x
        aps[name] = nc.dram_tensor(f"in_{name}_dram", x.shape, _mybir.dt.from_np(x.dtype), kind="ExternalInput").ap()
    outs = [nc.dram_tensor(f"out_{i}_dram", shape, _mybir.dt.float32, kind="ExternalOutput").ap()
            for i, shape in enumerate(_OUTS)]
    kernel_program(nc, aps, outs)
    r = _run(nc, [arrays], core_ids=[0])
    return tuple(r.results[0][f"out_{i}_dram"] for i in range(len(_OUTS)))
```

```python
from contextlib import ExitStack

import concourse.bass as bass
from concourse import mybir

F32 = mybir.dt.float32
U32 = mybir.dt.uint32
BF16 = mybir.dt.bfloat16
ALU = mybir.AluOpType
ACT = mybir.ActivationFunctionType
AX = mybir.AxisListType.X

P = 128
D = 1024
KD = D // P
T = 512
B = 8
TT = T + B
HALF = TT // 2
TM = T // P
DC = 512
CT = DC // P
CW = 31
H = 8
N = 64
LW = 64
LA = 64
LG = 160
DS = 3 * 512 + LW + LA + LG
L = 32
NCH = T // L
CM = P // L
E = 64
FE = 256
K = 8
G = 8
KG = 4
CAP = 96
NB = 4
EXPERT_FLOATS = 3 * KD * FE
ALPHA = 2.0 ** 0.25
LN_EPS = 1e-5
GN_EPS = 64e-5
ROUTED_SCALE = 2.5
DECAY_SCALE = 0.6065306597126334
TOK_TILES = [(i * P, P) for i in range(TM)] + [(T, B)]
NT = len(TOK_TILES)

CONV_TILES = [(kind, i, off + i * P, P) for i in range(CT) for kind, off in (("glu_a", 0), ("glu_gate", DC))]
_RW = 2 * DC
SHIFT_TILES = [("lora", 0, _RW + 1536, P), ("gate0", 0, _RW + 1664, P)] \
    + [(kind, i, _RW + j * 512 + i * P, P) for i in range(CT) for j, kind in enumerate("rkv")] \
    + [("gate1", 0, _RW + 1792, 32)]
COL_TILES = CONV_TILES + SHIFT_TILES
NCOL = len(COL_TILES)
NCONV = len(CONV_TILES)
NSH = len(SHIFT_TILES)
LORA, GATE0, GATE1 = 0, 1, NSH - 1


def shift_index(kind, i):
    return 2 + 3 * i + "rkv".index(kind)


PARAMS = ["conv_b", "conv_ln_g", "conv_ln_b", "w0", "a0", "k_k", "k_a", "r_k"]
NPAR = CW + len(PARAMS)


def par(name):
    return CW + PARAMS.index(name)


class Chain:

    def __init__(self, eng, sem, state):
        self.eng, self.sem, self.state = eng, sem, state

    def link(self, ins):
        self.state[0] += 1
        ins.then_inc(self.sem, 1)
        self.eng.wait_ge(self.sem, self.state[0])


def cols(i):
    t0, n = TOK_TILES[i]
    return slice(t0, t0 + n)


def place(m, at, *shape):
    size = 1
    for n in shape:
        size *= n
    assert at + size <= NB * EXPERT_FLOATS
    names = "abcde"[:len(shape)]
    flat = m.w_exp[:, at:at + size]
    return flat.rearrange(f"p ({' '.join(names)}) -> p {' '.join(names)}", **dict(zip(names, shape)))


def halves(ap):
    return ap.rearrange("p (b t) -> p b t", b=2)


def banks(ap):
    return ap.rearrange("p (b t) -> p b t", b=2)[:, :, 0:HALF]


def project(nc, m, ctx_out):
    WB = 6
    ZB = 3
    PER_GLU, PER_SHIFT = 20, 3
    assert PER_GLU * CT + PER_SHIFT * NSH >= CT * CW
    with ExitStack() as ctx:
        def sb(name, shape, dt=F32):
            return ctx.enter_context(nc.sbuf_tensor(name, shape, dt))

        def ps(name, shape, dt=F32):
            return ctx.enter_context(nc.psum_tensor(name, shape, dt))

        def sem(name):
            m.spent.append(ctx_out.enter_context(nc.semaphore(name)))
            return m.spent[-1]

        x_rows = sb("x_rows", [P, NT, D])
        x_t = place(m, 0, KD, TT)
        w_col = place(m, KD * TT, WB, KD, P)
        staged = sb("staged", [P, ZB, 1 + TT])
        glu_stage = sb("glu_stage", [P, 2, TT])
        u_pad = sb("u_pad", [P, CT, CW - 1 + T])
        z_last = sb("z_last", [P, NSH, 1 + B])
        z_diff = sb("z_diff", [P, 2, T])
        z_sample = sb("z_sample", [P, NCOL, B])
        gate_sample = sb("gate_sample", [P, CT, B])
        u_sample = sb("u_sample", [P, CT, B])
        zd_sample = sb("zd_sample", [P, NSH, B])
        par_rows = sb("par_rows", [NPAR, DC])
        shift_rows = sb("shift_rows", [B + 1, DS])
        conv_rows = sb("conv_rows", [120, 2, DC])
        shift_t = sb("shift_t", [P, NSH, B + 1])
        conv_state = sb("conv_state", [P, CT, B * (CW - 1)])
        conv_prod = sb("conv_prod", [P, CT, B * (CW - 1)])
        conv_sum = sb("conv_sum", [P, CT, B])
        tail_rows = sb("tail_rows", [38, DC])
        tail_in = sb("tail_in", [P, CT, 38])
        shift_out = sb("shift_out", [1 + B, DS])
        pz = ps("pz", [P, 3, 1024])
        pt = pz[:, 2, :].rearrange("p (b n) -> p b n", b=2)
        pm = ps("pm", [P, 2, 512])

        x_loaded = [sem(f"x_loaded{i}") for i in range(NT)]
        small_loaded = sem("small_loaded")
        w_loaded = [sem(f"w_loaded{i}") for i in range(WB)]
        consts_ready = sem("consts_ready")
        xt_turned = sem("xt_turned")
        xt_ready = sem("xt_ready")
        small_turned = sem("small_turned")
        small_ready = sem("small_ready")
        tile_projected = sem("tile_projected")
        tile_taken = sem("tile_taken")
        staged_used = sem("staged_used")
        glu_used = sem("glu_used")
        sample_gated = sem("sample_gated")
        tails_ready = sem("tails_ready")
        tails_turned = sem("tails_turned")
        tails_copied = sem("tails_copied")
        state_stored = sem("state_stored")
        zeros_ready = sem("zeros_ready")
        XT_GROUPS = 2 * TM + 1
        SMALL = 4

        with nc.Block() as block:
            @block.sync
            def _(sp):
                for i, (t0, n) in enumerate(TOK_TILES):
                    src = m.x_prompt[t0:t0 + n, :] if i < TM else m.x_sample
                    sp.dma_start(x_rows[0:n, i, :], src).then_inc(x_loaded[i], 16)
                for c, (_, _, c0, w) in enumerate(COL_TILES):
                    if c >= WB:
                        sp.wait_ge(tile_projected, c - WB + 1)
                    sp.dma_start(w_col[:, c % WB, :, 0:w],
                                 m.w_in[:, c0:c0 + w].rearrange("(k p) n -> p k n", p=P)).then_inc(w_loaded[c % WB], 16)
                sp.wait_ge(tails_copied, 2)
                sp.dma_start(m.new_conv_p, tail_rows[0:30, :]).then_inc(state_stored, 16)
                sp.dma_start(m.new_conv_s[:, CW - 2, :], tail_rows[30:38, :]).then_inc(state_stored, 16)
                sp.wait_ge(tails_copied, 6)
                sp.dma_start(m.new_shift_p, shift_out[0:1, :]).then_inc(state_stored, 16)
                sp.dma_start(m.new_shift_s, shift_out[1:1 + B, :]).then_inc(state_stored, 16)
                sp.wait_ge(state_stored, 16 * 5)

            @block.scalar
            def _(act):
                for g in range(XT_GROUPS):
                    act.wait_ge(xt_turned, g + 1)
                    if g < 2 * TM:
                        i, k0 = g // 2, 4 * (g % 2)
                        nc.scalar.copy(x_t[:, k0:k0 + 4, cols(i)],
                                       pt[:, g % 2, :].rearrange("p (k t) -> p k t", k=4)).then_inc(xt_ready, 1)
                    else:
                        nc.scalar.copy(x_t[:, :, cols(TM)],
                                       pt[:, g % 2, 0:KD * B].rearrange("p (k t) -> p k t", k=KD)).then_inc(xt_ready, 1)
                act.dma_start(par_rows[0:CW, :], m.conv_w).then_inc(small_loaded, 16)
                for name in PARAMS:
                    act.dma_start(par_rows[par(name):par(name) + 1, :], m.vec[name]).then_inc(small_loaded, 16)
                act.dma_start(shift_rows[0:B, :], m.state_shift).then_inc(small_loaded, 16)
                act.dma_start(shift_rows[B:B + 1, :], m.mu_shift).then_inc(small_loaded, 16)
                for j in range(2):
                    act.dma_start(conv_rows[:, j, :],
                                  m.state_conv[4 * j:4 * j + 4].rearrange("b w c -> (b w) c")).then_inc(small_loaded, 16)
                act.dma_start(m.new_conv_s[:, 0:CW - 2, :], m.state_conv[:, 1:CW - 1, :]).then_inc(state_stored, 16)
                act.wait_ge(zeros_ready, 3)
                for c, (kind, i, _, w) in enumerate(COL_TILES):
                    if c == NCONV:
                        act.wait_ge(tile_taken, NCONV)
                        nc.scalar.activation(gate_sample[:], z_sample[:, 1:NCONV:2, :], ACT.Sigmoid).then_inc(sample_gated, 1)
                    act.wait_ge(tile_projected, c + 1)
                    z = banks(pz[0:w, c % 3, :])
                    nc.scalar.copy(z_sample[0:w, c, :], z[:, 1, HALF - B:HALF])
                    if kind == "glu_a":
                        if i >= 1:
                            act.wait_ge(glu_used, i)
                        nc.scalar.copy(halves(glu_stage[:, 0, :]), z).then_inc(tile_taken, 1)
                    elif kind == "glu_gate":
                        nc.scalar.activation(halves(glu_stage[:, 1, :]), z, ACT.Sigmoid).then_inc(tile_taken, 1)
                    else:
                        s = c - NCONV
                        if s >= ZB:
                            act.wait_ge(staged_used, s - ZB + 1)
                        nc.scalar.copy(z_last[0:w, s, 0:1], z[:, 1, HALF - B - 1:HALF - B])
                        nc.scalar.copy(halves(staged[0:w, s % ZB, 1:1 + TT]), z).then_inc(tile_taken, 1)

            @block.tensor
            def _(pe):
                pe.wait_ge(consts_ready, 1)
                for g in range(XT_GROUPS):
                    i = g // 2
                    pe.wait_ge(x_loaded[i], 16)
                    if g >= 2:
                        pe.wait_ge(xt_ready, g - 1)
                    if g < 2 * TM:
                        for k in range(4):
                            d0 = (4 * (g % 2) + k) * P
                            last = nc.tensor.transpose(pt[:, g % 2, k * P:(k + 1) * P], x_rows[:, i, d0:d0 + P], m.ident[:])
                    else:
                        for k in range(KD):
                            last = nc.tensor.transpose(pt[:, g % 2, k * B:(k + 1) * B],
                                                       x_rows[0:B, TM, k * P:(k + 1) * P], m.ident[0:B, 0:B])
                    last.then_inc(xt_turned, 1)
                def turn_small():
                    pe.wait_ge(small_loaded, 16 * (1 + len(PARAMS) + 4))
                    for i in range(CT):
                        last = nc.tensor.transpose(pm[:, 0, i * NPAR:(i + 1) * NPAR], par_rows[:, i * P:(i + 1) * P],
                                                   m.ident[0:NPAR, 0:NPAR])
                    last.then_inc(small_turned, 1)
                    for s, (_, _, c0, w) in enumerate(SHIFT_TILES):
                        last = nc.tensor.transpose(pm[0:w, 1, s * (B + 1):(s + 1) * (B + 1)],
                                                   shift_rows[:, c0 - _RW:c0 - _RW + w], m.ident[0:B + 1, 0:B + 1])
                    last.then_inc(small_turned, 1)
                    for h in range(2):
                        pe.wait_ge(small_ready, h + 1)
                        for i in range(2):
                            for j in range(2):
                                last = nc.tensor.transpose(pm[:, h, (2 * i + j) * 120:(2 * i + j + 1) * 120],
                                                           conv_rows[:, j, (2 * h + i) * P:(2 * h + i + 1) * P],
                                                           m.ident[0:120, 0:120])
                        last.then_inc(small_turned, 1)

                pe.wait_ge(xt_ready, XT_GROUPS)
                for c, (_, _, _, w) in enumerate(COL_TILES):
                    if c == 2:
                        turn_small()
                    pe.wait_ge(w_loaded[c % WB], 16 * (c // WB + 1))
                    if c >= 3:
                        pe.wait_ge(tile_taken, c - 2)
                    for k in range(KD):
                        for b in range(2):
                            last = nc.tensor.matmul(banks(pz[0:w, c % 3, :])[:, b, :], w_col[:, c % WB, k, 0:w],
                                                    halves(x_t[:, k, :])[:, b, :], start=(k == 0), stop=(k == KD - 1))
                    last.then_inc(tile_projected, 1)
                pe.wait_ge(tails_ready, 1)
                for i in range(CT):
                    last = nc.tensor.transpose(pm[0:38, 0, i * P:(i + 1) * P], tail_in[:, i, :], m.ident[:])
                last.then_inc(tails_turned, 1)
                pe.wait_ge(tails_ready, 2)
                for q in range(4):
                    if q >= 1:
                        pe.wait_ge(tails_copied, q + 1)
                    for s in range(4 * q, min(4 * q + 4, NSH)):
                        w = SHIFT_TILES[s][3]
                        last = nc.tensor.transpose(pm[0:1 + B, 1 - q % 2, (s % 4) * P:(s % 4) * P + w],
                                                   z_last[0:w, s, :], m.ident[0:w, 0:w])
                    last.then_inc(tails_turned, 1)

            @block.vector
            def _(dve):
                ch = Chain(dve, m.vector_step, m.vector_count)
                nc.vector.memset(u_pad[:, :, 0:CW - 1], 0.0).then_inc(zeros_ready, 1)
                for b in range(ZB):
                    last = nc.vector.memset(staged[:, b, 0:1], 0.0)
                last.then_inc(zeros_ready, 1)
                nc.vector.memset(shift_t[:], 0.0).then_inc(zeros_ready, 1)
                dve.wait_ge(zeros_ready, 3)
                dve.wait_ge(small_turned, 1)
                ch.link(nc.vector.tensor_copy(m.params[:], pm[:, 0, 0:CT * NPAR].rearrange("p (i n) -> p i n", i=CT)))
                dve.wait_ge(small_turned, 2)
                nc.vector.tensor_copy(shift_t[:, 0:NSH - 1, :], pm[:, 1, 0:(NSH - 1) * (B + 1)].rearrange("p (i n) -> p i n", n=B + 1))
                nc.vector.tensor_copy(shift_t[0:32, NSH - 1, :], pm[0:32, 1, (NSH - 1) * (B + 1):NSH * (B + 1)]).then_inc(small_ready, 2)
                for h in range(2):
                    dve.wait_ge(small_turned, 3 + h)
                    nc.vector.tensor_copy(conv_state[:, 2 * h:2 * h + 2, :],
                                          pm[:, h, 0:480].rearrange("p (i n) -> p i n", i=2)).then_inc(small_ready, 1)
                dve.wait_ge(small_ready, 4)

                def convolve(n):
                    i, j = n // CW, n % CW
                    out, u = m.conv[:, i, 0:T], u_pad[:, i, j:j + T]
                    if j == 0:
                        ch.link(nc.vector.tensor_scalar(out, u, m.params[:, i, 0:1],
                                                        m.params[:, i, par("conv_b"):par("conv_b") + 1], ALU.mult, ALU.add))
                    else:
                        ch.link(nc.vector.scalar_tensor_tensor(out, u, m.params[:, i, j:j + 1], out, ALU.mult, ALU.add))

                for i in range(CT):
                    dve.wait_ge(tile_taken, 2 * i + 2)
                    nc.vector.tensor_tensor(u_pad[:, i, CW - 1:CW - 1 + T], glu_stage[:, 0, 0:T], glu_stage[:, 1, 0:T],
                                            ALU.mult).then_inc(glu_used, 1)
                    dve.wait_ge(glu_used, i + 1)
                    for n in range(PER_GLU * i, PER_GLU * (i + 1)):
                        convolve(n)
                glu = z_sample[:, 0:NCONV, :].rearrange("p (i two) b -> p i two b", two=2)
                dve.wait_ge(sample_gated, 1)
                ch.link(nc.vector.tensor_tensor(u_sample[:], glu[:, :, 0, :], gate_sample[:], ALU.mult))
                ch.link(nc.vector.tensor_tensor(conv_prod[:].rearrange("p i (b j) -> p i b j", b=B),
                                                conv_state[:].rearrange("p i (b j) -> p i b j", b=B),
                                                m.params[:, :, 0:CW - 1].unsqueeze(2).broadcast_to([P, CT, B, CW - 1]), ALU.mult))
                ch.link(nc.vector.tensor_reduce(conv_sum[:], conv_prod[:].rearrange("p i (b j) -> p i b j", b=B), AX, ALU.add))
                ch.link(nc.vector.tensor_tensor(m.conv[:, :, T:TT], u_sample[:],
                                                m.params[:, :, CW - 1:CW].broadcast_to([P, CT, B]), ALU.mult))
                ch.link(nc.vector.tensor_tensor(conv_sum[:], conv_sum[:],
                                                m.params[:, :, par("conv_b"):par("conv_b") + 1].broadcast_to([P, CT, B]), ALU.add))
                ch.link(nc.vector.tensor_tensor(m.conv[:, :, T:TT], m.conv[:, :, T:TT], conv_sum[:], ALU.add))
                nc.vector.tensor_copy(tail_in[:, :, 0:30], u_pad[:, :, T:T + CW - 1])
                nc.vector.tensor_copy(tail_in[:, :, 30:38], u_sample[:]).then_inc(tails_ready, 1)
                for s, (_, _, _, w) in enumerate(SHIFT_TILES):
                    dve.wait_ge(tile_taken, NCONV + s + 1)
                    st = staged[0:w, s % ZB, :]
                    ch.link(nc.vector.tensor_tensor(z_diff[0:w, s % 2, :], st[:, 0:T], st[:, 1:T + 1], ALU.subtract))
                    nc.vector.scalar_tensor_tensor(m.zs[0:w, s, 0:T], z_diff[0:w, s % 2, :], shift_t[0:w, s, B:B + 1],
                                                   st[:, 1:T + 1], ALU.mult, ALU.add).then_inc(staged_used, 1)
                    for n in range(min(PER_GLU * CT + PER_SHIFT * s, CT * CW), min(PER_GLU * CT + PER_SHIFT * (s + 1), CT * CW)):
                        convolve(n)
                dve.wait_ge(tile_taken, NCOL)
                nc.vector.tensor_copy(z_last[:, 0:NSH - 1, 1:], z_sample[:, NCONV:NCOL - 1, :])
                nc.vector.tensor_copy(z_last[0:32, NSH - 1, 1:], z_sample[0:32, NCOL - 1, :]).then_inc(tails_ready, 1)
                for sl, w in ((slice(0, NSH - 1), P), (slice(NSH - 1, NSH), 32)):
                    zc = slice(NCONV + sl.start, NCONV + sl.stop)
                    n = sl.stop - sl.start
                    ch.link(nc.vector.tensor_tensor(zd_sample[0:w, sl, :], shift_t[0:w, sl, 0:B], z_sample[0:w, zc, :], ALU.subtract))
                    ch.link(nc.vector.tensor_tensor(zd_sample[0:w, sl, :], zd_sample[0:w, sl, :],
                                                    shift_t[0:w, sl, B:B + 1].broadcast_to([w, n, B]), ALU.mult))
                    ch.link(nc.vector.tensor_tensor(m.zs[0:w, sl, T:TT], zd_sample[0:w, sl, :], z_sample[0:w, zc, :], ALU.add))
                dve.wait_ge(tails_turned, 1)
                nc.vector.tensor_copy(tail_rows[:], pm[0:38, 0, :]).then_inc(tails_copied, 2)
                for q in range(4):
                    dve.wait_ge(tails_turned, q + 2)
                    for s in range(4 * q, min(4 * q + 4, NSH)):
                        _, _, c0, w = SHIFT_TILES[s]
                        last = nc.vector.tensor_copy(shift_out[:, c0 - _RW:c0 - _RW + w],
                                                     pm[0:1 + B, 1 - q % 2, (s % 4) * P:(s % 4) * P + w])
                    last.then_inc(tails_copied, 1)

            @block.gpsimd
            def _(pool):
                constants(nc, m, consts_ready)(pool)



def time_prepare(nc, m, ctx_out):
    with ExitStack() as ctx:
        def sb(name, shape, dt=F32):
            return ctx.enter_context(nc.sbuf_tensor(name, shape, dt))

        def ps(name, shape, dt=F32):
            return ctx.enter_context(nc.psum_tensor(name, shape, dt))

        def sem(name):
            m.spent.append(ctx_out.enter_context(nc.semaphore(name)))
            return m.spent[-1]

        lora_w = sb("lora_w", [P, DC])
        g_up0 = sb("g_up0", [P, DC])
        g_up1 = sb("g_up1", [32, DC])
        wd_tanh = sb("wd_tanh", [LW, TT])
        gd_sig = place(m, m.BESIDE_ROWS, 2, TT)
        decay = place(m, m.BESIDE_ZS, CT, TT)
        rate = place(m, m.BESIDE_ZS + CT * TT, CT, TT)
        norm = [m.read_decayed[:, i].rearrange("p j a t -> p (j a t)")[:, 0:TT] for i in range(CT)]
        kk = sb("kk", [P, TT])
        k2 = sb("k2", [P, TT])
        kb = sb("kb", [P, TT])
        tmp = sb("tmp", [P, TT])
        rk = sb("rk", [P, TT])
        cum = sb("cum", [P, T])
        cum_before = sb("cum_before", [P, T])
        cum_end = sb("cum_end", [P, T])
        e_before = sb("e_before", [P, T])
        e_after = sb("e_after", [P, T])
        e_inverse = sb("e_inverse", [P, T])
        e_end = sb("e_end", [P, T])
        b_end = sb("b_end", [P, T])
        k_end = sb("k_end", [P, T])
        big = ps("big", [P, 2, 1024])
        turn = ps("turn", [P, 2, 512])
        pg = ps("pg", [P, 512])
        pb = ps("pb", [P, NT * H])

        w_in2 = sem("lora_loaded")
        tanh_ready = sem("tanh_ready")
        lora_done = sem("lora_done")
        lora_taken = sem("lora_taken")
        sq_ready = sem("sq_ready")
        ss_done = sem("ss_done")
        norm_root = sem("norm_root")
        cum_ready = sem("cum_ready")
        exp_ready = sem("exp_ready")
        bonus_in = sem("bonus_in")
        bonus_done = sem("bonus_done")
        scaled_ready = sem("scaled_ready")
        turned = sem("turned")
        turned_taken = sem("turned_taken")
        gate_done = sem("gate_done")
        gate_taken = sem("gate_taken")
        norm_inverted = sem("norm_inverted")
        NTURN = 5

        with nc.Block() as block:
            @block.sync
            def _(sp):
                sp.dma_start(lora_w[0:LW, :], m.w_up).then_inc(w_in2, 16)
                sp.dma_start(lora_w[LW:P, :], m.a_up).then_inc(w_in2, 16)
                sp.dma_start(g_up0[:], m.g_up[0:P, :]).then_inc(w_in2, 16)
                sp.dma_start(g_up1[:], m.g_up[P:LG, :]).then_inc(w_in2, 16)

            @block.tensor
            def _(pe):
                for i in range(CT):
                    pe.wait_ge(sq_ready, i + 1)
                    if i >= 2:
                        pe.wait_ge(norm_root, i - 1)
                    for b in range(2):
                        last = nc.tensor.matmul(banks(big[:, i % 2, :])[:, b, :], m.head_ones[:], halves(norm[i])[:, b, :],
                                                start=True, stop=True)
                    last.then_inc(ss_done, 1)
                pe.wait_ge(w_in2, 64)
                pe.wait_ge(tanh_ready, 1)
                for j in range(2 * CT):
                    i, rows = j // 2, slice(0, LW) if j % 2 == 0 else slice(LW, P)
                    src = wd_tanh[:, :] if j % 2 == 0 else m.zs[LW:P, LORA, :]
                    if j >= 2:
                        pe.wait_ge(lora_taken, j - 1)
                    else:
                        pe.wait_ge(norm_root, CT)
                    for b in range(2):
                        last = nc.tensor.matmul(banks(big[:, j % 2, :])[:, b, :], lora_w[rows, i * P:(i + 1) * P], halves(src)[:, b, :],
                                                start=True, stop=True)
                    last.then_inc(lora_done, 1)
                pe.wait_ge(tanh_ready, 2)

                def gate(i):
                    t0, n = TOK_TILES[i]
                    if i >= 1:
                        pe.wait_ge(gate_taken, i)
                    nc.tensor.matmul(pg[0:n, :], gd_sig[:, 0, t0:t0 + n], g_up0[:], start=True, stop=False)
                    nc.tensor.matmul(pg[0:n, :], gd_sig[0:32, 1, t0:t0 + n], g_up1[:], start=False, stop=True).then_inc(gate_done, 1)
                gate(0)
                for i in range(CT):
                    gate(i + 1)
                    pe.wait_ge(bonus_in, i + 1)
                    for j, (t0, n) in enumerate(TOK_TILES):
                        last = nc.tensor.matmul(pb[0:n, j * H + 2 * i:j * H + 2 * i + 2], rk[:, t0:t0 + n], m.head_ones[:, 0:P:N],
                                                start=True, stop=True)
                    last.then_inc(bonus_done, 1)
                    for q in range(NTURN):
                        g = NTURN * i + q
                        if g >= 2:
                            pe.wait_ge(turned_taken, g - 1)
                        if q < 4:
                            if q == 0:
                                pe.wait_ge(scaled_ready, i + 1)
                            for j in range(TM):
                                src = (m.read_decayed[:, i, j, 0, :], b_end[:, cols(j)], k_end[:, cols(j)],
                                       m.zs[:, shift_index("v", i), cols(j)])[q]
                                last = nc.tensor.transpose(turn[:, g % 2, j * P:(j + 1) * P], src, m.ident[:])
                        else:
                            last = nc.tensor.transpose(turn[0:B, g % 2, 0:P], m.zs[:, shift_index("v", i), T:TT], m.ident[:])
                        last.then_inc(turned, 1)

            @block.scalar
            def _(act):
                for i in range(CT):
                    nc.scalar.activation(norm[i], m.zs[:, shift_index("k", i), :], ACT.Square,
                                         scale=m.params[:, i, par("k_k"):par("k_k") + 1]).then_inc(sq_ready, 1)
                for i in range(CT):
                    act.wait_ge(ss_done, i + 1)
                    nc.scalar.activation(halves(norm[i]), banks(big[:, i % 2, :]), ACT.Sqrt).then_inc(norm_root, 1)
                nc.scalar.activation(wd_tanh[:], m.zs[0:LW, LORA, :], ACT.Tanh).then_inc(tanh_ready, 1)
                nc.scalar.activation(gd_sig[:, 0, :], m.zs[:, GATE0, :], ACT.Sigmoid)
                nc.scalar.activation(gd_sig[0:32, 1, :], m.zs[0:32, GATE1, :], ACT.Sigmoid).then_inc(tanh_ready, 1)
                for j in range(2 * CT):
                    i = j // 2
                    act.wait_ge(lora_done, j + 1)
                    dst, bias = (decay, "w0") if j % 2 == 0 else (rate, "a0")
                    nc.scalar.activation(halves(dst[:, i, :]), banks(big[:, j % 2, :]), ACT.Sigmoid,
                                         bias=m.params[:, i, par(bias):par(bias) + 1]).then_inc(lora_taken, 1)

                def copy_gate(i):
                    n = TOK_TILES[i][1]
                    act.wait_ge(gate_done, i + 1)
                    nc.scalar.copy(m.gate[0:n, i, :], pg[0:n, :]).then_inc(gate_taken, 1)

                def exponentials(i):
                    act.wait_ge(cum_ready, i + 1)
                    if i >= 1:
                        act.wait_ge(scaled_ready, i)
                    nc.scalar.activation(e_before[:], cum_before[:], ACT.Exp, scale=-DECAY_SCALE)
                    nc.scalar.activation(e_after[:], cum[:], ACT.Exp, scale=-DECAY_SCALE)
                    nc.scalar.activation(e_inverse[:], cum[:], ACT.Exp, scale=DECAY_SCALE)
                    nc.scalar.activation(e_end[:], cum_end[:], ACT.Exp, scale=DECAY_SCALE)
                    nc.scalar.activation(m.chunk_decay[:, i, :], cum[:, L - 1:T:L], ACT.Exp, scale=-DECAY_SCALE)
                    nc.scalar.activation(m.sample_vec[:, 0, i, :], decay[:, i, T:TT], ACT.Exp, scale=-DECAY_SCALE).then_inc(exp_ready, 1)

                exponentials(0)
                copy_gate(0)
                for i in range(CT):
                    copy_gate(i + 1)
                    if i + 1 < CT:
                        exponentials(i + 1)
                    for q in range(NTURN):
                        g = NTURN * i + q
                        act.wait_ge(turned, g + 1)
                        if q < 4:
                            nc.scalar.copy((m.a_rows, m.b_rows, m.k_rows, m.v_rows)[q][:, 0:TM, i * P:(i + 1) * P],
                                           turn[:, g % 2, :].rearrange("p (j c) -> p j c", j=TM)).then_inc(turned_taken, 1)
                        else:
                            nc.scalar.copy(m.v_rows[0:B, TM, i * P:(i + 1) * P], turn[0:B, g % 2, 0:P]).then_inc(turned_taken, 1)

            @block.vector
            def _(dve):
                ch = Chain(dve, m.vector_step, m.vector_count)

                def cumulate(i):
                    dve.wait_ge(lora_taken, 2 * i + 2)
                    if i >= 1:
                        dve.wait_ge(exp_ready, i)
                    ch.link(nc.vector.tensor_tensor_scan(cum[:], m.chunk_keep[:], decay[:, i, 0:T], 0.0, ALU.mult, ALU.add))
                    nc.vector.tensor_tensor(cum_before[:], cum[:], decay[:, i, 0:T], ALU.subtract)
                    nc.vector.tensor_tensor(cum_end[:].rearrange("p (c l) -> p c l", l=L), cum[:].rearrange("p (c l) -> p c l", l=L),
                                            cum[:, L - 1:T:L].unsqueeze(2).broadcast_to([P, NCH, L]), ALU.subtract).then_inc(cum_ready, 1)

                for i in range(CT):
                    dve.wait_ge(norm_root, i + 1)
                    ch.link(nc.vector.tensor_scalar(norm[i], norm[i], 1e-12, None, ALU.max))
                    nc.vector.reciprocal(norm[i], norm[i]).then_inc(norm_inverted, 1)
                cumulate(0)
                for i in range(CT):
                    r = m.zs[:, shift_index("r", i), :]
                    k = m.zs[:, shift_index("k", i), :]
                    v = m.zs[:, shift_index("v", i), :]
                    if i >= 1:
                        dve.wait_ge(scaled_ready, i)
                    ch.link(nc.vector.tensor_scalar(tmp[:], rate[:, i, :], 1.0, m.params[:, i, par("k_a"):par("k_a") + 1],
                                                    ALU.subtract, ALU.mult))
                    ch.link(nc.vector.scalar_tensor_tensor(k2[:], tmp[:], 1.0, k, ALU.add, ALU.mult))
                    if i >= 1:
                        dve.wait_ge(bonus_done, i)
                    nc.vector.scalar_tensor_tensor(rk[:], r, m.params[:, i, par("r_k"):par("r_k") + 1], k2[:],
                                                   ALU.mult, ALU.mult).then_inc(bonus_in, 1)
                    dve.wait_ge(norm_inverted, i + 1)
                    ch.link(nc.vector.scalar_tensor_tensor(kk[:], k, m.params[:, i, par("k_k"):par("k_k") + 1], norm[i],
                                                           ALU.mult, ALU.mult))
                    nc.vector.tensor_copy(m.sample_vec[:, 1, i, :], kk[:, T:TT])
                    ch.link(nc.vector.scalar_tensor_tensor(kb[:], kk[:], -1.0, rate[:, i, :], ALU.mult, ALU.mult))
                    nc.vector.tensor_copy(m.sample_vec[:, 2, i, :], kb[:, T:TT])
                    nc.vector.tensor_copy(m.sample_vec[:, 3, i, :], k2[:, T:TT])
                    nc.vector.tensor_copy(m.sample_vec[:, 4, i, :], r[:, T:TT])
                    nc.vector.tensor_copy(m.sample_vec[:, 5, i, :], v[:, T:TT])
                    if i + 1 < CT:
                        cumulate(i + 1)
                    dve.wait_ge(exp_ready, i + 1)
                    if i >= 1:
                        dve.wait_ge(turned, NTURN * (i - 1) + 3)
                    tiles = lambda ap: ap.rearrange("p (j t) -> p j t", j=TM)
                    nc.vector.tensor_tensor(m.read_decayed[:, i, :, 0, :], tiles(kk[:, 0:T]), tiles(e_before[:]), ALU.mult)
                    nc.vector.tensor_tensor(b_end[:], kb[:, 0:T], e_end[:], ALU.mult)
                    nc.vector.tensor_tensor(k_end[:], k2[:, 0:T], e_end[:], ALU.mult)
                    nc.vector.tensor_tensor(m.read_decayed[:, i, :, 1, :], tiles(r[:, 0:T]), tiles(e_after[:]), ALU.mult)
                    nc.vector.tensor_tensor(m.b_grown[:, i, :], kb[:, 0:T], e_inverse[:], ALU.mult)
                    nc.vector.tensor_tensor(m.k_grown[:, i, :], k2[:, 0:T], e_inverse[:], ALU.mult).then_inc(scaled_ready, 1)
                dve.wait_ge(bonus_done, CT)
                nc.vector.tensor_copy(m.bonus[:, 0:TM, :], pb[:, 0:TM * H].rearrange("p (j h) -> p j h", h=H))
                nc.vector.tensor_copy(m.bonus[0:B, TM, :], pb[0:B, TM * H:])

def solve_chunks(nc, m, ctx_out):
    SETS = TM * H
    MASK_STEPS = (18, 21, 24, 27)
    with ExitStack() as ctx:
        def sb(name, shape, dt=F32):
            return ctx.enter_context(nc.sbuf_tensor(name, shape, dt))

        def ps(name, shape, dt=F32):
            return ctx.enter_context(nc.psum_tensor(name, shape, dt))

        def sem(name):
            m.spent.append(ctx_out.enter_context(nc.semaphore(name)))
            return m.spent[-1]

        lower = sb("lower", [P, SETS, L])
        sys_n = place(m, m.BESIDE_ZS, L, L)
        sol_t = place(m, m.BESIDE_ZS + L * L, L, L)
        prod = sb("prod", [P, L * L])
        sample_rows = sb("sample_rows", [B, 6, DC])
        sv = place(m, m.BESIDE_ZS + 2 * L * L + CT * TT, 5, N)
        sval = sb("sval", [P, 32])
        free = m.zs[:].rearrange("p s t -> p (s t)")
        st, st_p, st_q = (free[:, i * 32 * N:(i + 1) * 32 * N].rearrange("p (v k) -> p v k", k=N) for i in range(3))
        s_a = sb("s_a", [P, 32])
        s_y = sb("s_y", [P, 32])
        sq = place(m, m.BESIDE_ZS + 2 * L * L, CT, TT)
        scale = sb("ln_scale", [P, TT])
        pa = ps("pa", [P, 2, TM, CT, L])
        big = ps("big3", [P, 2, 1024])
        psv = ps("psv", [P, 2, 512])

        mask = sb("mask", [P, 3, L])
        pin = big[:, 0, :].rearrange("p (b n) -> p b n", b=2)[:, :, 0:CT * 3 * L].rearrange("p b (i a t) -> p b i a t", i=CT, a=3)

        inside_done = sem("inside_done")
        inside_taken = sem("inside_taken")
        pairs_done = sem("pairs_done")
        pairs_taken = sem("pairs_taken")
        lower_stored = sem("lower_stored")
        sys_loaded = sem("sys_loaded")
        solved = sem("solved")
        inverse_cleared = sem("inverse_cleared")
        sol_stored = sem("sol_stored")
        sol_loaded = sem("sol_loaded")
        sample_turned = sem("sample_turned")
        sample_copied = sem("sample_copied")
        sample_stored = sem("sample_stored")
        sample_loaded = sem("sample_loaded")
        state_loaded = sem("state_loaded")
        outer_done = sem("outer_done")
        reduced = sem("reduced")
        y_stored = sem("y_stored")
        y_loaded = sem("y_loaded")
        mean_done = sem("mean_done")
        centred = sem("centred")
        squared = sem("squared")
        var_done = sem("var_done")
        rooted = sem("rooted")
        root_inverted = sem("root_inverted")
        scaled = sem("scaled")
        gated = sem("gated")
        sample_state_stored = sem("sample_state_stored")

        with nc.Block() as block:
            @block.tensor
            def _(pe):
                for odd in range(2):
                    rows = slice(N * odd, N * odd + N)
                    for j in range(TM):
                        for c in range(CM):
                            t = slice(j * P + L * c, j * P + L * (c + 1))
                            q = slice(L * c, L * (c + 1))
                            for i in range(CT):
                                last = nc.tensor.matmul(pa[q, odd, j, i, :], m.read_decayed[rows, i, j, 0, q], m.b_grown[rows, i, t],
                                                        start=True, stop=True)
                    last.then_inc(pairs_done, 1)
                for s in range(6):
                    if s >= 2:
                        pe.wait_ge(sample_copied, s - 1)
                    for i in range(CT):
                        last = nc.tensor.transpose(psv[0:B, s % 2, i * P:(i + 1) * P], m.sample_vec[:, s, i, :], m.ident[:])
                    last.then_inc(sample_turned, 1)
                for b in range(2):
                    for i in range(CT):
                        last = nc.tensor.matmul(banks(big[:, 0, :])[:, b, :], m.ones_mean[:], halves(m.conv[:, i, :])[:, b, :],
                                                start=(i == 0), stop=(i == CT - 1))
                last.then_inc(mean_done, 1)
                pe.wait_ge(squared, 1)
                for b in range(2):
                    for i in range(CT):
                        last = nc.tensor.matmul(banks(big[:, 1, :])[:, b, :], m.ones_mean[:], halves(sq[:, i, :])[:, b, :],
                                                start=(i == 0), stop=(i == CT - 1))
                last.then_inc(var_done, 1)
                for j in range(TM):
                    for odd in range(2):
                        g = 2 * j + odd
                        if g >= 2:
                            pe.wait_ge(inside_taken, g - 1)
                        r = slice(N * odd, N * odd + N)
                        for c in range(CM):
                            t = slice(j * P + L * c, j * P + L * (c + 1))
                            q = slice(L * c, L * (c + 1))
                            for i in range(CT):
                                nc.tensor.matmul(pin[q, odd, i, 0:2, :], m.k_grown[r, i, t], m.read_decayed[r, i, j, :, q], start=True, stop=True)
                                last = nc.tensor.matmul(pin[q, odd, i, 2, :], m.b_grown[r, i, t], m.read_decayed[r, i, j, 1, q], start=True, stop=True)
                        last.then_inc(inside_done, 1)

            @block.sync
            def _(sp):
                sp.dma_start(st.rearrange("p v k -> p (v k)"), m.state_wkv).then_inc(state_loaded, 16)
                sp.wait_ge(pairs_taken, 2)
                sp.dma_start(m.scr_lower.rearrange("(s c) (t j) -> (c t) s j", c=CM, j=L), lower[:]).then_inc(lower_stored, 16)
                sp.wait_ge(sample_copied, 6)
                sp.dma_start(m.scr_sample.rearrange("s b c -> b s c"), sample_rows[:]).then_inc(sample_stored, 16)
                sp.wait_ge(lower_stored, 16)
                sp.dma_start(sys_n[:].rearrange("p t j -> p (t j)"), m.scr_lower).then_inc(sys_loaded, 16)
                sp.wait_ge(sample_stored, 16)
                for half in range(2):
                    sp.dma_start(sv[half::2, :, :], m.scr_sample[0:5].rearrange("s b (h n) -> (b h) s n", n=N)).then_inc(sample_loaded, 16)
                sp.dma_start(sval[:], m.scr_sample[5].rearrange("b (h two v) -> (b h two) v", two=2, v=32)).then_inc(sample_loaded, 16)
                sp.wait_ge(outer_done, 4)
                sp.dma_start(m.new_wkv_s, st.rearrange("p v k -> p (v k)")).then_inc(sample_state_stored, 16)
                sp.wait_ge(reduced, 2)
                sp.dma_start(m.scr_y.rearrange("b (h two v) -> (b h two) v", two=2, v=32), s_y[:]).then_inc(y_stored, 16)
                sp.wait_ge(y_stored, 16)
                sp.dma_start(m.y_sample_rows[:], m.scr_y).then_inc(y_loaded, 16)
                sp.wait_ge(solved, 1)
                sp.dma_start(m.scr_solved, sol_t[:].rearrange("p j t -> p (j t)")).then_inc(sol_stored, 16)
                sp.wait_ge(sol_stored, 16)
                sp.wait_ge(inverse_cleared, 1)
                for c in range(CM):
                    sp.dma_start(m.inverse[L * c:L * (c + 1), :, L * c:L * (c + 1)],
                                 m.scr_solved.rearrange("(s c) (j t) -> c j s t", c=CM, j=L)[c]).then_inc(sol_loaded, 16)
                sp.wait_ge(sol_loaded, 16 * CM)
                sp.wait_ge(y_loaded, 16)
                sp.wait_ge(sample_state_stored, 16)

            @block.scalar
            def _(act):
                for s in range(6):
                    act.wait_ge(sample_turned, s + 1)
                    nc.scalar.copy(sample_rows[:, s, :], psv[0:B, s % 2, :]).then_inc(sample_copied, 1)
                act.wait_ge(centred, 1)
                for i in range(CT):
                    last = nc.scalar.activation(sq[:, i, :], m.conv[:, i, :], ACT.Square)
                last.then_inc(squared, 1)
                act.wait_ge(var_done, 1)
                nc.scalar.activation(halves(scale[:]), banks(big[:, 1, :]), ACT.Sqrt, bias=m.eps_ln[:]).then_inc(rooted, 1)
                act.wait_ge(scaled, 1)
                for i in range(CT):
                    last = nc.scalar.activation(sq[:, i, :], m.conv[:, i, :], ACT.Sigmoid,
                                                scale=m.params[:, i, par("conv_ln_g"):par("conv_ln_g") + 1],
                                                bias=m.params[:, i, par("conv_ln_b"):par("conv_ln_b") + 1])
                last.then_inc(gated, 1)

            @block.gpsimd
            def _(pool):
                ch = Chain(pool, m.pool_step, m.pool_count)
                keys = lambda s: sv[:, s, :].unsqueeze(1).broadcast_to([P, 32, N])
                values = lambda ap: ap.unsqueeze(2).broadcast_to([P, 32, N])
                nc.gpsimd.memset(m.inverse[:], 0.0).then_inc(inverse_cleared, 1)
                pool.wait_ge(state_loaded, 16)
                pool.wait_ge(sample_loaded, 48)
                nc.gpsimd.tensor_tensor(st_p, st, keys(1), ALU.mult).then_inc(outer_done, 1)
                ch.link(nc.gpsimd.tensor_tensor(st_q, values(sval[:]), keys(3), ALU.mult))
                ch.link(nc.gpsimd.tensor_tensor(st, st, keys(0), ALU.mult))
                ch.link(nc.gpsimd.tensor_tensor(st, st, st_q, ALU.add))
                pool.wait_ge(reduced, 1)
                nc.gpsimd.tensor_tensor(st_q, values(s_a[:]), keys(2), ALU.mult).then_inc(outer_done, 1)
                pool.wait_ge(outer_done, 2)
                nc.gpsimd.tensor_tensor(st, st, st_q, ALU.add).then_inc(outer_done, 1)
                pool.wait_ge(outer_done, 3)
                nc.gpsimd.tensor_tensor(st_p, st, keys(4), ALU.mult).then_inc(outer_done, 1)
                pool.wait_ge(root_inverted, 1)
                for i in range(CT):
                    last = nc.gpsimd.tensor_tensor(m.conv[:, i, :], m.conv[:, i, :], scale[:], ALU.mult)
                last.then_inc(scaled, 1)
                pool.wait_ge(scaled, 1)
                pool.wait_ge(gated, 1)
                for i in range(CT):
                    ch.link(nc.gpsimd.tensor_scalar(m.conv[:, i, :], m.conv[:, i, :],
                                                    m.params[:, i, par("conv_ln_g"):par("conv_ln_g") + 1],
                                                    m.params[:, i, par("conv_ln_b"):par("conv_ln_b") + 1], ALU.mult, ALU.add))
                    nc.gpsimd.tensor_tensor(m.conv[:, i, :], m.conv[:, i, :], sq[:, i, :], ALU.mult)

            @block.vector
            def _(dve):
                ch = Chain(dve, m.vector_step, m.vector_count)
                for c in range(CM):
                    q = slice(L * c, L * (c + 1))
                    last = nc.vector.tensor_copy(mask[q], m.inside_mask[q, :, q])
                ch.link(last)
                for odd in range(2):
                    dve.wait_ge(pairs_done, odd + 1)
                    nc.vector.tensor_tensor(lower[:, odd::2, :], pa[:, odd].rearrange("p j i t -> p (j i) t"),
                                            m.below[:].unsqueeze(1).broadcast_to([P, TM * CT, L]), ALU.mult).then_inc(pairs_taken, 1)
                ch.link(nc.vector.memset(sol_t[:], 0.0))
                ch.link(nc.vector.memset(sol_t[:].rearrange("p j t -> p (j t)")[:, 0:L * L:L + 1], 1.0))
                dve.wait_ge(mean_done, 1)
                for i in range(CT):
                    last = nc.vector.tensor_tensor(halves(m.conv[:, i, :]), halves(m.conv[:, i, :]), banks(big[:, 0, :]), ALU.subtract)
                last.then_inc(centred, 1)
                dve.wait_ge(sys_loaded, 16)
                for t in range(1, L):
                    if t == 16:
                        dve.wait_ge(rooted, 1)
                        nc.vector.reciprocal(scale[:], scale[:]).then_inc(root_inverted, 1)
                    if t == 10:
                        dve.wait_ge(outer_done, 1)
                        nc.vector.tensor_reduce(s_a[:], st_p, AX, ALU.add).then_inc(reduced, 1)
                    if t in MASK_STEPS:
                        j = MASK_STEPS.index(t)
                        for odd in range(2):
                            dve.wait_ge(inside_done, 2 * j + odd + 1)
                            nc.vector.tensor_tensor(m.inside[j][:, odd::2], pin[:, odd], mask[:].unsqueeze(1).broadcast_to([P, CT, 3, L]),
                                                    ALU.mult).then_inc(inside_taken, 1)
                    if t == 28:
                        dve.wait_ge(outer_done, 4)
                        nc.vector.tensor_reduce(s_y[:], st_p, AX, ALU.add).then_inc(reduced, 1)
                    pr = prod[:, 0:t * t].rearrange("p (j s) -> p j s", j=t)
                    ch.link(nc.vector.tensor_tensor(pr, sol_t[:, 0:t, 0:t], sys_n[:, t, 0:t].unsqueeze(1).broadcast_to([P, t, t]), ALU.mult))
                    last = nc.vector.tensor_reduce(sol_t[:, 0:t, t], pr, AX, ALU.add)
                    if t < L - 1:
                        ch.link(last)
                last.then_inc(solved, 1)


def recur(nc, m, ctx_out):
    with ExitStack() as ctx:
        def sb(name, shape, dt=F32):
            return ctx.enter_context(nc.sbuf_tensor(name, shape, dt))

        def ps(name, shape, dt=F32):
            return ctx.enter_context(nc.psum_tensor(name, shape, dt))

        def sem(name):
            return ctx_out.enter_context(nc.semaphore(name))

        pushed = sb("pushed", [P, DC])
        w2 = place(m, m.UPPER + KD * FE, 2, DC)
        w1_t = place(m, m.BESIDE_ROWS, 2, CT, P)
        u = place(m, m.UPPER + KD * FE + 2 * DC, 2, DC)
        state = sb("state", [P, 2, CT, N])
        y = place(m, m.UPPER + KD * FE + 4 * DC, 2, DC)
        y_sq = sb("y_sq", [P, DC])
        o = sb("o", [P, 3, DC])
        stat = sb("stat", [P, 4, H])
        gn_g = sb("gn_g", [P, DC])
        gn_b = sb("gn_b", [P, DC])
        state_rows = w2[0:N, TM % 2, :].rearrange("v (h k) -> v h k", h=H)
        pw = ps("pw", [P, 2, 512])
        pu = ps("pu", [P, 2, 2, CT, N])
        pst = ps("pst", [P, CT, P])
        py = ps("py", [P, 512])

        gn_loaded = sem("gn_loaded")
        push_done = sem("push_done")
        push_taken = sem("push_taken")
        w2_done = sem("w2_done")
        w2_taken = sem("w2_taken")
        w1_done = sem("w1_done")
        w1_taken = sem("w1_taken")
        u_done = sem("u_done")
        u_taken = sem("u_taken")
        state_done = sem("state_done")
        state_ready = sem("state_ready")
        y_state_done = sem("y_state_done")
        y_done = sem("y_done")
        y_taken = sem("y_taken")
        y_state_taken = sem("y_state_taken")
        rooted = sem("gn_rooted")
        gn_var_ready = sem("gn_var_ready")
        gn_squared = sem("gn_squared")
        centred = sem("gn_centred")
        normed = sem("gn_normed")
        o_ready = sem("o_ready")
        o_turned = sem("o_turned")
        o_taken = sem("o_taken")
        final_turned = sem("final_turned")
        final_ready = sem("final_ready")
        final_stored = sem("final_stored")

        def rows(h):
            return slice(N * (h % 2), N * (h % 2) + N)

        with nc.Block() as block:
            @block.gpsimd
            def _(pool):
                for spent in m.spent:
                    pool.sem_clear(spent)
                ch = Chain(pool, m.pool_step, m.pool_count)
                tt = nc.gpsimd.tensor_tensor
                pool.wait_ge(gn_loaded, 32)
                for i, (_, n) in enumerate(TOK_TILES):
                    yi, oi = y[0:n, i % 2, :], o[0:n, i % 3, :]
                    by_head = lambda ap: ap.rearrange("p (h c) -> p h c", h=H)
                    if i >= 3:
                        pool.wait_ge(o_turned, i - 2)
                    ch.link(tt(by_head(oi), by_head(m.v_rows[0:n, i, :]), m.bonus[0:n, i, :].unsqueeze(2).broadcast_to([n, H, N]), ALU.mult))
                    pool.wait_ge(normed, i + 1)
                    ch.link(tt(yi, yi, gn_g[0:n, :], ALU.mult))
                    ch.link(tt(yi, yi, gn_b[0:n, :], ALU.add))
                    ch.link(tt(oi, oi, yi, ALU.add))
                    tt(oi, oi, m.gate[0:n, i, :], ALU.mult).then_inc(o_ready, 1)

            @block.sync
            def _(sp):
                sp.dma_start(gn_g[:], m.vec["gn_g"].broadcast_to([P, DC])).then_inc(gn_loaded, 16)
                sp.dma_start(gn_b[:], m.vec["gn_b"].broadcast_to([P, DC])).then_inc(gn_loaded, 16)
                sp.dma_start(m.w_out_half[0][:], m.w_out[:, 0:512].rearrange("(k p) n -> p k n", p=P)).then_inc(m.w_out_loaded[0], 16)
                for i in range(2):
                    sp.dma_start(m.x_again[:, i, :], m.x_prompt[i * P:(i + 1) * P, :]).then_inc(m.x_again_loaded[i], 16)
                sp.wait_ge(final_ready, 2)
                sp.dma_start(m.new_wkv_p.rearrange("h v k -> v h k"), state_rows).then_inc(final_stored, 16)
                sp.wait_ge(final_stored, 16)

            @block.tensor
            def _(pe):
                def push_first(j):
                    if j >= 1:
                        pe.wait_ge(w2_taken, j)
                    for h in range(H):
                        for c in range(CM):
                            q, hc = slice(L * c, L * (c + 1)), slice(h * N, (h + 1) * N)
                            last = nc.tensor.matmul(pw[q, 0, hc], m.inside[j][q, h, 0, :], m.v_rows[q, j, hc], start=True, stop=True)
                    last.then_inc(push_done, 1)
                    if j >= 1:
                        pe.wait_ge(w1_taken, j)
                    for h in range(H):
                        last = nc.tensor.matmul(pw[rows(h), 1, (h // 2) * P:(h // 2 + 1) * P], m.a_rows[:, j, h * N:(h + 1) * N],
                                                m.inverse[:, H * j + h, :], start=True, stop=True)
                    last.then_inc(w1_done, 1)

                def push_second(j):
                    pe.wait_ge(push_taken, j + 1)
                    for h in range(H):
                        last = nc.tensor.matmul(pw[:, 0, h * N:(h + 1) * N], m.inverse[:, H * j + h, :], pushed[:, h * N:(h + 1) * N],
                                                start=True, stop=True)
                    last.then_inc(w2_done, 1)

                def outputs_inside(j):
                    if j >= 1:
                        pe.wait_ge(y_taken, j)
                    for h in range(H):
                        hc = slice(h * N, (h + 1) * N)
                        for c in range(CM):
                            q = slice(L * c, L * (c + 1))
                            nc.tensor.matmul(py[q, hc], m.inside[j][q, h, 1, :], m.v_rows[q, j, hc], start=True, stop=False)
                        for c in range(CM):
                            q = slice(L * c, L * (c + 1))
                            last = nc.tensor.matmul(py[q, hc], m.inside[j][q, h, 2, :], u[q, j % 2, hc], start=False, stop=True)
                    last.then_inc(y_done, 1)

                push_first(0)
                push_second(0)
                for j in range(TM):
                    for c in range(CM):
                        n = CM * j + c
                        q = slice(L * c, L * (c + 1))
                        pe.wait_ge(w1_taken, j + 1)
                        pe.wait_ge(state_ready, n + 1)
                        if n >= 1:
                            pe.wait_ge(u_taken, n)
                        if c == 0 and j >= 1:
                            pe.wait_ge(y_state_taken, j)
                        for h in range(H):
                            last = nc.tensor.matmul(pu[q, h % 2, 0, h // 2, :], w1_t[rows(h), j % 2, h // 2, q],
                                                    state[rows(h), n % 2, h // 2, :], start=True, stop=True)
                        last.then_inc(u_done, 1)
                        for h in range(H):
                            hc = slice(h * N, (h + 1) * N)
                            nc.tensor.matmul(pst[rows(h), h // 2, N:], m.k_rows[q, j, hc], m.v_rows[q, j, hc], start=True, stop=True)
                        if c == 0 and j >= 1:
                            outputs_inside(j - 1)
                        if j + 1 < TM and c == CM - 1:
                            push_first(j + 1)
                        pe.wait_ge(u_taken, n + 1)
                        for h in range(H):
                            hc = slice(h * N, (h + 1) * N)
                            last = nc.tensor.matmul(pst[rows(h), h // 2, 0:N], m.b_rows[q, j, hc], u[q, j % 2, hc], start=True, stop=True)
                        last.then_inc(state_done, 1)
                        for h in range(H):
                            last = nc.tensor.matmul(pu[q, h % 2, 1, h // 2, :], m.read_decayed[rows(h), h // 2, j, 1, q],
                                                    state[rows(h), n % 2, h // 2, :], start=True, stop=True)
                        last.then_inc(y_state_done, 1)
                    if j + 1 < TM:
                        push_second(j + 1)
                outputs_inside(TM - 1)
                pe.wait_ge(state_ready, NCH + 1)
                pe.wait_ge(u_taken, NCH)
                pe.wait_ge(y_state_taken, TM)
                for h in range(H):
                    last = nc.tensor.transpose(pu[0:N, h % 2, 0, h // 2, :], state[rows(h), NCH % 2, h // 2, :], m.ident[rows(h), rows(h)])
                last.then_inc(final_turned, 1)
                for i, (t0, n) in enumerate(TOK_TILES):
                    pe.wait_ge(o_ready, i + 1)
                    pe.wait_ge(w1_taken, TM)
                    if i >= 1:
                        pe.wait_ge(o_taken, i)
                    for k in range(CT):
                        last = nc.tensor.transpose(pw[:, 1, k * P:k * P + n], o[0:n, i % 3, k * P:(k + 1) * P], m.ident[0:n, 0:n])
                    last.then_inc(o_turned, 1)

            @block.scalar
            def _(act):
                def copy_pushed(j):
                    act.wait_ge(push_done, j + 1)
                    nc.scalar.copy(pushed[:], pw[:, 0, :]).then_inc(push_taken, 1)
                    act.wait_ge(w1_done, j + 1)
                    nc.scalar.copy(w1_t[:, j % 2, :, :], pw[:, 1, :].rearrange("p (i t) -> p i t", i=CT)).then_inc(w1_taken, 1)

                def copy_w2(j):
                    act.wait_ge(w2_done, j + 1)
                    nc.scalar.copy(w2[:, j % 2, :], pw[:, 0, :]).then_inc(w2_taken, 1)

                def norm_part(i, n):
                    act.wait_ge(centred, i + 1)
                    nc.scalar.activation(y_sq[0:n, :], y[0:n, i % 2, :], ACT.Square).then_inc(gn_squared, 1)
                    act.wait_ge(gn_var_ready, i + 1)
                    nc.scalar.activation(stat[0:n, 2, :], stat[0:n, 1, :], ACT.Sqrt, scale=1.0 / N, bias=m.eps_gn[0:n, :]).then_inc(rooted, 1)

                copy_pushed(0)
                copy_w2(0)
                for j in range(TM):
                    if j >= 1:
                        norm_part(j - 1, P)
                    if j + 1 < TM:
                        copy_pushed(j + 1)
                    act.wait_ge(y_state_done, CM * (j + 1))
                    if j >= 2:
                        act.wait_ge(o_ready, j - 1)
                    nc.scalar.copy(y[:, j % 2, :].rearrange("p (i two c) -> p two i c", two=2, c=N), pu[:, :, 1, :, :]).then_inc(y_state_taken, 1)
                    if j + 1 < TM:
                        copy_w2(j + 1)
                act.wait_ge(final_turned, 1)
                nc.scalar.copy(state_rows.rearrange("v (i two) k -> v two i k", two=2), pu[0:N, :, 0, :, :]).then_inc(final_ready, 2)

                def copy_out(i):
                    t0, n = TOK_TILES[i]
                    act.wait_ge(o_turned, i + 1)
                    nc.scalar.copy(m.o_t[:, :, t0:t0 + n],
                                   pw[:, 1, :].rearrange("p (k t) -> p k t", k=CT)[:, :, 0:n]).then_inc(o_taken, 1)

                norm_part(TM - 1, P)
                for i in range(TM - 2):
                    copy_out(i)
                norm_part(TM, B)
                for i in range(TM - 2, NT):
                    copy_out(i)

            @block.vector
            def _(dve):
                ch = Chain(dve, m.vector_step, m.vector_count)

                def centre(i, n):
                    b = i % 2
                    yv = y[0:n, b, :].rearrange("p (h c) -> p h c", h=H)
                    if i < TM:
                        dve.wait_ge(y_state_taken, i + 1)
                        dve.wait_ge(y_done, i + 1)
                        nc.vector.tensor_tensor(y[:, b, :], y[:, b, :], py[:], ALU.add).then_inc(y_taken, 1)
                        dve.wait_ge(y_taken, i + 1)
                    else:
                        dve.wait_ge(o_ready, i - 1)
                        ch.link(nc.vector.tensor_copy(y[0:B, b, :], m.y_sample_rows[:]))
                    ch.link(nc.vector.tensor_reduce(stat[0:n, 0, :], yv, AX, ALU.add))
                    ch.link(nc.vector.tensor_scalar(stat[0:n, 0, :], stat[0:n, 0, :], 1.0 / N, None, ALU.mult))
                    nc.vector.tensor_tensor(yv, yv, stat[0:n, 0, :].unsqueeze(2).broadcast_to([n, H, N]), ALU.subtract).then_inc(centred, 1)

                def normalise(i, n):
                    yv = y[0:n, i % 2, :].rearrange("p (h c) -> p h c", h=H)
                    dve.wait_ge(gn_squared, i + 1)
                    nc.vector.tensor_reduce(stat[0:n, 1, :], y_sq[0:n, :].rearrange("p (h c) -> p h c", h=H), AX, ALU.add).then_inc(gn_var_ready, 1)
                    dve.wait_ge(rooted, i + 1)
                    ch.link(nc.vector.reciprocal(stat[0:n, 3, :], stat[0:n, 2, :]))
                    nc.vector.tensor_tensor(yv, yv, stat[0:n, 3, :].unsqueeze(2).broadcast_to([n, H, N]), ALU.mult).then_inc(normed, 1)

                nc.vector.memset(state[:, 0, :, :], 0.0).then_inc(state_ready, 1)
                for j in range(TM):
                    for c in range(CM):
                        n = CM * j + c
                        q = slice(L * c, L * (c + 1))
                        dve.wait_ge(w2_taken, j + 1)
                        if j >= 2:
                            dve.wait_ge(y_done, j - 1)
                        dve.wait_ge(u_done, n + 1)
                        by_parity = lambda ap: ap.rearrange("p (i two c) -> p two i c", two=2, c=N)
                        nc.vector.tensor_tensor(by_parity(u[q, j % 2, :]), pu[q, :, 0, :, :], by_parity(w2[q, j % 2, :]),
                                                ALU.add).then_inc(u_taken, 1)
                        if n >= 1:
                            dve.wait_ge(y_state_done, n)
                        dve.wait_ge(state_ready, n + 1)
                        ch.link(nc.vector.tensor_tensor(state[:, (n + 1) % 2, :, :], state[:, n % 2, :, :],
                                                        m.chunk_decay[:, :, n:n + 1].broadcast_to([P, CT, N]), ALU.mult))
                        dve.wait_ge(state_done, n + 1)
                        ch.link(nc.vector.tensor_tensor(state[:, (n + 1) % 2, :, :], state[:, (n + 1) % 2, :, :], pst[:, :, 0:N], ALU.add))
                        nc.vector.tensor_tensor(state[:, (n + 1) % 2, :, :], state[:, (n + 1) % 2, :, :], pst[:, :, N:],
                                                ALU.add).then_inc(state_ready, 1)
                        if j >= 1 and c == 1:
                            centre(j - 1, P)
                        if j >= 1 and c == 2:
                            normalise(j - 1, P)
                for i, n in ((TM - 1, P), (TM, B)):
                    centre(i, n)
                    normalise(i, n)


def mix(nc, m, ctx_out):
    BIG = 1e30
    GONE = -3e38
    with ExitStack() as ctx:
        def sb(name, shape, dt=F32):
            return ctx.enter_context(nc.sbuf_tensor(name, shape, dt))

        def ps(name, shape, dt=F32):
            return ctx.enter_context(nc.psum_tensor(name, shape, dt))

        def sem(name):
            return ctx_out.enter_context(nc.semaphore(name))

        w_out = m.w_out_half
        x_rows = m.x_again
        x1 = sb("x1", [P, NT, D])
        x1_t = sb("x1_t", [P, KD, TT])
        ln_g = place(m, m.UPPER + 3 * KD * FE, D)
        ln_b = place(m, m.UPPER + 3 * KD * FE + D, D)
        router_w = sb("router_w_sb", [P, KD, E])
        router_b = sb("router_b", [P, E])
        sh_w = sb("sh_w", [P, 2, KD, FE])
        sh_d = sb("sh_d", [P, 2, D])
        sh_sig = sb("sh_sig", [P, TT])
        sh_gate = m.conv[:, 0, :]
        sh_h = sb("sh_h", [P, 2, TT])
        stats = sb("stats", [P, 2, 6])
        aggr = sb("aggr", [P, 4])
        scores = sb("scores", [P, NT, E])
        sel = sb("sel", [P, NT, E])
        top = sb("top", [P, NT * G, 8])
        grp = sb("grp", [P, NT, G])
        gt = sb("gt", [P, NT, G, G])
        eq = sb("eq", [P, NT, G, G])
        keep = sb("keep", [P, NT, G])
        hit = sb("hit", [P, NT, E])
        gsum = sb("gsum", [P, NT])
        before = sb("before", [P, P])
        first = sb("first", [P, G, G])
        f0 = sb("f0", [P, 2, D])
        cnt = m.cnt
        ph = ps("ph", [P, 2, 1024])
        pt = ps("pt5", [P, 2, 512])
        plog = ps("plog", [P, NT, E])
        ppos = ps("ppos", [P, NT + 1, E])

        loaded = sem("mix_loaded")
        x_loaded = m.x_again_loaded
        ln_loaded = sem("ln1_loaded")
        sh_loaded = sem("sh_loaded")
        mixed = sem("mixed")
        mixed_taken = sem("mixed_taken")
        var_ready = sem("var_ready")
        rooted = sem("ln1_rooted")
        x1_ready = sem("x1_ready")
        x1_turned = sem("x1_turned")
        x1_t_ready = sem("x1_t_ready")
        x1_stored = sem("x1_stored")
        logits_done = sem("logits_done")
        scores_ready = sem("scores_ready")
        hits_ready = sem("hits_ready")
        positions_done = sem("positions_done")
        routing_consts = sem("routing_consts")
        sh_done = sem("sh_done")
        sh_sig_ready = sem("sh_sig_ready")
        sh_up_ready = sem("sh_up_ready")
        sh_h_ready = sem("sh_h_ready")
        f_done = sem("f_done")
        f_taken = sem("f_taken")
        f_stored = [sem(f"f_stored{i}") for i in range(2)]
        x_used = sem("x_used")

        with nc.Block() as block:
            @block.sync
            def _(sp):
                sp.dma_start(w_out[1][:], m.w_out[:, 512:1024].rearrange("(k p) n -> p k n", p=P)).then_inc(m.w_out_loaded[1], 16)
                sp.dma_start(ln_g[:], m.vec["ln1_g"].broadcast_to([P, D])).then_inc(ln_loaded, 16)
                sp.dma_start(ln_b[:], m.vec["ln1_b"].broadcast_to([P, D])).then_inc(ln_loaded, 16)
                sp.dma_start(router_w[:], m.router_w.rearrange("(k p) n -> p k n", p=P)).then_inc(loaded, 16)
                sp.dma_start(router_b[:], m.vec["router_bias"].broadcast_to([P, E])).then_inc(loaded, 16)
                sp.dma_start(sh_w[:, 0], m.sh_gate.rearrange("(k p) n -> p k n", p=P)).then_inc(sh_loaded, 16)
                sp.dma_start(sh_w[:, 1], m.sh_up.rearrange("(k p) n -> p k n", p=P)).then_inc(sh_loaded, 16)
                sp.dma_start(sh_d[:], m.sh_down.rearrange("(k p) n -> p k n", p=P)).then_inc(sh_loaded, 16)
                for i in range(2, NT):
                    t0, n = TOK_TILES[i]
                    sp.wait_ge(x_used, i - 1)
                    src = m.x_prompt[t0:t0 + n, :] if i < TM else m.x_sample
                    sp.dma_start(x_rows[0:n, i % 2, :], src).then_inc(x_loaded[i % 2], 16)
                for job in range(2):
                    load_expert(sp, m, job, job)
                for i, (t0, n) in enumerate(TOK_TILES):
                    sp.wait_ge(x1_ready, i + 1)
                    sp.dma_start(m.scr_x1[t0:t0 + n, :], x1[0:n, i, :]).then_inc(x1_stored, 16)
                sp.dma_start(m.scr_f[TT:TT + CAP, :], x1[0:CAP, 0, :]).then_inc(x1_stored, 16)
                sp.dma_start(m.scr_x1[TT:TT + CAP, :], x1[0:CAP, 0, :]).then_inc(x1_stored, 16)
                for job in range(2, NB):
                    load_expert(sp, m, job, job)
                for i, (t0, n) in enumerate(TOK_TILES):
                    sp.wait_ge(f_taken, 2 * (i + 1))
                    sp.dma_start(m.scr_f[t0:t0 + n, :], f0[0:n, i % 2, :]).then_inc(f_stored[i % 2], 16)
                sp.wait_ge(x1_stored, 16 * (NT + 2))
                sp.wait_ge(f_stored[0], 16 * 3)
                sp.wait_ge(f_stored[1], 16 * 2)

            @block.tensor
            def _(pe):
                def turn(i):
                    t0, n = TOK_TILES[i]
                    pe.wait_ge(x1_ready, i + 1)
                    for half in range(2):
                        g = 2 * i + half
                        if g >= 2:
                            pe.wait_ge(x1_t_ready, g - 1)
                        for k in range(4):
                            d0 = (4 * half + k) * P
                            last = nc.tensor.transpose(pt[:, half, k * P:k * P + n], x1[0:n, i, d0:d0 + P], m.ident[0:n, 0:n])
                        last.then_inc(x1_turned, 1)

                def logits(i):
                    t0, n = TOK_TILES[i]
                    pe.wait_ge(x1_t_ready, 2 * (i + 1))
                    for k in range(KD):
                        last = nc.tensor.matmul(plog[0:n, i, :], x1_t[:, k, t0:t0 + n], router_w[:, k, :], start=(k == 0), stop=(k == KD - 1))
                    if i == NT - 1:
                        last.then_inc(logits_done, 1)

                def shared_in(j, part, b):
                    for k in range(KD):
                        last = nc.tensor.matmul(banks(ph[:, 1 - part, :])[:, b, :], sh_w[:, part, k, j * P:(j + 1) * P],
                                                halves(x1_t[:, k, :])[:, b, :], start=(k == 0), stop=(k == KD - 1))
                    if b == 1:
                        last.then_inc(sh_done, 1)

                for i, (t0, n) in enumerate(TOK_TILES):
                    if i >= 2:
                        pe.wait_ge(mixed_taken, i - 1)
                    for c in range(2):
                        if i == 0:
                            pe.wait_ge(m.w_out_loaded[c], 16)
                        for k in range(KD):
                            lhs = m.conv[:, k, t0:t0 + n] if k < CT else m.o_t[:, k - CT, t0:t0 + n]
                            last = nc.tensor.matmul(ph[0:n, i % 2, c * 512:(c + 1) * 512], lhs, w_out[c][:, k, :],
                                                    start=(k == 0), stop=(k == KD - 1))
                    last.then_inc(mixed, 1)
                    if i >= 1:
                        turn(i - 1)
                    if i == 1:
                        pe.wait_ge(loaded, 16 * 2)
                    if i >= 2:
                        logits(i - 2)
                pe.wait_ge(sh_loaded, 16 * 3)
                pe.wait_ge(x1_t_ready, 2 * (HALF // P + 1))
                for part in range(2):
                    pe.wait_ge(mixed_taken, NT - 1 + part)
                    shared_in(0, part, 0)
                turn(NT - 1)
                logits(NT - 2)
                logits(NT - 1)
                for part in range(2):
                    shared_in(0, part, 1)
                pe.wait_ge(sh_up_ready, 1)
                for part in range(2):
                    for b in range(2):
                        shared_in(1, part, b)
                pe.wait_ge(sh_h_ready, 2)
                pe.wait_ge(hits_ready, 1)
                pe.wait_ge(routing_consts, 2)
                for i in range(NT):
                    for j in range(i + 1):
                        last = nc.tensor.matmul(ppos[:, i, :], before[:] if j == i else m.ones[:], hit[:, j, :], start=(j == 0), stop=(j == i))
                for j in range(NT):
                    last = nc.tensor.matmul(ppos[:, NT, :], m.ones[:], hit[:, j, :], start=(j == 0), stop=(j == NT - 1))
                last.then_inc(positions_done, 1)
                for i, (t0, n) in enumerate(TOK_TILES):
                    if i >= 2:
                        pe.wait_ge(f_taken, 2 * (i - 1))
                    for c in range(2):
                        for j in range(2):
                            last = nc.tensor.matmul(ph[0:n, i % 2, c * 512:(c + 1) * 512], sh_h[:, j, t0:t0 + n], sh_d[:, j, c * 512:(c + 1) * 512],
                                                    start=(j == 0), stop=(j == 1))
                    last.then_inc(f_done, 1)

            @block.scalar
            def _(act):
                for i, (t0, n) in enumerate(TOK_TILES):
                    act.wait_ge(var_ready, i + 1)
                    nc.scalar.activation(aggr[0:n, 2:3], aggr[0:n, 1:2], ACT.Sqrt, bias=m.eps_ln[0:n, :]).then_inc(rooted, 1)
                    for half in range(2):
                        act.wait_ge(x1_turned, 2 * i + half + 1)
                        nc.scalar.copy(x1_t[:, 4 * half:4 * half + 4, t0:t0 + n],
                                       pt[:, half, :].rearrange("p (k t) -> p k t", k=4)[:, :, 0:n]).then_inc(x1_t_ready, 1)
                act.wait_ge(routing_consts, 1)
                act.wait_ge(logits_done, 1)
                nc.scalar.activation(scores[:, 0:TM, :], plog[:, 0:TM, :], ACT.Sigmoid)
                nc.scalar.activation(scores[0:B, TM, :], plog[0:B, TM, :], ACT.Sigmoid).then_inc(scores_ready, 1)
                for j in range(2):
                    act.wait_ge(sh_done, 2 * j + 1)
                    if j >= 1:
                        act.wait_ge(sh_h_ready, j)
                    nc.scalar.activation(halves(sh_sig[:]), banks(ph[:, 1, :]), ACT.Sigmoid)
                    nc.scalar.copy(halves(sh_gate), banks(ph[:, 1, :])).then_inc(sh_sig_ready, 1)
                    act.wait_ge(sh_done, 2 * j + 2)
                    nc.scalar.copy(halves(sh_h[:, j, :]), banks(ph[:, 0, :])).then_inc(sh_up_ready, 1)

            @block.gpsimd
            def _(pool):
                nc.gpsimd.memset(scores[:, TM, :], 0.0).then_inc(routing_consts, 1)
                ch = Chain(pool, m.pool_step, m.pool_count)
                nc.gpsimd.memset(before[:], 1.0)
                ch.link(nc.gpsimd.memset(first[:], 1.0))
                nc.gpsimd.affine_select(out=before[:], in_=before[:], compare_op=ALU.is_gt, fill=0.0, base=0,
                                        pattern=[[1, P]], channel_multiplier=-1)
                nc.gpsimd.affine_select(out=first[:], in_=first[:], compare_op=ALU.is_gt, fill=0.0, base=0,
                                        pattern=[[1, G], [-1, G]], channel_multiplier=0).then_inc(routing_consts, 1)
                for j in range(2):
                    pool.wait_ge(sh_sig_ready, j + 1)
                    ch.link(nc.gpsimd.tensor_tensor(sh_sig[:], sh_sig[:], sh_gate, ALU.mult))
                    pool.wait_ge(sh_up_ready, j + 1)
                    nc.gpsimd.tensor_tensor(sh_h[:, j, :], sh_sig[:], sh_h[:, j, :], ALU.mult).then_inc(sh_h_ready, 1)

            @block.vector
            def _(dve):
                ch = Chain(dve, m.vector_step, m.vector_count)

                def layer_norm(i, n):
                    r = x_rows[0:n, i % 2, :]
                    dve.wait_ge(x_loaded[i % 2], 16 * (i // 2 + 1))
                    dve.wait_ge(mixed, i + 1)
                    for c in range(2):
                        cs = slice(c * 512, (c + 1) * 512)
                        last = nc.vector.scalar_tensor_tensor(x1[0:n, i, cs], r[:, cs], ALPHA, ph[0:n, i % 2, cs], ALU.mult, ALU.add)
                    last.then_inc(mixed_taken, 1)
                    dve.wait_ge(mixed_taken, i + 1)
                    for c in range(2):
                        last = nc.vector.bn_stats(stats[0:n, c, :], x1[0:n, i, c * 512:(c + 1) * 512])
                    last.then_inc(x_used, 1)
                    dve.wait_ge(x_used, i + 1)
                    nc.vector.bn_aggr(aggr[0:n, 0:2], stats[0:n, :, :]).then_inc(var_ready, 1)
                    dve.wait_ge(var_ready, i + 1)
                    dve.wait_ge(rooted, i + 1)
                    ch.link(nc.vector.reciprocal(aggr[0:n, 3:4], aggr[0:n, 2:3]))
                    ch.link(nc.vector.tensor_scalar(x1[0:n, i, :], x1[0:n, i, :], aggr[0:n, 0:1], aggr[0:n, 3:4], ALU.subtract, ALU.mult))
                    ch.link(nc.vector.tensor_tensor(x1[0:n, i, :], x1[0:n, i, :], ln_g[0:n, :], ALU.mult))
                    nc.vector.tensor_tensor(x1[0:n, i, :], x1[0:n, i, :], ln_b[0:n, :], ALU.add).then_inc(x1_ready, 1)

                dve.wait_ge(ln_loaded, 32)
                for i, (_, n) in enumerate(TOK_TILES):
                    layer_norm(i, n)
                dve.wait_ge(scores_ready, 1)
                dve.wait_ge(routing_consts, 2)
                dve.wait_ge(loaded, 16 * 2)
                ch.link(nc.vector.tensor_tensor(sel[:], scores[:], router_b[:].unsqueeze(1).broadcast_to([P, NT, E]), ALU.add))
                sel_g = sel[:].rearrange("p i (g e) -> p (i g) e", g=G)
                for g in range(NT * G):
                    last = nc.vector.max(top[:, g, :], sel_g[:, g, :])
                ch.link(last)
                grp_f = grp[:].rearrange("p i g -> p (i g)")
                ch.link(nc.vector.tensor_tensor(grp_f, top[:, :, 0], top[:, :, 1], ALU.add))
                me = grp[:].unsqueeze(3).broadcast_to([P, NT, G, G])
                other = grp[:].unsqueeze(2).broadcast_to([P, NT, G, G])
                nc.vector.tensor_tensor(gt[:], other, me, ALU.is_gt)
                ch.link(nc.vector.tensor_tensor(eq[:], other, me, ALU.is_equal))
                ch.link(nc.vector.tensor_tensor(eq[:], eq[:], first[:].unsqueeze(1).broadcast_to([P, NT, G, G]), ALU.mult))
                ch.link(nc.vector.tensor_tensor(gt[:], gt[:], eq[:], ALU.add))
                ch.link(nc.vector.tensor_reduce(grp[:], gt[:], AX, ALU.add))
                ch.link(nc.vector.tensor_scalar(keep[:], grp[:], float(KG), None, ALU.is_lt))
                keep_f = keep[:].rearrange("p i g -> p (i g)").unsqueeze(2).broadcast_to([P, NT * G, E // G])
                ch.link(nc.vector.tensor_tensor(sel_g, sel_g, keep_f, ALU.mult))
                ch.link(nc.vector.tensor_scalar(grp[:], keep[:], 1.0, BIG, ALU.subtract, ALU.mult))
                ch.link(nc.vector.tensor_tensor(sel_g, sel_g, grp_f.unsqueeze(2).broadcast_to([P, NT * G, E // G]), ALU.add))
                for i in range(NT):
                    last = nc.vector.max(top[:, i, :], sel[:, i, :])
                ch.link(last)
                for i in range(NT):
                    last = nc.vector.match_replace(hit[:, i, :], top[:, i, :], sel[:, i, :], GONE)
                ch.link(last)
                ch.link(nc.vector.tensor_scalar(hit[:], hit[:], GONE / 2, None, ALU.is_lt))
                nc.vector.tensor_tensor(hit[:], hit[:], m.is_token[:].unsqueeze(2).broadcast_to([P, NT, E]), ALU.mult).then_inc(hits_ready, 1)
                dve.wait_ge(hits_ready, 1)
                ch.link(nc.vector.tensor_tensor(scores[:], scores[:], hit[:], ALU.mult))
                ch.link(nc.vector.tensor_reduce(gsum[:], scores[:], AX, ALU.add))
                ch.link(nc.vector.tensor_scalar(gsum[:], gsum[:], 1e-20, None, ALU.add))
                ch.link(nc.vector.reciprocal(gsum[:], gsum[:]))
                by_tile = lambda ap: ap.rearrange("p i e -> p e i")
                ch.link(nc.vector.tensor_tensor(scores[:], scores[:], gsum[:].unsqueeze(2).broadcast_to([P, NT, E]), ALU.mult))
                ch.link(nc.vector.tensor_scalar(scores[:], scores[:], ROUTED_SCALE, None, ALU.mult))
                for part in range(3):
                    col = m.table[:, :, :, 3 + part]
                    ch.link(nc.vector.tensor_copy(col, by_tile(scores[:])))
                    if part < 2:
                        ch.link(nc.vector.tensor_tensor(scores[:], scores[:], col.rearrange("p e i -> p i e"), ALU.subtract))
                nc.vector.tensor_copy(m.table[:, :, :, 0], m.tile_index[:].unsqueeze(1).broadcast_to([P, E, NT]))
                nc.vector.tensor_copy(m.table[:, :, :, 1], m.partition_index[:].unsqueeze(1).broadcast_to([P, E, NT]))
                ch.link(nc.vector.memset(m.table[:, :, :, 2], 1.0))
                dve.wait_ge(positions_done, 1)
                ch.link(nc.vector.scalar_tensor_tensor(sel[:], ppos[:, 0:NT, :], 1.0, hit[:], ALU.add, ALU.mult))
                ch.link(nc.vector.tensor_scalar(m.position[:], by_tile(sel[:]), 1.0, None, ALU.subtract))
                nc.vector.memset(cnt[:, 1:4, :], 0.0)
                ch.link(nc.vector.tensor_copy(cnt[:, 0, :], ppos[:, NT, :]))
                for b in range(1, m.MAX_JOBS):
                    ch.link(nc.vector.tensor_scalar(cnt[:, 2, :], cnt[:, 0, :], float(b * CAP), None, ALU.is_gt))
                    ch.link(nc.vector.tensor_tensor(cnt[:, 1, :], cnt[:, 1, :], cnt[:, 2, :], ALU.add))
                ch.link(nc.vector.tensor_tensor_scan(cnt[:, 2, :], m.ones[:, 0:E], cnt[:, 1, :], 0.0, ALU.mult, ALU.add))

                def residual(i):
                    n = TOK_TILES[i][1]
                    dve.wait_ge(f_done, i + 1)
                    if i >= 2:
                        dve.wait_ge(f_stored[i % 2], 16 * (i // 2))
                    for c in range(2):
                        cs = slice(c * 512, (c + 1) * 512)
                        nc.vector.scalar_tensor_tensor(f0[0:n, i % 2, cs], x1[0:n, i, cs], ALPHA, ph[0:n, i % 2, cs],
                                                       ALU.mult, ALU.add).then_inc(f_taken, 1)

                for i in range(NT):
                    residual(i)


def load_expert(sp, m, q, s):
    pick = lambda w: w[bass.ds(q, 1)].rearrange("o p n -> p (o n)")
    sp.dma_start(m.expert_gate[s][:].rearrange("p k f -> p (k f)"), pick(m.exp_gate)).then_inc(m.gate_loaded[s], 16)
    sp.dma_start(m.expert_up[s][:].rearrange("p k f -> p (k f)"), pick(m.exp_up)).then_inc(m.up_loaded[s], 16)
    sp.dma_start(m.expert_down[s][:], m.exp_down[bass.ds(q, 1)].rearrange("o p j d -> p (o j) d")).then_inc(m.down_loaded[s], 16)


def experts(nc, m, ctx_out):
    STEPS = 2 * NB
    with ExitStack() as ctx:
        def sb(name, shape, dt=F32):
            return ctx.enter_context(nc.sbuf_tensor(name, shape, dt))

        def ps(name, shape, dt=F32):
            return ctx.enter_context(nc.psum_tensor(name, shape, dt))

        def sem(name):
            return ctx_out.enter_context(nc.semaphore(name))

        member = sb("member", [P, 2, NT, CAP], BF16)
        entry = sb("entry", [CAP, STEPS, 6])
        row = sb("row", [CAP, STEPS], U32)
        spare = sb("spare", [CAP, STEPS])
        token = sb("token", [CAP, STEPS])
        weight = sb("weight", [CAP, STEPS])
        x_list = sb("x_list", [CAP, NB, D])
        x_list_t = sb("x_list_t", [P, 2, KD, CAP])
        sig = sb("sig", [P, 2, 2, CAP])
        hid = sb("hid", [P, 2, 2, CAP])
        y_list = sb("y_list", [CAP, 2, D])
        jobs3 = sb("jobs3", [P, m.EXTRA, E])
        pl = ps("pl", [P, 2, 512])
        px = ps("px", [P, 2, 512])
        pgu = ps("pgu", [P, 2, 512])
        pyl = ps("pyl", [P, 2, 512])

        member_ready = sem("member_ready")
        list_done = sem("list_done")
        entry_ready = sem("entry_ready")
        rows_ready = sem("rows_ready")
        gathered = [sem(f"gathered{i}") for i in range(NB)]
        added = [sem(f"added{i}") for i in range(2)]
        x_turned = sem("x_list_turned")
        x_ready = sem("x_list_ready")
        gu_done = sem("gu_done")
        sig_ready = sem("sig_ready")
        hid_ready = sem("hid_ready")
        y_done = sem("y_list_done")
        y_act = sem("y_act_ready")
        y_dve = sem("y_dve_ready")
        silu_ready = sem("silu_ready")
        weight_ready = sem("weight_ready")
        waits_over = sem("waits_over")
        LOOPS = E // STEPS - 1
        AHEAD = NB
        KA = 512 // CAP if 512 // CAP < KD else KD // 2

        class Job:

            def __init__(self, turn, s):
                self.q = STEPS * turn + s
                self.s = s % NB
                self.l = s % STEPS
                self.pair = STEPS // 2 * turn + s // 2
                self.before = STEPS // 2 * turn + (s + 1) // 2
                self.turn = STEPS // NB * turn + s // NB

            def has_before(self, n):
                return not isinstance(self.q, int) or self.q >= n

        def build_member(dve, job):
            q, s = job.q, job.s
            if job.has_before(2):
                dve.wait_ge(list_done, q - 1)
            src = m.position[:, bass.ds(q, 1), :].rearrange("p o i -> p (o i)")
            nc.vector.tensor_tensor(member[:, s % 2], m.slot_index[:].unsqueeze(1).broadcast_to([P, NT, CAP]),
                                    src.unsqueeze(2).broadcast_to([P, NT, CAP]), ALU.is_equal).then_inc(member_ready, 1)

        def make_list(pe, job):
            q, s = job.q, job.s
            pe.wait_ge(member_ready, q + 1)
            if job.has_before(2):
                pe.wait_ge(entry_ready, q - 1)
            for i in range(NT):
                last = nc.tensor.matmul(pl[0:CAP, s % 2, 0:6], member[:, s % 2, i, :],
                                        m.table[:, bass.ds(q, 1), i, :].rearrange("p o c -> p (o c)"),
                                        start=(i == 0), stop=(i == NT - 1))
            last.then_inc(list_done, 1)

        def read_list(dve, job):
            q, s = job.q, job.l
            dve.wait_ge(list_done, q + 1)
            if job.has_before(STEPS):
                dve.wait_ge(added[s % 2], 16 * (job.pair - STEPS // 2 + 1))
            nc.vector.tensor_copy(entry[:, s, :], pl[0:CAP, s % 2, 0:6]).then_inc(entry_ready, 1)
            dve.wait_ge(entry_ready, q + 1)
            nc.vector.tensor_scalar(spare[:, s:s + 1], entry[:, s, 2:3], m.minus_spare[0:CAP, :], m.spare_row[0:CAP, :], ALU.mult, ALU.add)
            nc.vector.scalar_tensor_tensor(token[:, s:s + 1], entry[:, s, 0:1], float(P), entry[:, s, 1:2],
                                           ALU.mult, ALU.add).then_inc(rows_ready, 1)
            dve.wait_ge(rows_ready, 2 * q + 1)
            nc.vector.tensor_tensor(row[:, s:s + 1], spare[:, s:s + 1], token[:, s:s + 1], ALU.add).then_inc(rows_ready, 1)
            nc.vector.tensor_reduce(weight[:, s:s + 1], entry[:, s, 3:6], AX, ALU.add).then_inc(weight_ready, 1)

        def gather(pool, job):
            q, s = job.q, job.s
            pool.wait_ge(rows_ready, 2 * q + 2)
            if job.has_before(NB):
                pool.wait_ge(x_turned, 2 * (q - NB + 1))
            pool.sem_inc(waits_over)
            nc.gpsimd.indirect_dma_start(x_list[:, s, :], None, m.scr_x1,
                                         bass.IndirectOffsetOnAxis(ap=row[:, job.l:job.l + 1], axis=0)).then_inc(gathered[s], 16)

        def turn_list(pe, job):
            q, s = job.q, job.s
            pe.wait_ge(gathered[s], 16 * job.turn + 16)
            if job.has_before(1):
                pe.wait_ge(x_ready, 2 * q)
            v = x_list[:, s, :].rearrange("t (p k) -> t k p", k=KD)
            for k in range(KD):
                bank, at = (0, k) if k < KA else (1, k - KA)
                last = nc.tensor.transpose(px[:, bank, at * CAP:(at + 1) * CAP], v[:, k, :], m.ident[0:CAP, 0:CAP])
                if k in (KA - 1, KD - 1):
                    last.then_inc(x_turned, 1)

        def copy_turned(act, job):
            q, s = job.q, job.s
            for bank, (k0, k1) in enumerate(((0, KA), (KA, KD))):
                act.wait_ge(x_turned, 2 * q + bank + 1)
                if job.has_before(2) and bank == 0:
                    act.wait_ge(gu_done, q - 1)
                nc.scalar.copy(x_list_t[:, s % 2, k0:k1, :],
                               px[:, bank, 0:(k1 - k0) * CAP].rearrange("p (k t) -> p k t", t=CAP)).then_inc(x_ready, 1)

        def gate_up(pe, job):
            q, s = job.q, job.s
            pe.wait_ge(x_ready, 2 * q + 2)
            if job.has_before(2):
                pe.wait_ge(hid_ready, q - 1)
            for part, w in enumerate((m.expert_gate, m.expert_up)):
                pe.wait_ge((m.gate_loaded, m.up_loaded)[part][s], 16 * job.turn + 16)
                for j in range(2):
                    for k in range(KD):
                        last = nc.tensor.matmul(pgu[:, s % 2, (2 * part + j) * CAP:(2 * part + j + 1) * CAP],
                                                w[s][:, k, j * P:(j + 1) * P], x_list_t[:, s % 2, k, :],
                                                start=(k == 0), stop=(k == KD - 1))
            last.then_inc(gu_done, 1)

        def gate_act(act, job):
            q, s = job.q, job.s
            act.wait_ge(gu_done, q + 1)
            nc.scalar.activation(sig[:, s % 2].rearrange("p j t -> p (j t)"), pgu[:, s % 2, 0:2 * CAP], ACT.Sigmoid).then_inc(sig_ready, 1)

        def gate_mul(dve, job):
            q, s = job.q, job.s
            g = sig[:, s % 2].rearrange("p j t -> p (j t)")
            h = hid[:, s % 2].rearrange("p j t -> p (j t)")
            dve.wait_ge(sig_ready, q + 1)
            nc.vector.tensor_tensor(g, g, pgu[:, s % 2, 0:2 * CAP], ALU.mult).then_inc(silu_ready, 1)
            dve.wait_ge(silu_ready, q + 1)
            nc.vector.tensor_tensor(h, g, pgu[:, s % 2, 2 * CAP:4 * CAP], ALU.mult).then_inc(hid_ready, 1)

        def down(pe, job):
            q, s = job.q, job.s
            pe.wait_ge(hid_ready, q + 1)
            pe.wait_ge(m.down_loaded[s], 16 * job.turn + 16)
            for c in range(2):
                if job.has_before(1):
                    pe.wait_ge((y_act, y_dve)[c], q)
                for j in range(2):
                    last = nc.tensor.matmul(pyl[0:CAP, c, :], hid[:, s % 2, j, :], m.expert_down[s][:, j, c * 512:(c + 1) * 512],
                                            start=(j == 0), stop=(j == 1))
                last.then_inc(y_done, 1)

        def weigh_act(act, job):
            q, s = job.q, job.s
            act.wait_ge(y_done, 2 * q + 1)
            act.wait_ge(weight_ready, q + 1)
            if job.has_before(2):
                act.wait_ge(added[s % 2], 16 * job.pair)
            nc.scalar.activation(y_list[:, s % 2, 0:512], pyl[0:CAP, 0, :], ACT.Copy, scale=weight[:, job.l:job.l + 1]).then_inc(y_act, 1)

        def weigh_dve(dve, job):
            q, s = job.q, job.s
            dve.wait_ge(y_done, 2 * q + 2)
            dve.wait_ge(weight_ready, q + 1)
            if job.has_before(2):
                dve.wait_ge(added[s % 2], 16 * job.pair)
            nc.vector.tensor_scalar(y_list[:, s % 2, 512:1024], pyl[0:CAP, 1, :], weight[:, job.l:job.l + 1], None, ALU.mult).then_inc(y_dve, 1)

        def add_rows(pool, job):
            q, s = job.q, job.s
            pool.wait_ge(y_act, q + 1)
            pool.wait_ge(y_dve, q + 1)
            if job.has_before(1):
                pool.wait_ge(added[(s + 1) % 2], 16 * job.before)
            pool.sem_inc(waits_over)
            nc.gpsimd.indirect_dma_start(m.scr_f, bass.IndirectOffsetOnAxis(ap=row[:, job.l:job.l + 1], axis=0), y_list[:, s % 2, :], None,
                                         compute_op=ALU.add).then_inc(added[s % 2], 16)

        def each(eng, step):
            for s in range(STEPS):
                step(0, s, False)
            with eng.Fori(1, LOOPS) as turn:
                for s in range(STEPS):
                    step(turn, s, False)
            for s in range(STEPS):
                step(LOOPS, s, True)

        with nc.Block() as block:
            @block.sync
            def _(sp):
                sp.dma_start(m.ln2_g[:], m.vec["ln2_g"].broadcast_to([P, D])).then_inc(m.ln2_loaded, 16)
                sp.dma_start(m.ln2_b[:], m.vec["ln2_b"].broadcast_to([P, D])).then_inc(m.ln2_loaded, 16)
                with sp.Fori(1, E // NB) as turn:
                    for s in range(NB):
                        sp.wait_ge(y_done, 2 * (NB * turn + s - NB + 1))
                        load_expert(sp, m, NB * turn + s, s)

            @block.tensor
            def _(pe):
                def step(turn, s, last):
                    if not last or s + AHEAD < STEPS:
                        make_list(pe, Job(turn, s + AHEAD))
                    if not last or s + 1 < STEPS:
                        gate_up(pe, Job(turn, s + 1))
                    if not last or s + 2 < STEPS:
                        turn_list(pe, Job(turn, s + 2))
                    down(pe, Job(turn, s))

                for s in range(AHEAD):
                    make_list(pe, Job(0, s))
                for s in range(2):
                    turn_list(pe, Job(0, s))
                gate_up(pe, Job(0, 0))
                each(pe, step)

            @block.vector
            def _(dve):
                def step(turn, s, last):
                    if not last or s + AHEAD < STEPS:
                        read_list(dve, Job(turn, s + AHEAD))
                    if not last or s + 1 < STEPS:
                        gate_mul(dve, Job(turn, s + 1))
                    if not last or s + AHEAD + 1 < STEPS:
                        build_member(dve, Job(turn, s + AHEAD + 1))
                    if isinstance(turn, int) and not last and s < 4:
                        count_jobs(s)
                    weigh_dve(dve, Job(turn, s))

                ch = Chain(dve, m.vector_step, m.vector_count)

                def count_jobs(part):
                    if part == 0:
                        upto = m.cnt[:, 2, :].unsqueeze(1).broadcast_to([P, m.EXTRA, E])
                        ch.link(nc.vector.tensor_tensor(jobs3[:], upto, m.job_index[:].unsqueeze(2).broadcast_to([P, m.EXTRA, E]), ALU.is_le))
                    elif part == 1:
                        ch.link(nc.vector.tensor_reduce(m.job_expert[:], jobs3[:], AX, ALU.add))
                        nc.vector.tensor_copy(m.job_table[:, 1:], m.job_expert[0:1, :])
                    elif part == 2:
                        ch.link(nc.vector.tensor_tensor(jobs3[:], jobs3[:], m.cnt[:, 1, :].unsqueeze(1).broadcast_to([P, m.EXTRA, E]), ALU.mult))
                    else:
                        ch.link(nc.vector.tensor_reduce(m.job_base[:], jobs3[:], AX, ALU.add))
                        ch.link(nc.vector.tensor_tensor(m.job_base[:], m.job_index[:], m.job_base[:], ALU.subtract))
                        ch.link(nc.vector.tensor_scalar(m.job_base[:], m.job_base[:], 1.0, float(CAP), ALU.add, ALU.mult))
                        ch.link(nc.vector.tensor_copy(m.job_table[:, 0:1], m.cnt[0:1, 2, E - 1:E]))

                build_member(dve, Job(0, 0))
                for s in range(AHEAD):
                    build_member(dve, Job(0, s + 1))
                    read_list(dve, Job(0, s))
                gate_mul(dve, Job(0, 0))
                each(dve, step)

            @block.scalar
            def _(act):
                def step(turn, s, last):
                    if not last or s + 1 < STEPS:
                        gate_act(act, Job(turn, s + 1))
                    if not last or s + 2 < STEPS:
                        copy_turned(act, Job(turn, s + 2))
                    weigh_act(act, Job(turn, s))

                for s in range(2):
                    copy_turned(act, Job(0, s))
                gate_act(act, Job(0, 0))
                each(act, step)

            @block.gpsimd
            def _(pool):
                def step(turn, s, last):
                    if not last or s + AHEAD < STEPS:
                        gather(pool, Job(turn, s + AHEAD))
                    add_rows(pool, Job(turn, s))

                for s in range(AHEAD):
                    gather(pool, Job(0, s))
                each(pool, step)
                for b in range(2):
                    pool.wait_ge(added[b], 16 * (E // 2))


def overflow(nc, m, ctx_out):
    with ExitStack() as ctx:
        def sb(name, shape, dt=F32):
            return ctx.enter_context(nc.sbuf_tensor(name, shape, dt))

        def ps(name, shape, dt=F32):
            return ctx.enter_context(nc.psum_tensor(name, shape, dt))

        def sem(name):
            return ctx_out.enter_context(nc.semaphore(name))

        w_gu = sb("w_gu", [P, 2, KD, FE])
        w_down = sb("w_down_o", [P, 2, D])
        place = sb("place", [P, NT])
        member = sb("member_o", [P, NT, CAP], BF16)
        entry = sb("entry_o", [CAP, 6])
        row = sb("row_o", [CAP, 1], U32)
        spare = sb("spare_o", [CAP, 1])
        token = sb("token_o", [CAP, 1])
        weight = sb("weight_o", [CAP, 1])
        x_list = sb("x_list_o", [CAP, D])
        x_list_t = sb("x_list_t_o", [P, KD, CAP])
        sig = sb("sig_o", [P, 2 * CAP])
        hid = sb("hid_o", [P, 2, CAP])
        y_list = sb("y_list_o", [CAP, D])
        pl = ps("pl_o", [P, 512])
        px = ps("px_o", [P, 2, 512])
        pgu = ps("pgu_o", [P, 512])
        pyl = ps("pyl_o", [P, 2, 512])
        KA = 512 // CAP if 512 // CAP < KD else KD // 2
        weights_loaded = sem("o_weights_loaded")
        member_ready = sem("o_member_ready")
        list_done = sem("o_list_done")
        rows_ready = sem("o_rows_ready")
        gathered = sem("o_gathered")
        x_turned = sem("o_x_turned")
        x_ready = sem("o_x_ready")
        gu_done = sem("o_gu_done")
        sig_ready = sem("o_sig_ready")
        hid_ready = sem("o_hid_ready")
        y_done = sem("o_y_done")
        y_ready = sem("o_y_ready")
        added = sem("o_added")
        waits_over = sem("o_waits_over")

        def each_job(eng, body, expert=True):
            n = eng.value_load(m.job_table[0:1, 0:1], min_val=0, max_val=m.EXTRA)
            with eng.If(n > 0):
                with eng.Fori(0, m.EXTRA) as k:
                    with eng.If(k < n):
                        ex = eng.value_load(m.job_table[0:1, bass.ds(k + 1, 1)], min_val=0, max_val=E - 1) if expert else None
                        body(k, ex)

        with nc.Block() as block:
            @block.sync
            def _(sp):
                def body(k, ex):
                    sp.wait_ge(y_done, k)
                    pick = lambda w: w[bass.ds(ex, 1)].rearrange("o p n -> p (o n)")
                    sp.dma_start(w_gu[:, 0].rearrange("p k f -> p (k f)"), pick(m.exp_gate)).then_inc(weights_loaded, 16)
                    sp.dma_start(w_gu[:, 1].rearrange("p k f -> p (k f)"), pick(m.exp_up)).then_inc(weights_loaded, 16)
                    sp.dma_start(w_down[:], m.exp_down[bass.ds(ex, 1)].rearrange("o p j d -> p (o j) d")).then_inc(weights_loaded, 16)
                each_job(sp, body)

            @block.vector
            def _(dve):
                def body(k, ex):
                    dve.wait_ge(added, 16 * k)
                    nc.vector.tensor_scalar(place[:], m.position[:, bass.ds(ex, 1), :].rearrange("p o i -> p (o i)"),
                                            m.job_base[:, bass.ds(k, 1)], None, ALU.subtract).then_inc(member_ready, 1)
                    dve.wait_ge(member_ready, 2 * k + 1)
                    nc.vector.tensor_tensor(member[:], m.slot_index[:].unsqueeze(1).broadcast_to([P, NT, CAP]),
                                            place[:].unsqueeze(2).broadcast_to([P, NT, CAP]), ALU.is_equal).then_inc(member_ready, 1)
                    dve.wait_ge(list_done, k + 1)
                    nc.vector.tensor_copy(entry[:], pl[0:CAP, 0:6]).then_inc(rows_ready, 1)
                    dve.wait_ge(rows_ready, 4 * k + 1)
                    nc.vector.tensor_reduce(weight[:], entry[:, 3:6], AX, ALU.add)
                    nc.vector.tensor_scalar(spare[:], entry[:, 2:3], m.minus_spare[0:CAP, :], m.spare_row[0:CAP, :],
                                            ALU.mult, ALU.add).then_inc(rows_ready, 1)
                    nc.vector.scalar_tensor_tensor(token[:], entry[:, 0:1], float(P), entry[:, 1:2], ALU.mult, ALU.add).then_inc(rows_ready, 1)
                    dve.wait_ge(rows_ready, 4 * k + 3)
                    nc.vector.tensor_tensor(row[:], spare[:], token[:], ALU.add).then_inc(rows_ready, 1)
                    dve.wait_ge(sig_ready, k + 1)
                    nc.vector.tensor_tensor(sig[:], sig[:], pgu[:, 0:2 * CAP], ALU.mult).then_inc(hid_ready, 1)
                    dve.wait_ge(hid_ready, 2 * k + 1)
                    nc.vector.tensor_tensor(hid[:].rearrange("p j t -> p (j t)"), sig[:], pgu[:, 2 * CAP:4 * CAP], ALU.mult).then_inc(hid_ready, 1)
                    dve.wait_ge(y_done, k + 1)
                    for c in range(2):
                        last = nc.vector.tensor_scalar(y_list[:, c * 512:(c + 1) * 512], pyl[0:CAP, c, :], weight[:], None, ALU.mult)
                    last.then_inc(y_ready, 1)
                each_job(dve, body)

            @block.tensor
            def _(pe):
                def body(k, ex):
                    pe.wait_ge(member_ready, 2 * k + 2)
                    for i in range(NT):
                        last = nc.tensor.matmul(pl[0:CAP, 0:6], member[:, i, :], m.table[:, bass.ds(ex, 1), i, :].rearrange("p o c -> p (o c)"),
                                                start=(i == 0), stop=(i == NT - 1))
                    last.then_inc(list_done, 1)
                    pe.wait_ge(gathered, 16 * k + 16)
                    v = x_list[:].rearrange("t (p k) -> t k p", k=KD)
                    for kk in range(KD):
                        bank, at = (0, kk) if kk < KA else (1, kk - KA)
                        last = nc.tensor.transpose(px[:, bank, at * CAP:(at + 1) * CAP], v[:, kk, :], m.ident[0:CAP, 0:CAP])
                    last.then_inc(x_turned, 1)
                    pe.wait_ge(x_ready, k + 1)
                    pe.wait_ge(weights_loaded, 48 * k + 48)
                    for part in range(2):
                        for j in range(2):
                            for kk in range(KD):
                                last = nc.tensor.matmul(pgu[:, (2 * part + j) * CAP:(2 * part + j + 1) * CAP],
                                                        w_gu[:, part, kk, j * P:(j + 1) * P], x_list_t[:, kk, :],
                                                        start=(kk == 0), stop=(kk == KD - 1))
                    last.then_inc(gu_done, 1)
                    pe.wait_ge(hid_ready, 2 * k + 2)
                    for c in range(2):
                        for j in range(2):
                            last = nc.tensor.matmul(pyl[0:CAP, c, :], hid[:, j, :], w_down[:, j, c * 512:(c + 1) * 512],
                                                    start=(j == 0), stop=(j == 1))
                    last.then_inc(y_done, 1)
                each_job(pe, body)

            @block.scalar
            def _(act):
                def body(k, ex):
                    act.wait_ge(x_turned, k + 1)
                    for bank, (k0, k1) in enumerate(((0, KA), (KA, KD))):
                        last = nc.scalar.copy(x_list_t[:, k0:k1, :], px[:, bank, 0:(k1 - k0) * CAP].rearrange("p (k t) -> p k t", t=CAP))
                    last.then_inc(x_ready, 1)
                    act.wait_ge(gu_done, k + 1)
                    nc.scalar.activation(sig[:], pgu[:, 0:2 * CAP], ACT.Sigmoid).then_inc(sig_ready, 1)
                each_job(act, body, expert=False)

            @block.gpsimd
            def _(pool):
                def body(k, ex):
                    pool.wait_ge(rows_ready, 4 * k + 4)
                    pool.sem_inc(waits_over)
                    nc.gpsimd.indirect_dma_start(x_list[:], None, m.scr_x1,
                                                 bass.IndirectOffsetOnAxis(ap=row[:], axis=0)).then_inc(gathered, 16)
                    pool.wait_ge(y_ready, k + 1)
                    pool.sem_inc(waits_over)
                    nc.gpsimd.indirect_dma_start(m.scr_f, bass.IndirectOffsetOnAxis(ap=row[:], axis=0), y_list[:], None,
                                                 compute_op=ALU.add).then_inc(added, 16)
                    pool.wait_ge(added, 16 * k + 16)
                each_job(pool, body, expert=False)


def finish(nc, m, ctx_out):
    with ExitStack() as ctx:
        def sb(name, shape, dt=F32):
            return ctx.enter_context(nc.sbuf_tensor(name, shape, dt))

        def sem(name):
            return ctx_out.enter_context(nc.semaphore(name))

        f = sb("f", [P, NT, D])
        stats = sb("stats7", [P, NT, 2, 6])
        aggr = sb("aggr7", [P, NT, 5])
        f_loaded = [sem(f"f_loaded{i}") for i in range(NT)]
        stats_ready = sem("stats_ready")
        var_ready = sem("var7_ready")
        rooted = sem("ln2_rooted")
        shift_ready = sem("ln2_shift_ready")
        normed = sem("ln2_normed")
        scaled = sem("ln2_scaled")
        y_ready = sem("y_ready")
        y_stored = sem("out_stored")
        with nc.Block() as block:
            @block.sync
            def _(sp):
                for i, (t0, n) in enumerate(TOK_TILES):
                    sp.dma_start(f[0:n, i, :], m.scr_f[t0:t0 + n, :]).then_inc(f_loaded[i], 16)
                for i, (t0, n) in enumerate(TOK_TILES):
                    sp.wait_ge(y_ready, i + 1)
                    dst = m.y_prompt[t0:t0 + n, :] if i < TM else m.y_sample
                    sp.dma_start(dst, f[0:n, i, :]).then_inc(y_stored, 16)
                sp.wait_ge(y_stored, 16 * NT)

            @block.scalar
            def _(act):
                for i, (_, n) in enumerate(TOK_TILES):
                    act.wait_ge(var_ready, i + 1)
                    nc.scalar.activation(aggr[0:n, i, 2:3], aggr[0:n, i, 1:2], ACT.Sqrt, bias=m.eps_ln[0:n, :]).then_inc(rooted, 1)
                    act.wait_ge(shift_ready, i + 1)
                    nc.scalar.activation(f[0:n, i, :], f[0:n, i, :], ACT.Identity, scale=aggr[0:n, i, 3:4],
                                         bias=aggr[0:n, i, 4:5]).then_inc(normed, 1)

            @block.gpsimd
            def _(pool):
                for i, (_, n) in enumerate(TOK_TILES):
                    pool.wait_ge(scaled, i + 1)
                    nc.gpsimd.tensor_tensor(f[0:n, i, :], f[0:n, i, :], m.ln2_b[0:n, :], ALU.add).then_inc(y_ready, 1)

            @block.vector
            def _(dve):
                ch = Chain(dve, m.vector_step, m.vector_count)
                dve.wait_ge(m.ln2_loaded, 32)

                def scale(i):
                    n = TOK_TILES[i][1]
                    dve.wait_ge(normed, i + 1)
                    nc.vector.tensor_tensor(f[0:n, i, :], f[0:n, i, :], m.ln2_g[0:n, :], ALU.mult).then_inc(scaled, 1)

                for i, (_, n) in enumerate(TOK_TILES):
                    x = f[0:n, i, :]
                    dve.wait_ge(f_loaded[i], 16)
                    for c in range(2):
                        last = nc.vector.bn_stats(stats[0:n, i, c, :], x[:, c * 512:(c + 1) * 512])
                    last.then_inc(stats_ready, 1)
                    dve.wait_ge(stats_ready, i + 1)
                    nc.vector.bn_aggr(aggr[0:n, i, 0:2], stats[0:n, i, :, :]).then_inc(var_ready, 1)
                    dve.wait_ge(var_ready, i + 1)
                    dve.wait_ge(rooted, i + 1)
                    ch.link(nc.vector.reciprocal(aggr[0:n, i, 3:4], aggr[0:n, i, 2:3]))
                    nc.vector.scalar_tensor_tensor(aggr[0:n, i, 4:5], aggr[0:n, i, 0:1], -1.0, aggr[0:n, i, 3:4],
                                                   ALU.mult, ALU.mult).then_inc(shift_ready, 1)
                    if i >= 1:
                        scale(i - 1)
                scale(NT - 1)


def constants(nc, m, ready):
    def build(pool):
        ch = Chain(pool, m.pool_step, m.pool_count)
        g = nc.gpsimd
        ch.link(g.memset(m.ident[:], 0.0))
        g.affine_select(out=m.ident[:], in_=m.ident[:], compare_op=ALU.not_equal, fill=1.0, base=0,
                        pattern=[[-1, P]], channel_multiplier=1).then_inc(ready, 1)
        g.memset(m.eps_ln[:], LN_EPS)
        g.memset(m.eps_gn[:], GN_EPS)
        g.memset(m.ones[:], 1.0)
        g.memset(m.ones_mean[:], 1.0 / DC)
        g.memset(m.head_ones[:], 1.0)
        g.memset(m.below[:], 1.0)
        g.memset(m.is_token[:], 1.0)
        g.memset(m.chunk_keep[:], 1.0)
        ch.link(g.memset(m.inside_mask[:], 1.0))
        heads = m.head_ones[:].rearrange("p (h c) -> p h c", c=N)
        ch.link(g.affine_select(out=heads, in_=heads, compare_op=ALU.is_ge, fill=0.0, base=0, pattern=[[-N, 2], [0, N]], channel_multiplier=1))
        ch.link(g.affine_select(out=heads, in_=heads, compare_op=ALU.is_ge, fill=0.0, base=N - 1, pattern=[[N, 2], [0, N]], channel_multiplier=-1))
        for c in range(CM):
            r = m.below[L * c:L * (c + 1), :]
            ch.link(g.affine_select(out=r, in_=r, compare_op=ALU.is_gt, fill=0.0, base=0, pattern=[[-1, L]], channel_multiplier=1))
        for part in range(3):
            v = m.inside_mask[:, part, :].rearrange("p (c t) -> p c t", t=L)
            ch.link(g.affine_select(out=v, in_=v, compare_op=ALU.is_ge, fill=0.0, base=0, pattern=[[-L, CM], [0, L]], channel_multiplier=1))
            ch.link(g.affine_select(out=v, in_=v, compare_op=ALU.is_ge, fill=0.0, base=L - 1, pattern=[[L, CM], [0, L]], channel_multiplier=-1))
            ch.link(g.affine_select(out=m.inside_mask[:, part, :], in_=m.inside_mask[:, part, :],
                                    compare_op=ALU.is_gt if part == 0 else ALU.is_ge, fill=0.0, base=0,
                                    pattern=[[1, P]], channel_multiplier=-1))
        g.memset(m.chunk_keep[:, 0:T:L], 0.0)
        g.affine_select(out=m.is_token[:, TM:], in_=m.is_token[:, TM:], compare_op=ALU.is_ge, fill=0.0, base=B - 1,
                        pattern=[[0, 1]], channel_multiplier=-1)
        wide = dict(allow_small_or_imprecise_dtypes=True)
        g.iota(m.tile_index[:], pattern=[[1, NT]], base=0, channel_multiplier=0, **wide)
        g.iota(m.partition_index[:], pattern=[[0, NT]], base=0, channel_multiplier=1, **wide)
        g.iota(m.minus_spare[:], pattern=[[0, 1]], base=-TT, channel_multiplier=-1, **wide)
        g.iota(m.slot_index[:], pattern=[[1, CAP]], base=0, channel_multiplier=0, **wide)
        g.iota(m.job_index[:], pattern=[[1, m.EXTRA]], base=0, channel_multiplier=0, **wide)
        g.iota(m.spare_row[:], pattern=[[0, 1]], base=TT, channel_multiplier=1, **wide)
    return build


class Shared:
    pass


def kernel_program(nc, a, outs):
    m = Shared()
    flat = "l k n -> (l k) n"
    m.x_prompt = a["x_prompt"].rearrange("b t d -> (b t) d")
    m.x_sample = a["x_sample"].rearrange("b t d -> (b t) d")
    m.state_conv = a["state_conv"].rearrange("l b w c -> (l b) w c")
    m.state_shift = a["state_shift"].rearrange("l b c -> (l b) c")
    m.state_wkv = a["state_wkv"].rearrange("l b h (two v) k -> (l b h two) (v k)", two=2)
    m.w_in = a["w_in"].rearrange(flat)
    m.conv_w = a["conv_w"].rearrange("l w c -> (l w) c")
    m.mu_shift = a["mu_shift"]
    m.vec = {n: a[n] if n != "r_k" else a[n].rearrange("l h n -> l (h n)")
             for n in PARAMS + ["gn_g", "gn_b", "ln1_g", "ln1_b", "ln2_g", "ln2_b", "router_bias"]}
    m.w_up, m.a_up, m.g_up = (a[n].rearrange(flat) for n in ("w_up", "a_up", "g_up"))
    m.w_out, m.router_w = (a[n].rearrange(flat) for n in ("w_out", "router_w"))
    m.sh_gate, m.sh_up, m.sh_down = (a[n].rearrange(flat) for n in ("sh_gate", "sh_up", "sh_down"))
    m.exp_gate = a["exp_gate"].rearrange("l e (p k) f -> (l e) p (k f)", p=P)
    m.exp_up = a["exp_up"].rearrange("l e (p k) f -> (l e) p (k f)", p=P)
    m.exp_down = a["exp_down"].rearrange("l e (j p) d -> (l e) p j d", p=P)
    m.y_prompt = outs[0].rearrange("b t d -> (b t) d")
    m.y_sample = outs[1].rearrange("b t d -> (b t) d")
    m.new_conv_p = outs[2].rearrange("l b w c -> (l b w) c")
    m.new_shift_p = outs[3].rearrange("l b c -> (l b) c")
    m.new_wkv_p = outs[4].rearrange("l b h v k -> (l b h) v k")
    m.new_conv_s = outs[5].rearrange("l b w c -> (l b) w c")
    m.new_shift_s = outs[6].rearrange("l b c -> (l b) c")
    m.new_wkv_s = outs[7].rearrange("l b h (two v) k -> (l b h two) (v k)", two=2)
    m.scr_lower = nc.dram_tensor("scr_lower", (P, L * L), F32).ap()
    m.scr_solved = nc.dram_tensor("scr_solved", (P, L * L), F32).ap()
    m.scr_sample = nc.dram_tensor("scr_sample", (6, B, DC), F32).ap()
    m.scr_y = nc.dram_tensor("scr_y", (B, DC), F32).ap()
    m.scr_x1 = nc.dram_tensor("scr_x1", (TT + CAP, D), F32).ap()
    m.scr_f = nc.dram_tensor("scr_f", (TT + CAP, D), F32).ap()
    m.MAX_JOBS = -(-TT // CAP)
    m.EXTRA = TT * K // CAP
    with ExitStack() as top:
        def sb(name, shape, dt=F32):
            return top.enter_context(nc.sbuf_tensor(name, shape, dt))

        m.vector_step = top.enter_context(nc.semaphore("vector_step"))
        m.vector_count = [0]
        m.pool_step = top.enter_context(nc.semaphore("pool_step"))
        m.pool_count = [0]
        first_sems = ExitStack()
        m.spent = []
        m.ident = sb("ident", [P, P])
        m.ones = sb("ones", [P, P])
        m.eps_ln = sb("eps_ln", [P, 1])
        m.eps_gn = sb("eps_gn", [P, 1])
        m.is_token = sb("is_token", [P, NT])
        m.tile_index = sb("tile_index", [P, NT])
        m.partition_index = sb("partition_index", [P, NT])
        m.slot_index = sb("slot_index", [P, CAP])
        m.job_index = sb("job_index", [P, m.EXTRA])
        m.job_expert = sb("job_expert", [P, m.EXTRA])
        m.job_base = sb("job_base", [P, m.EXTRA])
        m.job_table = sb("job_table", [1, m.EXTRA + 1], U32)
        m.spare_row = sb("spare_row", [P, 1])
        m.minus_spare = sb("minus_spare", [P, 1])
        m.position = sb("position", [P, E, NT])
        m.cnt = sb("cnt", [P, 4, E])
        m.table = sb("table", [P, E, NT, 6], BF16)
        m.w_exp = sb("w_exp", [P, NB * EXPERT_FLOATS])
        at = lambda s, part: EXPERT_FLOATS * s + KD * FE * part
        m.expert_gate = [place(m, at(s, 0), KD, FE) for s in range(NB)]
        m.expert_up = [place(m, at(s, 1), KD, FE) for s in range(NB)]
        m.expert_down = [place(m, at(s, 2), 2, D) for s in range(NB)]
        m.UPPER = 2 * EXPERT_FLOATS
        m.BESIDE_ROWS = TM * DC * 3 + NT * DC + CT * T
        m.BESIDE_ZS = m.UPPER + NSH * TT
        m.zs = place(m, m.UPPER, NSH, TT)
        m.x_again = place(m, m.UPPER, 2, D)
        m.w_out_half = [place(m, m.UPPER + 4 * KD * FE, KD, 512), place(m, m.UPPER + KD * FE, KD, 512)]
        m.gate_loaded = [top.enter_context(nc.semaphore(f"gate_loaded{i}")) for i in range(NB)]
        m.up_loaded = [top.enter_context(nc.semaphore(f"up_loaded{i}")) for i in range(NB)]
        m.down_loaded = [top.enter_context(nc.semaphore(f"down_loaded{i}")) for i in range(NB)]
        m.w_out_loaded = [top.enter_context(nc.semaphore(f"w_out_loaded{i}")) for i in range(2)]
        m.x_again_loaded = [top.enter_context(nc.semaphore(f"x_again_loaded{i}")) for i in range(2)]
        with ExitStack() as late:
            def sb2(name, shape, dt=F32):
                return late.enter_context(nc.sbuf_tensor(name, shape, dt))

            m.conv = sb2("conv", [P, CT, TT])
            m.o_t = sb2("o_t", [P, CT, TT])
            with ExitStack() as mid:
                def sb3(name, shape, dt=F32):
                    return mid.enter_context(nc.sbuf_tensor(name, shape, dt))

                m.ones_mean = sb3("ones_mean", [P, P])
                m.head_ones = sb3("head_ones", [P, P])
                m.below = sb3("below", [P, L])
                m.inside_mask = sb3("inside_mask", [P, 3, P])
                m.chunk_keep = sb3("chunk_keep", [P, T])
                m.params = sb3("params", [P, CT, NPAR])
                project(nc, m, first_sems)
                m.v_rows = place(m, 0, NT, DC)
                m.gate = sb3("gate", [P, NT, DC])
                m.bonus = sb3("bonus", [P, NT, H])
                m.a_rows, m.b_rows, m.k_rows = (place(m, NT * DC + i * TM * DC, TM, DC) for i in range(3))
                m.read_decayed = sb3("read_decayed", [P, CT, TM, 2, P])
                m.b_grown = place(m, NT * DC + 3 * TM * DC, CT, T)
                m.k_grown = sb3("k_grown", [P, CT, T])
                m.chunk_decay = sb3("chunk_decay", [P, CT, NCH])
                m.sample_vec = sb3("sample_vec", [P, 6, CT, B])
                m.y_sample_rows = sb3("y_sample_rows", [B, DC])
                time_prepare(nc, m, first_sems)
                m.inverse = sb3("inverse", [P, TM * H, P])
                inside_late = sb3("inside_late", [P, 2, H, 3, L])
                m.inside = [place(m, m.UPPER + 3 * 32 * N + j * H * 3 * L, H, 3, L) for j in range(2)] + [inside_late[:, j] for j in range(2)]
                solve_chunks(nc, m, first_sems)
                recur(nc, m, top)
            first_sems.close()
            mix(nc, m, top)
        m.ln2_g = sb("ln2_g", [P, D])
        m.ln2_b = sb("ln2_b", [P, D])
        m.ln2_loaded = top.enter_context(nc.semaphore("ln2_loaded"))
        experts(nc, m, top)
        overflow(nc, m, top)
        finish(nc, m, top)


_INS = ["x_prompt", "x_sample", "state_conv", "state_shift", "state_wkv", "w_in", "mu_shift", "conv_w", "conv_b",
        "conv_ln_g", "conv_ln_b", "w0", "w_up", "a0", "a_up", "g_up", "k_k", "k_a", "r_k", "gn_g", "gn_b", "w_out",
        "ln1_g", "ln1_b", "router_w", "router_bias", "exp_gate", "exp_up", "exp_down", "sh_gate", "sh_up", "sh_down",
        "ln2_g", "ln2_b"]
_OUTS = [(1, T, D), (B, 1, D), (1, 1, CW - 1, DC), (1, 1, DS), (1, 1, H, N, N), (1, B, CW - 1, DC), (1, B, DS),
         (1, B, H, N, N)]


def kernel(**inputs):
    import numpy as _np
    import concourse.bacc as _bacc
    from concourse import mybir as _mybir
    from concourse.bass_utils import run_bass_kernel_spmd as _run

    nc = _bacc.Bacc("TRN2", target_bir_lowering=False, num_devices=1)
    arrays, aps = {}, {}
    for name in _INS:
        x = _np.ascontiguousarray(inputs[name])
        arrays[f"in_{name}_dram"] = x
        aps[name] = nc.dram_tensor(f"in_{name}_dram", x.shape, _mybir.dt.from_np(x.dtype), kind="ExternalInput").ap()
    outs = [nc.dram_tensor(f"out_{i}_dram", shape, _mybir.dt.float32, kind="ExternalOutput").ap()
            for i, shape in enumerate(_OUTS)]
    kernel_program(nc, aps, outs)
    r = _run(nc, [arrays], core_ids=[0])
    return tuple(r.results[0][f"out_{i}_dram"] for i in range(len(_OUTS)))
```
